# Optimizing a Trainium2 kernel written in Bass

```python
import math
import jax, jax.numpy as jnp
from jax import lax
import numpy as np

D_MODEL = 1024
BATCH = 1
SEQ = 1024
DEPTH = 1

D_MIX = D_MODEL
C_CONV = D_MIX // 4
C_POOL = D_MIX // 4
C_ATTN = D_MIX - C_CONV - C_POOL
DIFF_HEADS = 4
DIFF_HEAD_DIM = C_ATTN // (2 * DIFF_HEADS)
CONV_WIDTH = 31
POOL_WINDOWS = (2, 4, 8, 16)
POOL_GROUP = C_POOL // len(POOL_WINDOWS)
N_IN = 2 * C_CONV + C_POOL + 3 * C_ATTN
N_EXPERT_GROUPS = 4
EXPERTS_PER_GROUP = 4
N_EXPERTS = N_EXPERT_GROUPS * EXPERTS_PER_GROUP
D_EXPERT = D_MODEL // 4
MOE_TOP_K = 2
ATTN_BLOCK = 128
NORM_EPS = 1e-6


def rms_norm(x, g):
    xf = x.astype(jnp.float32)
    y = xf * lax.rsqrt(jnp.mean(xf * xf, axis=-1, keepdims=True) + NORM_EPS)
    return (y * g.astype(jnp.float32)).astype(x.dtype)

def layer_norm(x, g, b):
    xf = x.astype(jnp.float32)
    mu = jnp.mean(xf, axis=-1, keepdims=True)
    xc = xf - mu
    y = xc * lax.rsqrt(jnp.mean(xc * xc, axis=-1, keepdims=True) + NORM_EPS)
    return (y * g.astype(jnp.float32) + b.astype(jnp.float32)).astype(x.dtype)

def alibi_slopes(n_heads):
    start = 2.0 ** (-8.0 / n_heads)
    return jnp.asarray(np.array([start ** (i + 1) for i in range(n_heads)], dtype=np.float32))

def conv_mixer(a_val, a_gate, w_dw, b_dw, ln_g, ln_b, w_pw, b_pw):
    u = a_val * jax.nn.sigmoid(a_gate)
    y = lax.conv_general_dilated(
        u, w_dw[:, None, :].astype(u.dtype), window_strides=(1,),
        padding=[(CONV_WIDTH - 1, 0)],
        dimension_numbers=("NWC", "WIO", "NWC"),
        feature_group_count=C_CONV) + b_dw
    y = jax.nn.silu(layer_norm(y, ln_g, ln_b))
    return y @ w_pw + b_pw

def pool_mixer(u, w_pool, scale):
    s_len = u.shape[1]
    uf = u.astype(jnp.float32)
    c0 = jnp.pad(lax.cumsum(uf, axis=1), ((0, 0), (1, 0), (0, 0)))
    t = jnp.arange(s_len)
    outs = []
    for gi, win in enumerate(POOL_WINDOWS):
        sl = slice(gi * POOL_GROUP, (gi + 1) * POOL_GROUP)
        lo = jnp.maximum(t + 1 - win, 0)
        window_sum = c0[:, 1:, sl] - c0[:, lo, sl]
        count = jnp.minimum(t + 1, win).astype(jnp.float32)[None, :, None]
        d = (window_sum / count - uf[:, :, sl]).astype(u.dtype)
        outs.append(jnp.einsum("bsc,cd->bsd", d, w_pool[gi]))
    return jnp.concatenate(outs, axis=-1) * scale

def diff_attention(q, k, v, lam, slopes):
    s_len = q.shape[1]
    q = q.transpose(0, 2, 3, 1, 4)
    k = k.transpose(0, 2, 3, 1, 4)
    v = v.transpose(0, 2, 1, 3)
    scale = DIFF_HEAD_DIM ** -0.5
    outs = []
    for blk in range(s_len // ATTN_BLOCK):
        q0 = blk * ATTN_BLOCK
        end = q0 + ATTN_BLOCK
        qb = q[:, :, :, q0:end]
        kb = k[:, :, :, :end]
        vb = v[:, :, :end]
        s = jnp.einsum("bhmqd,bhmkd->bhmqk", qb, kb,
                       preferred_element_type=jnp.float32) * scale
        tq = jnp.arange(q0, end)[:, None]
        tk = jnp.arange(end)[None, :]
        dist = (tq - tk).astype(jnp.float32)
        s = s - slopes[None, :, None, None, None] * dist
        s = jnp.where(tk <= tq, s, -jnp.inf)
        p = jax.nn.softmax(s, axis=-1)
        a = p[:, :, 0] - lam * p[:, :, 1]
        outs.append(jnp.einsum("bhqk,bhkd->bhqd", a.astype(vb.dtype), vb))
    o = jnp.concatenate(outs, axis=2)
    return o.transpose(0, 2, 1, 3)

def hier_moe(h, wg, bg, we, be, w_gate, w_up, w_down):
    b_, s_, d_ = h.shape
    t = h.reshape(-1, d_)
    pg = jax.nn.softmax((t @ wg).astype(jnp.float32) + bg.astype(jnp.float32), axis=-1)
    g_idx = jnp.argmax(pg, axis=-1)
    g_p = jnp.take_along_axis(pg, g_idx[:, None], axis=1)[:, 0]
    le = ((t @ we).astype(jnp.float32) + be.astype(jnp.float32)).reshape(-1, N_EXPERT_GROUPS, EXPERTS_PER_GROUP)
    le = jnp.take_along_axis(le, g_idx[:, None, None], axis=1)[:, 0]
    pe = jax.nn.softmax(le, axis=-1)
    top_p, top_i = lax.top_k(pe, MOE_TOP_K)
    top_p = top_p / jnp.sum(top_p, axis=-1, keepdims=True)
    weights = g_p[:, None] * top_p
    eid = g_idx[:, None] * EXPERTS_PER_GROUP + top_i
    gates = jnp.sum(jax.nn.one_hot(eid, N_EXPERTS, dtype=jnp.float32) * weights[..., None], axis=1)
    gates = gates.astype(t.dtype)
    y = jnp.zeros_like(t)
    for e in range(N_EXPERTS):
        act = jax.nn.silu(t @ w_gate[e]) * (t @ w_up[e]) * gates[:, e:e + 1]
        y = y + act @ w_down[e]
    return y.reshape(b_, s_, d_)

def first_inputs(seed: int = 0) -> dict:
    key = jax.random.key(seed)
    ks = iter(jax.random.split(key, 40))
    L = DEPTH

    def nrm(shape, scale):
        return jax.random.normal(next(ks), shape, jnp.float32) * scale

    def gain(shape):
        return 1.0 + nrm(shape, 0.02)

    return {
        "x": nrm((BATCH, SEQ, D_MODEL), 1.0),
        "attn_norm_g": gain((L, D_MODEL)),
        "w_in": nrm((L, D_MODEL, N_IN), D_MODEL ** -0.5),
        "conv_w": nrm((L, CONV_WIDTH, C_CONV), CONV_WIDTH ** -0.5),
        "conv_b": nrm((L, C_CONV), 0.02),
        "conv_ln_g": gain((L, C_CONV)),
        "conv_ln_b": nrm((L, C_CONV), 0.02),
        "conv_pw_w": nrm((L, C_CONV, C_CONV), C_CONV ** -0.5),
        "conv_pw_b": nrm((L, C_CONV), 0.02),
        "pool_w": nrm((L, len(POOL_WINDOWS), POOL_GROUP, POOL_GROUP), POOL_GROUP ** -0.5),
        "pool_scale": gain((L, C_POOL)),
        "q_norm_g": gain((L, DIFF_HEAD_DIM)),
        "k_norm_g": gain((L, DIFF_HEAD_DIM)),
        "lambda_q1": nrm((L, DIFF_HEAD_DIM), 0.1),
        "lambda_k1": nrm((L, DIFF_HEAD_DIM), 0.1),
        "lambda_q2": nrm((L, DIFF_HEAD_DIM), 0.1),
        "lambda_k2": nrm((L, DIFF_HEAD_DIM), 0.1),
        "attn_sub_norm_g": gain((L, 2 * DIFF_HEAD_DIM)),
        "w_out": nrm((L, D_MIX, D_MODEL), D_MIX ** -0.5),
        "ffn_norm_g": gain((L, D_MODEL)),
        "router_g_w": nrm((L, D_MODEL, N_EXPERT_GROUPS), D_MODEL ** -0.5),
        "router_g_b": nrm((L, N_EXPERT_GROUPS), 0.01),
        "router_e_w": nrm((L, D_MODEL, N_EXPERTS), D_MODEL ** -0.5),
        "router_e_b": nrm((L, N_EXPERTS), 0.01),
        "w_gate": nrm((L, N_EXPERTS, D_MODEL, D_EXPERT), D_MODEL ** -0.5),
        "w_up": nrm((L, N_EXPERTS, D_MODEL, D_EXPERT), D_MODEL ** -0.5),
        "w_down": nrm((L, N_EXPERTS, D_EXPERT, D_MODEL), D_EXPERT ** -0.5),
    }

def first_block(x, attn_norm_g, w_in, conv_w, conv_b, conv_ln_g, conv_ln_b, conv_pw_w, conv_pw_b,
              pool_w, pool_scale, q_norm_g, k_norm_g, lambda_q1, lambda_k1, lambda_q2, lambda_k2,
              attn_sub_norm_g, w_out, ffn_norm_g, router_g_w, router_g_b, router_e_w, router_e_b,
              w_gate, w_up, w_down):
    b_, s_, _ = x.shape
    slopes = alibi_slopes(DIFF_HEADS)
    splits = [C_CONV, 2 * C_CONV, 2 * C_CONV + C_POOL,
              2 * C_CONV + C_POOL + C_ATTN, 2 * C_CONV + C_POOL + 2 * C_ATTN]
    for l in range(DEPTH):
        h = rms_norm(x, attn_norm_g[l])
        z = h @ w_in[l]
        a_val, a_gate, p_in, q, k, v = jnp.split(z, splits, axis=-1)

        y_conv = conv_mixer(a_val, a_gate, conv_w[l], conv_b[l], conv_ln_g[l], conv_ln_b[l],
                            conv_pw_w[l], conv_pw_b[l])
        y_pool = pool_mixer(p_in, pool_w[l], pool_scale[l])

        q = rms_norm(q.reshape(b_, s_, DIFF_HEADS, 2, DIFF_HEAD_DIM), q_norm_g[l])
        k = rms_norm(k.reshape(b_, s_, DIFF_HEADS, 2, DIFF_HEAD_DIM), k_norm_g[l])
        v = v.reshape(b_, s_, DIFF_HEADS, 2 * DIFF_HEAD_DIM)
        lam_init = 0.8 - 0.6 * math.exp(-0.3 * l)
        lam = (jnp.exp(jnp.sum(lambda_q1[l].astype(jnp.float32) * lambda_k1[l].astype(jnp.float32)))
               - jnp.exp(jnp.sum(lambda_q2[l].astype(jnp.float32) * lambda_k2[l].astype(jnp.float32)))
               + lam_init)
        o = diff_attention(q, k, v, lam, slopes)
        o = rms_norm(o, attn_sub_norm_g[l]) * (1.0 - lam_init)
        y_attn = o.reshape(b_, s_, C_ATTN)

        mix = jnp.concatenate([y_conv, y_pool, y_attn], axis=-1)
        x = x + mix @ w_out[l]

        hf = rms_norm(x, ffn_norm_g[l])
        x = x + hier_moe(hf, router_g_w[l], router_g_b[l], router_e_w[l], router_e_b[l],
                         w_gate[l], w_up[l], w_down[l])
    return x


DEPTH_2 = 2

PLE_DIM = 256
EPS = 1e-6

MLA_HEADS = 4
MLA_Q_RANK = 384
MLA_KV_RANK = 256
MLA_NOPE = 128
MLA_ROPE = 64
MLA_V = 128
MLA_WIDTH = MLA_HEADS * MLA_V
ROPE_THETA = 10000.0
Q_BLOCK = 128

GLA_HEADS = 4
GLA_DK = 64
GLA_DV = 128
GLA_WIDTH = GLA_HEADS * GLA_DV
GLA_GATE_RANK = 16
GLA_TAU = 16.0
GLA_CHUNK = 64

D_MIX_2 = MLA_WIDTH + GLA_WIDTH

IN_SPLITS = (
    MLA_Q_RANK,
    MLA_KV_RANK,
    MLA_ROPE,
    MLA_WIDTH,
    GLA_HEADS * GLA_DK,
    GLA_HEADS * GLA_DK,
    GLA_WIDTH,
    GLA_GATE_RANK,
    GLA_GATE_RANK,
    GLA_WIDTH,
)
D_IN = sum(IN_SPLITS)


def rmsnorm(x, g):
    xf = x.astype(jnp.float32)
    y = xf * lax.rsqrt(jnp.mean(xf * xf, axis=-1, keepdims=True) + EPS)
    return (y * g.astype(jnp.float32)).astype(x.dtype)

def split_cols(u, sizes):
    out, start = [], 0
    for s in sizes:
        out.append(u[..., start:start + s])
        start += s
    return out

def apply_rope(x, pos):
    half = MLA_ROPE // 2
    inv = ROPE_THETA ** (-jnp.arange(half, dtype=jnp.float32) / half)
    ang = pos.astype(jnp.float32)[..., None] * inv
    cos, sin = jnp.cos(ang), jnp.sin(ang)
    if x.ndim == 4:
        cos, sin = cos[:, :, None, :], sin[:, :, None, :]
    xf = x.astype(jnp.float32)
    x1, x2 = xf[..., :half], xf[..., half:]
    return jnp.concatenate([x1 * cos - x2 * sin, x1 * sin + x2 * cos], axis=-1).astype(x.dtype)

def mla_branch(c_q, c_kv, k_rope, pos, q_norm, w_uq, kv_norm, w_ukv):
    B, S, _ = c_q.shape
    q = (rmsnorm(c_q, q_norm) @ w_uq).reshape(B, S, MLA_HEADS, MLA_NOPE + MLA_ROPE)
    q_nope = q[..., :MLA_NOPE]
    q_rope = apply_rope(q[..., MLA_NOPE:], pos)
    kv = (rmsnorm(c_kv, kv_norm) @ w_ukv).reshape(B, S, MLA_HEADS, MLA_NOPE + MLA_V)
    k_nope, v = kv[..., :MLA_NOPE], kv[..., MLA_NOPE:]
    k_r = apply_rope(k_rope, pos)
    scale = (MLA_NOPE + MLA_ROPE) ** -0.5
    nb = S // Q_BLOCK
    qn_b = q_nope.reshape(B, nb, Q_BLOCK, MLA_HEADS, MLA_NOPE).transpose(1, 0, 2, 3, 4)
    qr_b = q_rope.reshape(B, nb, Q_BLOCK, MLA_HEADS, MLA_ROPE).transpose(1, 0, 2, 3, 4)

    def block(args):
        qn, qr = args
        s = (jnp.einsum('bqhd,bkhd->bhqk', qn, k_nope)
             + jnp.einsum('bqhr,bkr->bhqk', qr, k_r))
        prob = jax.nn.softmax(s.astype(jnp.float32) * scale, axis=-1).astype(v.dtype)
        return jnp.einsum('bhqk,bkhd->bqhd', prob, v)

    o = lax.map(block, (qn_b, qr_b))
    return o.transpose(1, 0, 2, 3, 4).reshape(B, S, MLA_WIDTH)

def gla_chunked(q, k, v, log_a):
    B, S, H, DK = q.shape
    DV = v.shape[-1]
    C = GLA_CHUNK
    N = S // C

    def to_chunks(t):
        return t.astype(jnp.float32).reshape(B, N, C, H, -1).transpose(1, 0, 3, 2, 4)

    qc, kc, vc, gc = to_chunks(q), to_chunks(k), to_chunks(v), to_chunks(log_a)
    b = jnp.cumsum(gc, axis=-2)
    ref = b[..., C // 2 - 1:C // 2, :]
    q_in = qc * jnp.exp(b - ref)
    k_in = kc * jnp.exp(ref - b)
    mask = jnp.tril(jnp.ones((C, C), dtype=bool))
    A = jnp.where(mask, jnp.einsum('nbhid,nbhjd->nbhij', q_in, k_in), 0.0)
    o_intra = jnp.einsum('nbhij,nbhjv->nbhiv', A, vc)

    b_last = b[..., -1:, :]
    q_inter = qc * jnp.exp(b)
    k_state = kc * jnp.exp(b_last - b)
    decay = jnp.exp(b_last[..., 0, :])

    def step(state, inp):
        qi, ki, vi, di = inp
        o = jnp.einsum('bhid,bhdv->bhiv', qi, state)
        state = state * di[..., None] + jnp.einsum('bhjd,bhjv->bhdv', ki, vi)
        return state, o

    s0 = jnp.zeros((B, H, DK, DV), jnp.float32)
    _, o_inter = lax.scan(step, s0, (q_inter, k_state, vc, decay))
    o = o_intra + o_inter
    return o.transpose(1, 0, 3, 2, 4).reshape(B, S, H, DV).astype(v.dtype)

def gla_branch(q, k, v, lr_f, lr_b, w_g_f, b_g_f, w_g_b, b_g_b, out_norm):
    B, S, _ = q.shape
    q = (q * GLA_DK ** -0.5).reshape(B, S, GLA_HEADS, GLA_DK)
    k = k.reshape(B, S, GLA_HEADS, GLA_DK)
    v = v.reshape(B, S, GLA_HEADS, GLA_DV)
    la_f = (jax.nn.log_sigmoid((lr_f @ w_g_f + b_g_f).astype(jnp.float32)) / GLA_TAU)
    la_b = (jax.nn.log_sigmoid((lr_b @ w_g_b + b_g_b).astype(jnp.float32)) / GLA_TAU)
    la_f = la_f.reshape(B, S, GLA_HEADS, GLA_DK)
    la_b = la_b.reshape(B, S, GLA_HEADS, GLA_DK)
    o_f = gla_chunked(q, k, v, la_f)
    flip = lambda t: jnp.flip(t, axis=1)
    o_b = flip(gla_chunked(flip(q), flip(k), flip(v), flip(la_b)))
    o = rmsnorm(o_f + o_b, out_norm)
    return o.reshape(B, S, GLA_WIDTH)

def second_inputs(seed: int = 0) -> dict:
    key = jax.random.key(seed)
    ks = jax.random.split(key, 24)
    nrm = lambda k, shape, fan_in: jax.random.normal(k, shape, jnp.float32) * fan_in ** -0.5
    gain = lambda k, shape: 1.0 + 0.02 * jax.random.normal(k, shape, jnp.float32)
    L = DEPTH_2
    x = jax.random.normal(ks[0], (BATCH, SEQ, D_MODEL), jnp.float32)
    p = jax.random.normal(ks[1], (DEPTH_2, BATCH, SEQ, PLE_DIM), jnp.float32)
    offs = jax.random.randint(ks[2], (BATCH, 1), 0, 1024, dtype=jnp.int32)
    positions = offs + jnp.arange(SEQ, dtype=jnp.int32)[None, :]
    return {
        "x": x,
        "p": p,
        "positions": positions,
        "ln_mix": gain(ks[3], (L, D_MODEL)),
        "w_in": nrm(ks[4], (L, D_MODEL, D_IN), D_MODEL),
        "mla_q_norm": gain(ks[5], (L, MLA_Q_RANK)),
        "w_uq": nrm(ks[6], (L, MLA_Q_RANK, MLA_HEADS * (MLA_NOPE + MLA_ROPE)), MLA_Q_RANK),
        "mla_kv_norm": gain(ks[7], (L, MLA_KV_RANK)),
        "w_ukv": nrm(ks[8], (L, MLA_KV_RANK, MLA_HEADS * (MLA_NOPE + MLA_V)), MLA_KV_RANK),
        "gla_w_gate_fwd": nrm(ks[9], (L, GLA_GATE_RANK, GLA_HEADS * GLA_DK), GLA_GATE_RANK),
        "gla_b_gate_fwd": 0.1 * jax.random.normal(ks[10], (L, GLA_HEADS * GLA_DK), jnp.float32),
        "gla_w_gate_bwd": nrm(ks[11], (L, GLA_GATE_RANK, GLA_HEADS * GLA_DK), GLA_GATE_RANK),
        "gla_b_gate_bwd": 0.1 * jax.random.normal(ks[12], (L, GLA_HEADS * GLA_DK), jnp.float32),
        "gla_out_norm": gain(ks[13], (L, GLA_DV)),
        "w_out": nrm(ks[14], (L, D_MIX_2, D_MODEL), D_MIX_2),
        "ple_norm": gain(ks[15], (L, D_MODEL)),
        "w_ple_gate": nrm(ks[16], (L, D_MODEL, D_MODEL), D_MODEL),
        "w_ple_proj": nrm(ks[17], (L, PLE_DIM, D_MODEL), PLE_DIM),
        "final_norm": gain(ks[18], (D_MODEL,)),
    }

def second_block(x, p, positions, ln_mix, w_in, mla_q_norm, w_uq, mla_kv_norm, w_ukv,
              gla_w_gate_fwd, gla_b_gate_fwd, gla_w_gate_bwd, gla_b_gate_bwd,
              gla_out_norm, w_out, ple_norm, w_ple_gate, w_ple_proj, final_norm):
    h = x
    for i in range(DEPTH_2):
        u = rmsnorm(h, ln_mix[i]) @ w_in[i]
        (c_q, c_kv, k_rope, gate_a, gq, gk, gv, lr_f, lr_b, gate_g) = split_cols(u, IN_SPLITS)
        y_mla = mla_branch(c_q, c_kv, k_rope, positions,
                           mla_q_norm[i], w_uq[i], mla_kv_norm[i], w_ukv[i]) * jax.nn.silu(gate_a)
        y_gla = gla_branch(gq, gk, gv, lr_f, lr_b,
                           gla_w_gate_fwd[i], gla_b_gate_fwd[i],
                           gla_w_gate_bwd[i], gla_b_gate_bwd[i],
                           gla_out_norm[i]) * jax.nn.silu(gate_g)
        h = h + jnp.concatenate([y_mla, y_gla], axis=-1) @ w_out[i]
        gate = jax.nn.sigmoid(rmsnorm(h, ple_norm[i]) @ w_ple_gate[i])
        h = h + gate * (p[i] @ w_ple_proj[i])
    return rmsnorm(h, final_norm)


def setup_inputs(seed=0):
    out = dict(first_inputs(seed))
    for name, value in second_inputs(seed + 1).items():
        if name != "x":
            out[name + "_2"] = value
    return out


def reference(
    x, attn_norm_g, w_in, conv_w, conv_b, conv_ln_g, conv_ln_b, conv_pw_w, conv_pw_b, pool_w,
    pool_scale, q_norm_g, k_norm_g, lambda_q1, lambda_k1, lambda_q2, lambda_k2, attn_sub_norm_g,
    w_out, ffn_norm_g, router_g_w, router_g_b, router_e_w, router_e_b, w_gate, w_up, w_down,
    p_2, positions_2, ln_mix_2, w_in_2, mla_q_norm_2, w_uq_2, mla_kv_norm_2, w_ukv_2,
    gla_w_gate_fwd_2, gla_b_gate_fwd_2, gla_w_gate_bwd_2, gla_b_gate_bwd_2, gla_out_norm_2,
    w_out_2, ple_norm_2, w_ple_gate_2, w_ple_proj_2, final_norm_2,
):
    x = first_block(
        x, attn_norm_g, w_in, conv_w, conv_b, conv_ln_g, conv_ln_b, conv_pw_w, conv_pw_b,
        pool_w, pool_scale, q_norm_g, k_norm_g, lambda_q1, lambda_k1, lambda_q2, lambda_k2,
        attn_sub_norm_g, w_out, ffn_norm_g, router_g_w, router_g_b, router_e_w, router_e_b,
        w_gate, w_up, w_down,
    )
    return second_block(
        x, p_2, positions_2, ln_mix_2, w_in_2, mla_q_norm_2, w_uq_2, mla_kv_norm_2, w_ukv_2,
        gla_w_gate_fwd_2, gla_b_gate_fwd_2, gla_w_gate_bwd_2, gla_b_gate_bwd_2, gla_out_norm_2,
        w_out_2, ple_norm_2, w_ple_gate_2, w_ple_proj_2, final_norm_2,
    )


_drawn_inputs = setup_inputs


def setup_inputs(seed=0):
    import zlib

    import numpy as np

    out = dict(_drawn_inputs(seed))
    spreads = {}
    factors = {'conv_b': 3.333,
     'conv_ln_g': 4.686,
     'conv_ln_b': 5.549,
     'conv_pw_b': 3.004,
     'pool_scale': 4.021,
     'q_norm_g': 4.034,
     'k_norm_g': 3.552,
     'attn_sub_norm_g': 2.822,
     'router_g_b': 7.978,
     'router_e_b': 8.0,
     'ln_mix_2': 3.304,
     'mla_q_norm_2': 8.0,
     'mla_kv_norm_2': 8.0,
     'gla_b_gate_fwd_2': 4.463,
     'gla_b_gate_bwd_2': 4.271,
     'gla_out_norm_2': 6.697,
     'ple_norm_2': 8.0,
     'final_norm_2': 2.791}
    for name, (base, spread) in spreads.items():
        noise = np.random.default_rng([zlib.crc32(name.encode()), seed]).standard_normal(out[name].shape)
        drawn = base * np.exp(spread * noise) if base else spread * noise
        out[name] = __import__('jax').numpy.asarray(drawn.astype(out[name].dtype))
    for name, factor in factors.items():
        out[name] = (out[name] * factor).astype(out[name].dtype)
    return out
```

```python
from contextlib import ExitStack

import numpy as np
import concourse.bass as bass
from concourse import mybir

F32 = mybir.dt.float32
I32 = mybir.dt.int32
U32 = mybir.dt.uint32
ALU = mybir.AluOpType
ACT = mybir.ActivationFunctionType
AX = mybir.AxisListType
ds = bass.ds

P = 128
S = 1024
D = 1024
NT = S // P
KD = D // P
HALF = 512
EPS = 1e-6

TAPS = 31
PADC = TAPS - 1
HEADS = 4
DH = 64
C_POOL0, C_Q, C_K, C_V = 512, 768, 1280, 1792
WINDOWS = (2, 4, 8, 16)
PADP = 16
LAM_INIT = 0.8 - 0.6 * np.exp(-0.3 * 0)
GROUPS, PER_GROUP, EXPERTS = 4, 4, 16
DE = 256
MTILES = EXPERTS + 2 * S // P - 1
NEG = -3.0e38

LAYERS = 2
C_CQ, C_CKV, C_KR, C_GA, C_GQ, C_GK, C_GV, C_LR, C_GG = 0, 384, 640, 704, 1216, 1472, 1728, 2240, 2272
CH = 64
NCH = S // CH
MLA_SCALE = float(np.float32(192) ** np.float32(-0.5))
PLE = 256

V_AG, V_FG, V_CB, V_LG, V_LB, V_PB, V_PS, V_QG, V_KG, V_SG, V_CW = 0, 8, 16, 18, 20, 22, 24, 26, 27, 28, 29
NV1 = V_CW + 2 * TAPS
L_MIX, L_PLE, L_QN, L_KVN, L_GB, L_GO = 0, 8, 16, 19, 21, 25
NV2 = 26
K_INV, K_OFF, K_RAD, K_SIGN, K_SLOPE, K_POOLW, K_POOL16 = 0, 1, 2, 3, 4, 8, 10
NK = K_POOL16 + 2 * 16


def shape_constants():
    c = np.zeros((P, NK), np.float32)
    p = np.arange(P)
    c[:, K_INV] = 10000.0 ** (-(p % 32) / 32.0)
    c[:, K_OFF] = np.where(p < 64, 0.25, 0.0)
    c[:, K_RAD] = np.where(p < 64, np.pi / 2, 0.0)
    c[:, K_SIGN] = np.where((p >= 64) & (p < 96), -1.0, 1.0)
    for h in range(HEADS):
        c[:, K_SLOPE + h] = (2.0 ** (-8.0 / HEADS)) ** (h + 1)
    for i in range(2):
        w = np.where(p < 64, WINDOWS[2 * i], WINDOWS[2 * i + 1])
        c[:, K_POOLW + i] = 1.0 / w
        c[:, K_POOL16 + 16 * i:K_POOL16 + 16 * i + 16] = 1.0 / np.minimum(np.arange(16)[None, :] + 1, w[:, None])
    return c



class Chain:

    def __init__(self, eng, semaphore, base=0):
        self.eng, self.semaphore, self.base, self.n = eng, semaphore, base, 0

    def link(self, ins):
        self.n += 1
        ins.then_inc(self.semaphore, 1)
        self.eng.wait_ge(self.semaphore, self.base + self.n)


def settle(eng, semaphore):
    eng.sem_inc(semaphore, 1)


def accumulate(pe, o, pairs):
    last = len(pairs) - 1
    for i, (l, r) in enumerate(pairs):
        mm = pe.matmul(o, l, r, start=(i == 0), stop=(i == last))
    return mm


def program(nc, A, out):
    ctx = ExitStack()
    with ctx:
        def sb(name, shape, dt=F32):
            return ctx.enter_context(nc.sbuf_tensor(name, shape, dt))

        def sem(name):
            return ctx.enter_context(nc.semaphore(name))

        def sems(name, n):
            return [sem(f"{name}{i}") for i in range(n)]

        H = sb("H", [P, NT, D])
        HT = sb("HT", [P, KD, S])
        MIX = sb("MIX", [P, KD, S])
        WF = sb("WF", [P, 4, KD, P])
        WT = sb("WT", [P, 2, KD, HALF])
        X = sb("X", [P, 10240])
        ident = sb("ident", [P, P])
        ones = sb("ones", [P, P])
        vec1 = sb("vec1", [P, NV1])
        vec2 = sb("vec2", [P, LAYERS, NV2])
        vl = sb("vl", [P, NV2])
        kc = sb("kc", [P, NK])
        eps = sb("eps", [P, 1])
        mhalf = sb("mhalf", [P, 8])
        ss = sb("ss", [P, 8])
        rs = sb("rs", [P, 8])
        stat = sb("stat", [P, 64])
        xn = sb("xn", [P, 2, D])
        rope = sb("rope", [P, S])
        shared = sb("shared", [P, 1280])
        lamt = sb("lamt", [P, 4, DH])
        pwb = sb("pwb", [P, 2, P])
        ps = ctx.enter_context(nc.psum_tensor("ps", [P, 8, HALF], F32))
        psf = ps[:, :, :].rearrange("p b n -> p (b n)")

        def bank(b, n=HALF, at=0):
            return ps[:, b, at:at + n]

        def quads(b):
            return ps[:, b, :].rearrange("p (c n) -> p c n", n=P)

        xn_dram = nc.dram_tensor("xn_dram", (S, D), F32).ap()
        y_dram = nc.dram_tensor("y_dram", (2 * S, D), F32).ap()
        slot_dram = nc.dram_tensor("slot_dram", (MTILES * P, 4), I32).ap()

        Hf = H[:, :, :].rearrange("p t d -> p (t d)")
        HTf = HT[:, :, :].rearrange("p k t -> p (k t)")
        MXf = MIX[:, :, :].rearrange("p k t -> p (k t)")
        WTf = WT[:, :, :, :].rearrange("p s k n -> p (s k n)")
        WFf = WF[:, :, :, :].rearrange("p s k n -> p (s k n)")

        u_pad = Hf[:, 0:2108].rearrange("p (c t) -> p c t", c=2)
        y_cv = Hf[:, 2108:4156].rearrange("p (c t) -> p c t", c=2)
        sq_cv = Hf[:, 4156:6204].rearrange("p (c t) -> p c t", c=2)
        wB = Hf[:, 6204:7244]
        sig_g = MXf[:, 0:2048].rearrange("p (c t) -> p c t", c=2)
        r_cv = MXf[:, 0:1024]
        p_pad = MXf[:, 4096:6176].rearrange("p (c t) -> p c t", c=2)
        wA = MXf[:, 6176:7216]
        fix16 = MXf[:, 7216:7232]
        qT = X[:, 0:4096].rearrange("p (h t) -> p h t", h=4)
        kT = X[:, 4096:8192].rearrange("p (h t) -> p h t", h=4)
        qtok = X[:, 8192:9216].rearrange("p (b n) -> p b n", b=2)
        qn = X[:, 9216:10240].rearrange("p (b n) -> p b n", b=2)
        V1 = WFf.rearrange("p (t n) -> p t n", t=NT)
        qz = X[:, 8192:10240].rearrange("p (m t) -> p m t", m=2)
        sS = HTf[:, 0:4096].rearrange("p (b m t) -> p b m t", b=2, m=2)
        ATb = HTf[:, 4096:6144].rearrange("p (b k q) -> p b k q", b=2, k=8)
        BH = HTf[:, 6144:7168]
        on = HTf[:, 7168:7424].rearrange("p (b q) -> p b q", b=2)
        osq = HTf[:, 7424:7552]
        qsum = stat[:, 0:16].rearrange("p (b g) -> p b g", b=2)
        qrs = stat[:, 16:32].rearrange("p (b g) -> p b g", b=2)
        lam4 = stat[:, 32:40]
        sm = sb("sm", [P, 2, 16])
        cpw = xn[:, 0, 512:1024].rearrange("p (k n) -> p k n", k=2)
        lgT = X[:, 0:1024]
        rb = X[:, 1024:1044]
        R0 = 1056

        def rbuf(at, *shape):
            n = int(np.prod(shape))
            v = X[:, R0 + at:R0 + at + n]
            if len(shape) == 2:
                v = v.rearrange("p (a b) -> p a b", a=shape[0])
            if len(shape) == 3:
                v = v.rearrange("p (a b c) -> p a b c", a=shape[0], b=shape[1])
            return v
        lg = rbuf(0, NT, 20)
        first4 = rbuf(160, 4)
        g_max, g_sum, g_p, m1, v1, v2, w1, w2, den, pos1, pos2 = (rbuf(176 + 8 * i, NT) for i in range(11))
        ge, geq, oh, le, leq, oh1, oh2, pe2 = (rbuf(272 + 32 * i, NT, 4) for i in range(8))
        lsel = rbuf(544, NT, 4, 4)
        S1, S2, MM = rbuf(672, NT, 16), rbuf(800, NT, 16), rbuf(928, NT, 16)
        posn, toff, tmpe = rbuf(1056, NT, 16), rbuf(1184, NT, 16), rbuf(1312, NT, 16)
        cnt, tiles_f, tend, tbase, one16 = (rbuf(1440 + 16 * i, 16) for i in range(5))
        tiles_i = rbuf(1520, 16).bitcast(I32)
        cmpt = rbuf(1552, MTILES + 1, 16)
        iot = rbuf(2064, MTILES + 1)
        et_f = rbuf(2096, MTILES + 1)
        et_i = rbuf(2128, MTILES + 1).bitcast(I32)
        rows = rbuf(2160, NT, 2, 4).bitcast(I32)
        rows_f = rbuf(2160, NT, 2, 4)
        sidx = rbuf(2224, NT, 2).bitcast(I32)
        initrow = rbuf(2240, MTILES, 4).bitcast(I32)
        initrow_f = rbuf(2240, MTILES, 4)
        tri = rbuf(2368, P)
        tokid = rbuf(2496, NT)
        tab = rbuf(2512, 2, 4).bitcast(I32)
        tab_f = rbuf(2512, 2, 4)
        M0 = R0 + 2528
        sgb = X[:, M0:M0 + 512].rearrange("p (b n) -> p b n", b=2)
        actb = X[:, M0 + 512:M0 + 1024].rearrange("p (b n) -> p b n", b=2)
        actT = X[:, M0 + 1024:M0 + 1536].rearrange("p (b k n) -> p b k n", b=2, k=2)
        yb = X[:, M0 + 1536:M0 + 3584].rearrange("p (b n) -> p b n", b=2)
        wd = MXf[:, 0:4096].rearrange("p (b k n) -> p b k n", b=2, k=2)
        hg = MXf[:, 4096:6144].rearrange("p (b n) -> p b n", b=2)
        hgT = MXf[:, 6144:8192].rearrange("p (b k n) -> p b k n", b=2, k=KD)

        def slot(flat, i, n=1):
            return flat[:, i * S:(i + n) * S]
        q_dup = [slot(X, 0), slot(X, 1)]
        k_dup = [slot(X, 2), slot(X, 3)]
        cum, la, gt, q_in, sqg = (slot(X, i) for i in range(4, 9))
        wgs = X[:, 9 * S:9 * S + 4 * P].rearrange("p (h n) -> p h n", h=4)
        refs, lasts, decay = (X[:, 9 * S + 512 + 16 * i:9 * S + 528 + 16 * i] for i in range(3))
        kf, kb = slot(WTf, 0), slot(WTf, 1)
        q_even, q_odd = slot(WTf, 2), slot(WTf, 3)
        kv = slot(WTf, 4, 2).rearrange("p (c v) -> p c v", c=NCH)
        st = slot(WTf, 6, 2).rearrange("p (c v) -> p c v", c=NCH)
        ks_even, ks_odd, Af, Ab = (MIX[:, i, :] for i in range(4))
        gv = [slot(WFf, 2), slot(WFf, 3)]
        lrz = xn[:, 0, :]
        reset = shared[:, 0:S]
        mask_f, mask_b = shared[:, S:S + P], shared[:, S + P:S + 2 * P]
        c_q = [slot(X, i) for i in range(3)]
        c_kv = [slot(X, 3), slot(X, 4)]
        kr = slot(X, 5)
        sq_q = [slot(X, 6), slot(X, 7), xn[:, 0, :]]
        sq_kv = [xn[:, 1, :], slot(X, 8)]
        r_q, r_kv = slot(X, 9), slot(X, 6)
        PT = [WTf[:, 4 * S:8 * S].rearrange("p (k q) -> p k q", k=KD), X[:, 6 * S:10 * S].rearrange("p (k q) -> p k q", k=KD)]
        uq = [WFf[:, o:o + 768].rearrange("p (k n) -> p k n", k=3) for o in (2048, 0)]
        ukv = [WFf[:, o + 768:o + 1280].rearrange("p (k n) -> p k n", k=2) for o in (2048, 0)]
        rtmp = WFf[0:64, 1280:1792]
        p_tok = slot(X, 0, 2).rearrange("p (t c) -> p t c", t=NT)
        pT = slot(X, 2, 2).rearrange("p (c t) -> p c t", c=2)
        wpp = slot(X, 4, 2).rearrange("p (c n) -> p c n", c=2)
        sgp = slot(X, 6).rearrange("p (b n) -> p b n", b=2)
        gp = X[:, 7 * S:7 * S + HALF]
        fgain = MIX[:, 0, :]
        pos_i = X[:, 7 * S:8 * S].bitcast(I32)
        ang, turns = slot(X, 8), slot(X, 9)

        UNITS = [("lr", 0, C_LR, 32)]
        for pair in range(2):
            UNITS += [("gq", pair, C_GQ + pair * P, P), ("gk", pair, C_GK + pair * P, P)]
            for h in (2 * pair, 2 * pair + 1):
                UNITS += [("gv", h, C_GV + h * P, P), ("gg", h, C_GG + h * P, P)]
        UNITS += [("cq", i, C_CQ + i * P, P) for i in range(3)] + [("ckv", i, C_CKV + i * P, P) for i in range(2)]
        UNITS += [("kr", 0, C_KR, P)] + [("ga", i, C_GA + i * P, P) for i in range(4)]
        NU = len(UNITS)
        UI = {(k, i): u for u, (k, i, _, _) in enumerate(UNITS)}
        W_DMAS = [3 if k == "kr" else 1 for k, _, _, _ in UNITS]
        W_SOFAR = [sum(W_DMAS[v] for v in range(u % 2, u + 1, 2)) for u in range(NU)]
        W_LAYER = [sum(W_DMAS[s::2]) for s in range(2)]
        FILLS = [("p", 0, j) for j in range(8)]
        STEPS = 4 * NT + 2
        for g in range(STEPS):
            if g // NT + 1 < 4 and g < 4 * NT:
                FILLS.append(("p", g // NT + 1, g % NT))
            if g >= 5 and (g - 2) % 4 == 3:
                FILLS.append(("v", (g - 2) // 4, 0))
        NF = len(FILLS)
        FI = {f: i for i, f in enumerate(FILLS)}

        x_in = sems("x_in", NT)
        const_in, idready = sem("const_in"), sem("idready")
        n_ss, n_rs, n_xn = sem("n_ss"), sem("n_rs"), sem("n_xn")
        n_tp, n_ht = sem("n_tp"), sem("n_ht")
        pool_chain, dve_chain, act_chain = sem("pool_chain"), sem("dve_chain"), sem("act_chain")
        b_w, b_ready, b_evac = sems("b_w", 3), sem("b_ready"), sems("b_evac", 2)
        p_ready = sem("p_ready")
        c_w, c_ready, c_evac = sems("c_w", 2), sem("c_ready"), sem("c_evac")
        c_red, c_rs, c_qn, c_tp, c_tev = (sem(n) for n in ("c_red", "c_rs", "c_qn", "c_tp", "c_tev"))
        cv_dve, pool_d = sem("cv_dve"), sem("pool_d")
        pl_ready, pl_evac = sem("pl_ready"), sem("pl_evac")
        ln_mu, ln_xc, ln_sq, ln_var, ln_sd, ln_n, ln_ys, pw_ready, pw_evac = (
            sem(n) for n in ("ln_mu", "ln_xc", "ln_sq", "ln_var", "ln_sd", "ln_n", "ln_ys", "pw_ready", "pw_evac"))
        lam_e, padded = sem("lam_e"), sem("padded")
        cpw_in, pwb_in = sem("cpw_in"), sem("pwb_in")
        qz_ready, s_ready, s_max, s_neg, e_ready, a_ready, t_ready, at_evac, o_ready, o_sq, o_rs, o_n, ot_ready, ot_evac = (
            sem(n) for n in ("qz_ready", "s_ready", "s_max", "s_neg", "e_ready", "a_ready", "t_ready", "at_evac",
                             "o_ready", "o_sq", "o_rs", "o_n", "ot_ready", "ot_evac"))
        wo_w, wo_ready, wo_evac = sems("wo_w", 2), sem("wo_ready"), sem("wo_evac")
        xn_st = sems("xn_st", 2)
        rw_zero, rw_in, rt_ready, rt_cp, rt_tp = (
            sem(n) for n in ("rw_zero", "rw_in", "rt_ready", "rt_cp", "rt_tp"))
        rx, rx_done, rm_ready, rp_ready, slots_set, slots_init, slots_in, experts_set = (
            sem(n) for n in ("rx", "rx_done", "rm_ready", "rp_ready", "slots_set", "slots_init", "slots_in", "experts_set"))
        iotas = sem("iotas")
        m_wgu, m_wd, m_tab, m_hg, m_sc = (sems(n, 2) for n in ("m_wgu", "m_wd", "m_tab", "m_hg", "m_sc"))
        m_xt, m_ht, m_gu, m_sg, m_act, m_at, m_aT, m_dn, m_y = (
            sem(n) for n in ("m_xt", "m_ht", "m_gu", "m_sg", "m_act", "m_at", "m_aT", "m_dn", "m_y"))
        y_in, h_in = sems("y_in", 2), sem("h_in")
        comb = sem("comb")
        v2_in, vl_ready, pos_in, rope_set, masks_set = (
            sem(n) for n in ("v2_in", "vl_ready", "pos_in", "rope_set", "masks_set"))
        z_ready, lz_ready, hz_ready, wg_in = (sem(n) for n in ("z_ready", "lz_ready", "hz_ready", "wg_in"))
        u_w, u_ready, u_evac = sems("u_w", 2), sem("u_ready"), sems("u_evac", 2)
        g_pe, g_act, g_dve = sem("g_pe"), sem("g_act"), sem("g_dve")
        GLA_STEPS = {g_pe: [("z", 0)], g_act: [("t", 0), ("e", 0)], g_dve: [("d", 0), ("k", 0), ("q", 0)]}
        for h in range(4):
            more = h < 3
            GLA_STEPS[g_pe] += [("a", h), ("kt", h), ("kv", h)] + [("z", h + 1)] * more + [("o", h), ("ms", h)]
            GLA_STEPS[g_act] += [("ks", h), ("kvc", h)] + [("t", h + 1), ("e", h + 1)] * more + [("sq", h), ("r", h)]
            GLA_STEPS[g_dve] += [("am", h), ("st", h)] + [("d", h + 1), ("k", h + 1), ("q", h + 1)] * more + [("done", h)]
        GLA_AT = {step: (s, i) for s, steps in GLA_STEPS.items() for i, step in enumerate(steps)}

        def gla(L, step, h):
            s, i = GLA_AT[(step, h)]
            return s, L * len(GLA_STEPS[s]) + i + 1

        l_ms, l_r, l_c = sem("l_ms"), sem("l_r"), sem("l_c")
        uw, f_ready, f_evac = sems("uw", 2), sem("f_ready"), sems("f_evac", 2)
        a_s, a_neg, a_e, a_p, a_t, a_tev = sem("a_s"), sem("a_neg"), sem("a_e"), sem("a_p"), sems("a_t", 2), sems("a_tev", 2)
        p_in, p_tp, p_ev, pg_ready, pg_sg, pg_evac = sem("p_in"), sem("p_tp"), sem("p_ev"), sem("pg_ready"), sem("pg_sg"), sem("pg_evac")
        fg_in, f_ss, f_rs, f_out, out_st = sem("fg_in"), sem("f_ss"), sem("f_rs"), sem("f_out"), sem("out_st")


        settled = sem("settled")

        block = ctx.enter_context(nc.Block())

        def nt_act(act, N, ready, stored=None):
            for t in range(NT):
                ready(t)
                if t >= 2:
                    act.wait_ge(n_ss, N * NT + t - 1)
                act.activation(xn[:, t % 2, :], H[:, t, :], ACT.Square, accum_out=ss[:, t:t + 1]).then_inc(n_ss, 1)
            act.wait_ge(n_rs, N + 1)
            act.wait_ge(n_ss, N * NT + NT)
            with act.Fori(0, NT // 2) as i:
                for p in range(2):
                    act.wait_ge(n_tp, N * NT + i * 2 + p + 1)
                    if stored is not None:
                        act.wait_ge(stored[p], i * 16 + 16)
                    act.activation(xn[:, p, :], H[:, ds(i * 2 + p, 1), :].rearrange("p a d -> p (a d)"), ACT.Copy,
                                   scale=rs[:, ds(i * 2 + p, 1)]).then_inc(n_xn, 1)

        def nt_pool(pool, chain, N):
            pool.wait_ge(n_ss, N * NT + NT)
            settle(pool, settled)
            chain.link(pool.tensor_scalar(ss[:, :], ss[:, :], 1.0 / D, EPS, ALU.mult, ALU.add))
            pool.tensor_tensor(rs[:, :], ss[:, :], mhalf[:, :], ALU.pow).then_inc(n_rs, 1)

        def nt_pe(pe, N):
            with pe.Fori(0, NT // 2) as i:
                for p in range(2):
                    pe.wait_ge(n_xn, N * NT + i * 2 + p + 1)
                    pe.wait_ge(n_ht, N * NT + i * 2 + p + 1)
                    for c in range(KD):
                        tp = pe.transpose(bank(2 + 2 * p + c // 4, P, (c % 4) * P), xn[:, p, c * P:(c + 1) * P], ident[:, :])
                    tp.then_inc(n_tp, 1)

        def nt_dve(dve, N, gain):
            with dve.Fori(0, NT // 2) as i:
                for p in range(2):
                    dve.wait_ge(n_tp, N * NT + i * 2 + p + 3)
                    for c in range(2):
                        g = gain[:, 4 * c:4 * c + 4].unsqueeze(2).to_broadcast([P, 4, P])
                        tt = dve.tensor_tensor(HT[:, 4 * c:4 * c + 4, ds((i * 2 + p) * P, P)], quads(2 + 2 * p + c), g, ALU.mult)
                    tt.then_inc(n_ht, 1)

        def layers(eng, layer):
            with eng.Fori(0, LAYERS) as L:
                layer(L)

        def unit_evac(L, u, half):
            return L * NU + (u + 2)

        def fill_evac(L, f):
            return L * (NF // 2) + (f // 2 + 2)

        @block.sync
        def _(sp):
            for p in range(2):
                sp.sem_inc(xn_st[p], 16)
            for t in range(NT):
                sp.dma_start(H[:, t, :], A["x"][0, t * P:(t + 1) * P, :]).then_inc(x_in[t], 16)
            for u in range(6):
                c, kind = u // 3, u % 3
                c0 = (256, 0, C_POOL0)[kind] + c * P
                if u >= 3:
                    sp.wait_ge(b_ready, 2 * (u - 3) + 2)
                sp.dma_start(WF[:, kind, :, :], A["w_in"][0, :, c0:c0 + P].rearrange("(k p) c -> p k c", p=P)).then_inc(b_w[kind], 16)
            for b in range(3):
                if b == 2:
                    sp.wait_ge(c_ready, NT)
                sp.dma_start(WT[:, b % 2, :, :], A["w_in"][0, :, C_Q + b * HALF:C_Q + (b + 1) * HALF]
                             .rearrange("(k p) c -> p k c", p=P)).then_inc(c_w[b % 2], 16)
                if b == 1:
                    sp.wait_ge(b_ready, 1)
                    sp.dma_start(cpw, A["conv_pw_w"][0].rearrange("(k p) n -> p k n", p=P)).then_inc(cpw_in, 16)
            for n in (1, 0):
                sp.wait_ge(c_ready, (3 - n) * NT)
                sp.dma_start(WT[:, n, :, :], A["w_out"][0, :, n * HALF:(n + 1) * HALF].rearrange("(k p) c -> p k c", p=P)).then_inc(wo_w[n], 16)
            sp.wait_ge(pw_ready, 4)
            sp.wait_ge(pl_ready, 4)
            for t in range(NT):
                sp.dma_start(H[:, t, :], A["x"][0, t * P:(t + 1) * P, :]).then_inc(x_in[t], 16)
            sp.wait_ge(o_ready, HEADS * NT)
            sp.wait_ge(ot_evac, HEADS * NT)
            sp.dma_start(pos_i, A["positions_2"][0:1, :].to_broadcast([P, S])).then_inc(pos_in, 16)
            with nc.allow_non_contiguous_dma(reason="gains and biases, one value a partition"):
                for l in range(LAYERS):
                    for at, n, name in ((L_MIX, 8, "ln_mix_2"), (L_PLE, 8, "ple_norm_2"), (L_QN, 3, "mla_q_norm_2"),
                                        (L_KVN, 2, "mla_kv_norm_2"), (L_GO, 1, "gla_out_norm_2")):
                        sp.dma_start(vec2[:, l, at:at + n], A[name][l].rearrange("(c p) -> p c", p=P)).then_inc(v2_in, 16)
                    for r, name in ((slice(0, 64), "gla_b_gate_fwd_2"), (slice(64, P), "gla_b_gate_bwd_2")):
                        sp.dma_start(vec2[r, l, L_GB:L_GB + 4], A[name][l].rearrange("(h p) -> p h", h=4)).then_inc(v2_in, 16)
            sp.dma_start(rb[:, 0:4], A["router_g_b"][0:1, :].to_broadcast([P, 4])).then_inc(rw_in, 16)
            sp.dma_start(rb[:, 4:20], A["router_e_b"][0:1, :].to_broadcast([P, 16])).then_inc(rw_in, 16)
            sp.wait_ge(rw_zero, 1)
            sp.dma_start(WF[:, 0, :, 0:4], A["router_g_w"][0].rearrange("(k p) c -> p k c", p=P)).then_inc(rw_in, 16)
            sp.dma_start(WF[:, 0, :, 4:20], A["router_e_w"][0].rearrange("(k p) c -> p k c", p=P)).then_inc(rw_in, 16)
            with sp.Fori(0, NT // 2) as i:
                for p in range(2):
                    sp.wait_ge(n_xn, i * 2 + (NT + p + 1))
                    sp.dma_start(xn_dram[ds((i * 2 + p) * P, P), :], xn[:, p, :]).then_inc(xn_st[p], 16)
            sp.wait_ge(slots_init, 1)
            sp.dma_start(slot_dram.rearrange("(a p) c -> p a c", p=P), initrow).then_inc(slots_in, 16)
            sp.wait_ge(slots_set, 16 * 2 * NT)
            sp.wait_ge(experts_set, 1)
            sp.wait_ge(wo_ready, 2 * NT)

            def expert_loads(t, i, p, first=False):
                e = sp.value_load(et_i[0:1, ds(t, 1)], min_val=0, max_val=EXPERTS - 1)
                if not first:
                    sp.wait_ge(m_sc[p], i * 16)
                sp.dma_start(tab[:, p, :], slot_dram[ds(t * P, P), :]).then_inc(m_tab[p], 16)
                sp.wait_ge(m_gu, t + 1)
                sp.dma_start(WT[:, p, :, 0:DE], A["w_gate"][0, ds(e, 1)].rearrange("a (k p) c -> p (a k) c", p=P)).then_inc(m_wgu[p], 16)
                sp.dma_start(WT[:, p, :, DE:2 * DE], A["w_up"][0, ds(e, 1)].rearrange("a (k p) c -> p (a k) c", p=P)).then_inc(m_wgu[p], 16)
                sp.wait_ge(m_dn, t + 1)
                sp.dma_start(wd[:, p, :, :], A["w_down"][0, ds(e, 1)].rearrange("a (k p) c -> p (a k) c", p=P)).then_inc(m_wd[p], 16)

            for p in range(2):
                expert_loads(p, 0, p, first=True)
            with sp.Fori(1, MTILES // 2) as i:
                for p in range(2):
                    expert_loads(i * 2 + p, i, p)
            expert_loads(MTILES - 1, MTILES // 2, 0)
            sp.wait_ge(m_sc[0], 16 * (MTILES // 2 + 1))
            sp.wait_ge(m_sc[1], 16 * (MTILES // 2))
            sp.dma_start(HT[:, :, :], y_dram[0:S, :].rearrange("(t p) d -> p t d", p=P)).then_inc(y_in[0], 16)
            sp.wait_ge(m_dn, 2 + MTILES)
            sp.dma_start(MIX[:, :, :], y_dram[S:2 * S, :].rearrange("(t p) d -> p t d", p=P)).then_inc(y_in[1], 16)
            def layer(L):
                win = A["w_in_2"][ds(L, 1)].rearrange("a (k p) c -> p (a k) c", p=P)

                def up_weights(h):
                    s = h % 2
                    wq = A["w_uq_2"][ds(L, 1)].rearrange("a (k p) c -> p (a k) c", p=P)
                    sp.dma_start(uq[s][:, :, 0:192], wq[:, :, h * 192:h * 192 + 192]).then_inc(uw[s], 16)
                    sp.dma_start(uq[s][:, :, 192:224], wq[:, :, h * 192 + 160:h * 192 + 192]).then_inc(uw[s], 16)
                    sp.dma_start(uq[s][:, :, 224:256], wq[:, :, h * 192 + 128:h * 192 + 160]).then_inc(uw[s], 16)
                    sp.dma_start(ukv[s], A["w_ukv_2"][ds(L, 1), :, h * 256:h * 256 + 256].rearrange("a (k p) c -> p (a k) c", p=P)).then_inc(uw[s], 16)
                for u, (kind, i, c0, n) in enumerate(UNITS):
                    if u >= 2:
                        sp.wait_ge(u_ready, L * 2 * NU + 2 * (u - 1))
                        settle(sp, settled)
                    if kind == "kr":
                        for to, c, m in ((0, c0, 64), (64, c0 + 32, 32), (96, c0, 32)):
                            sp.dma_start(WF[:, u % 2, :, to:to + m], win[:, :, c:c + m]).then_inc(u_w[u % 2], 16)
                        up_weights(0)
                    else:
                        sp.dma_start(WF[:, u % 2, :, 0:n], win[:, :, c0:c0 + n]).then_inc(u_w[u % 2], 16)
                    if u == 1:
                        sp.wait_ge(z_ready, L + 1)
                        for r, name in ((0, "gla_w_gate_fwd_2"), (1, "gla_w_gate_bwd_2")):
                            sp.dma_start(wgs[16 * r:16 * r + 16, :, 64 * r:64 * r + 64],
                                         A[name][ds(L, 1)].rearrange("a r (h d) -> r (a h) d", h=4)).then_inc(wg_in, 16)
                sp.dma_start(WT[:, 0, :, :], A["w_out_2"][ds(L, 1), :, 0:HALF].rearrange("a (k p) c -> p (a k) c", p=P)).then_inc(wo_w[0], 16)
                sp.wait_ge(u_ready, L * 2 * NU + 2 * NU)
                up_weights(1)
                for h in (2, 3):
                    sp.wait_ge(f_ready, L * NF + FI[("p", h - 2, 7)] + 1)
                    up_weights(h)
                sp.wait_ge(f_ready, L * NF + FI[("v", 6, 0)] + 1)
                sp.dma_start(WT[:, 1, :, :], A["w_out_2"][ds(L, 1), :, HALF:D].rearrange("a (k p) c -> p (a k) c", p=P)).then_inc(wo_w[1], 16)
                sp.wait_ge(f_ready, L * NF + NF)
                sp.dma_start(p_tok, A["p_2"][ds(L, 1), 0].rearrange("a (t p) c -> p (a t) c", p=P)).then_inc(p_in, 16)
                sp.dma_start(wpp, A["w_ple_proj_2"][ds(L, 1)].rearrange("a (k p) c -> p (a k) c", p=P)).then_inc(p_in, 16)
                for n in range(2):
                    sp.wait_ge(wo_ready, L * 2 * NT + (n + 3) * NT)
                    sp.dma_start(WT[:, n, :, :], A["w_ple_gate_2"][ds(L, 1), :, n * HALF:(n + 1) * HALF]
                                 .rearrange("a (k p) c -> p (a k) c", p=P)).then_inc(wo_w[n], 16)
            layers(sp, layer)
            sp.dma_start(fgain, A["final_norm_2"].rearrange("(a d) -> a d", a=1).to_broadcast([P, D])).then_inc(fg_in, 16)
            for t in range(NT):
                sp.wait_ge(f_out, t + 1)
                sp.dma_start(out[0, t * P:(t + 1) * P, :], HT[:, t, :]).then_inc(out_st, 16)
            sp.wait_ge(out_st, 16 * NT)

        @block.gpsimd
        def _(pool):
            chain = Chain(pool, pool_chain)
            chain.link(pool.memset(ident[:, :], 0.0))
            pool.affine_select(out=ident[:, :], in_=ident[:, :], pattern=[[-1, P]], compare_op=ALU.not_equal, fill=1.0,
                               base=0, channel_multiplier=1).then_inc(idready, 1)
            pool.memset(ones[:, :], 1.0).then_inc(idready, 1)
            pool.memset(mhalf[:, :], -0.5)
            pool.memset(eps[:, :], EPS).then_inc(idready, 1)
            pool.memset(pwb[:, :, :], 0.0).then_inc(padded, 1)
            chain.link(pool.iota(shared[:, 0:S], pattern=[[1, S]], base=-(S - P), channel_multiplier=-1, allow_small_or_imprecise_dtypes=True))
            pool.affine_select(out=shared[:, 0:S], in_=shared[:, 0:S], pattern=[[-1, S]], compare_op=ALU.is_ge, fill=NEG,
                               base=S - P, channel_multiplier=1).then_inc(idready, 1)
            nt_pool(pool, chain, 0)

            for n in range(2 * NT):
                pool.wait_ge(c_red, n + 1)
                if n >= 2:
                    pool.wait_ge(c_qn, n - 1)
                chain.link(pool.tensor_scalar(qsum[:, n % 2, :], qsum[:, n % 2, :], 1.0 / DH, EPS, ALU.mult, ALU.add))
                pool.tensor_tensor(qrs[:, n % 2, :], qsum[:, n % 2, :], mhalf[:, :], ALU.pow).then_inc(c_rs, 1)
            pool.wait_ge(p_ready, 4)
            W0 = S + PADP
            for c in range(2):
                pp = p_pad[:, c, :]
                chain.link(pool.tensor_tensor(wA[:, 1:W0], pp[:, 1:W0], pp[:, 0:W0 - 1], ALU.add))
                if c == 0:
                    chain.link(pool.tensor_tensor(wB[64:P, 3:W0], wA[64:P, 3:W0], wA[64:P, 1:W0 - 2], ALU.add))
                else:
                    chain.link(pool.tensor_tensor(wB[:, 3:W0], wA[:, 3:W0], wA[:, 1:W0 - 2], ALU.add))
                    chain.link(pool.tensor_tensor(wA[:, 7:W0], wB[:, 7:W0], wB[:, 3:W0 - 4], ALU.add))
                    chain.link(pool.tensor_tensor(wB[64:P, 15:W0], wA[64:P, 15:W0], wA[64:P, 7:W0 - 8], ALU.add))
                for lo, ww in ((0, wA), (64, wB)):
                    r = slice(lo, lo + 64)
                    k16 = kc[r, K_POOL16 + 16 * c:K_POOL16 + 16 * c + 16]
                    chain.link(pool.tensor_tensor(fix16[r, :], ww[r, PADP:2 * PADP], k16, ALU.mult))
                    pool.tensor_tensor(pp[r, PADP:2 * PADP], fix16[r, :], pp[r, PADP:2 * PADP], ALU.subtract)
                    chain.link(pool.tensor_scalar(ww[r, 2 * PADP:W0], ww[r, 2 * PADP:W0], kc[r, K_POOLW + c:K_POOLW + c + 1], None, ALU.mult))
                    last = pool.tensor_tensor(pp[r, 2 * PADP:W0], ww[r, 2 * PADP:W0], pp[r, 2 * PADP:W0], ALU.subtract)
                    chain.link(last)
            pool.sem_inc(pool_d, 1)

            pool.wait_ge(c_tp, 2 * NT)
            pool.wait_ge(c_tev, 2 * NT)
            chain.link(pool.memset(qz[:, :, :], 0.0))
            pool.tensor_copy(qz[0:64, 0, :], qT[0:64, 0, :])
            pool.tensor_copy(qz[64:P, 1, :], qT[64:P, 0, :]).then_inc(qz_ready, 1)
            base = chain.n

            def head(h, stage):
                pool.wait_ge(qz_ready, h + 1)
                for b in range(NT):
                    pool.wait_ge(o_sq, h * NT + b + 1)
                    settle(pool, settled)
                    pool.tensor_scalar(sm[:, b % 2, 8:9], sm[:, b % 2, 8:9], 1.0 / P, EPS, ALU.mult, ALU.add).then_inc(pool_chain, 1)
                    pool.wait_ge(pool_chain, h * NT + (base + b + 1))
                    pool.tensor_tensor(sm[:, b % 2, 9:10], sm[:, b % 2, 8:9], mhalf[:, 0:1], ALU.pow).then_inc(o_rs, 1)
                if stage:
                    pool.wait_ge(s_ready, h * 2 * NT + 2 * NT)
                    pool.wait_ge(o_rs, h * NT + NT)
                    pool.tensor_copy(qz[0:64, 0, :], qT[0:64, ds(h + 1, 1), :].rearrange("p a t -> p (a t)"))
                    pool.tensor_copy(qz[64:P, 1, :], qT[64:P, ds(h + 1, 1), :].rearrange("p a t -> p (a t)")).then_inc(qz_ready, 1)
            with pool.Fori(0, HEADS - 1) as h:
                head(h, True)
            head(HEADS - 1, False)
            chain.n = base + HEADS * NT

            pool.wait_ge(ot_evac, HEADS * NT)
            chain.link(pool.memset(shared[:, :], 1.0))
            pool.memset(reset.rearrange("p (c i) -> p c i", c=NCH)[:, :, 0:1], 0.0)
            pool.affine_select(out=mask_f, in_=mask_f, pattern=[[1, P]], compare_op=ALU.is_ge, fill=0.0, base=0, channel_multiplier=-1)
            chain.link(pool.affine_select(out=mask_b, in_=mask_b, pattern=[[-1, P]], compare_op=ALU.is_ge, fill=0.0, base=0, channel_multiplier=1))
            chain.link(pool.memset(mask_f[0:64, CH:P], 0.0))
            chain.link(pool.memset(mask_b[64:P, 0:CH], 0.0))
            pool.sem_inc(masks_set, 1)
            pool.wait_ge(o_ready, HEADS * NT)
            pool.wait_ge(ot_evac, HEADS * NT)
            pool.memset(WF[:, 0, :, :], 0.0).then_inc(rw_zero, 1)
            chain.link(pool.memset(tri, 1.0))
            pool.affine_select(out=tri, in_=tri, pattern=[[1, P]], compare_op=ALU.is_gt, fill=0.0, base=0, channel_multiplier=-1).then_inc(iotas, 1)
            pool.iota(first4, pattern=[[-1, 4]], base=4, channel_multiplier=0, allow_small_or_imprecise_dtypes=True)
            pool.iota(iot, pattern=[[1, MTILES + 1]], base=0, channel_multiplier=0, allow_small_or_imprecise_dtypes=True)
            pool.iota(tokid, pattern=[[P, NT]], base=0, channel_multiplier=1, allow_small_or_imprecise_dtypes=True)
            pool.memset(one16, 1.0)
            pool.iota(initrow[:, :, 0:1], pattern=[[0, MTILES]], base=0, channel_multiplier=0)
            pool.iota(initrow[:, :, 1:2], pattern=[[0, MTILES]], base=1 << 20, channel_multiplier=0)
            pool.memset(initrow_f[:, :, 2:4], 0.0).then_inc(slots_init, 1)
            pool.iota(rows[:, :, 0, 0:1], pattern=[[P, NT]], base=0, channel_multiplier=1)
            pool.iota(rows[:, :, 1, 0:1], pattern=[[P, NT]], base=0, channel_multiplier=1)
            pool.iota(rows[:, :, 0, 1:2], pattern=[[P, NT]], base=0, channel_multiplier=1)
            pool.iota(rows[:, :, 1, 1:2], pattern=[[P, NT]], base=S, channel_multiplier=1)
            pool.memset(rows_f[:, :, :, 3:4], 0.0).then_inc(iotas, 1)
            nt_pool(pool, chain, 1)
            pool.wait_ge(slots_in, 16)
            pool.wait_ge(rx_done, 1)
            for t in range(NT):
                for k in range(2):
                    pool.indirect_dma_start(out=slot_dram[:, :], out_offset=bass.IndirectOffsetOnAxis(ap=sidx[:, t, k:k + 1].bitcast(U32), axis=0),
                                            in_=rows[:, t, k, :], in_offset=None).then_inc(slots_set, 16)
            pool.wait_ge(xn_st[0], 16 * 5)
            pool.wait_ge(xn_st[1], 16 * 5)

            def gather(t, i, p):
                pool.wait_ge(m_tab[p], i * 16 + 16)
                pool.wait_ge(m_xt, t + 1)
                settle(pool, settled)
                pool.indirect_dma_start(out=hg[:, p, :], out_offset=None, in_=xn_dram[:, :],
                                        in_offset=bass.IndirectOffsetOnAxis(ap=tab[:, p, 0:1].bitcast(U32), axis=0)).then_inc(m_hg[p], 16)

            def scatter(t, p):
                pool.wait_ge(m_y, t + 2)
                settle(pool, settled)
                pool.indirect_dma_start(out=y_dram[:, :], out_offset=bass.IndirectOffsetOnAxis(ap=tab[:, p, 1:2].bitcast(U32), axis=0),
                                        in_=yb[:, p, :], in_offset=None, bounds_check=2 * S - 1, oob_is_err=False).then_inc(m_sc[p], 16)
            gather(0, 0, 0)
            with pool.Fori(0, MTILES // 2) as i:
                gather(i * 2 + 1, i, 1)
                scatter(i * 2, 0)
                gather(i * 2 + 2, i + 1, 0)
                scatter(i * 2 + 1, 1)
            scatter(MTILES - 1, 0)
            pool.wait_ge(v2_in, 16 * 14)
            base = chain.n

            def layer(L):
                hc = Chain(pool, pool_chain, L * 2 + base)
                pool.wait_ge(h_in, L * NT + NT)
                pool.tensor_copy(vl[:, :], vec2[:, ds(L, 1), :].rearrange("p a n -> p (a n)")).then_inc(vl_ready, 1)
                nt_pool(pool, hc, L * 2 + 2)
                pool.memset(wgs, 0.0)
                pool.memset(WT[:, 0, :, :], 0.0)
                pool.memset(MIX[:, 0:4, :], 0.0).then_inc(z_ready, 1)
                pool.wait_ge(n_tp, L * 2 * NT + 3 * NT + 2)
                settle(pool, settled)
                pool.memset(lrz, 0.0).then_inc(lz_ready, 1)
                pool.wait_ge(*gla(L, "kt", 3))
                settle(pool, settled)
                pool.memset(kr[64:P, :], 0.0)
                pool.wait_ge(u_ready, L * 2 * NU + 2 * NU)
                settle(pool, settled)
                pool.memset(HT[64:P, 1, :], 0.0)
                pool.memset(HT[64:P, 5, :], 0.0).then_inc(hz_ready, 1)
                nt_pool(pool, hc, L * 2 + 3)
                assert hc.n == 2
            layers(pool, layer)
            chain.n = base + 2 * LAYERS
            pool.wait_ge(f_ss, NT)
            chain.link(pool.tensor_scalar(ss[:, :], ss[:, :], 1.0 / D, EPS, ALU.mult, ALU.add))
            pool.tensor_tensor(rs[:, :], ss[:, :], mhalf[:, :], ALU.pow).then_inc(f_rs, 1)

        @block.scalar
        def _(act):
            def vec(dst, src):
                act.dma_start(dst, src).then_inc(const_in, 16)
            with nc.allow_non_contiguous_dma(reason="gains and biases, one value a partition"):
                for at, n, name in ((V_AG, 8, "attn_norm_g"), (V_FG, 8, "ffn_norm_g"), (V_CB, 2, "conv_b"), (V_LG, 2, "conv_ln_g"),
                                    (V_LB, 2, "conv_ln_b"), (V_PB, 2, "conv_pw_b"), (V_PS, 2, "pool_scale"), (V_SG, 1, "attn_sub_norm_g")):
                    vec(vec1[:, at:at + n], A[name][0].rearrange("(c p) -> p c", p=P))
                vec(kc[:, :], A["kc"])
                for m in range(2):
                    vec(vec1[64 * m:64 * m + 64, V_QG:V_QG + 1], A["q_norm_g"][0].rearrange("(p c) -> p c", c=1))
                    vec(vec1[64 * m:64 * m + 64, V_KG:V_KG + 1], A["k_norm_g"][0].rearrange("(p c) -> p c", c=1))
                for c in range(2):
                    vec(vec1[:, V_CW + TAPS * c:V_CW + TAPS * (c + 1)], A["conv_w"][0, :, c * P:(c + 1) * P].rearrange("j p -> p j"))
                for i, name in enumerate(("lambda_q1", "lambda_k1", "lambda_q2", "lambda_k2")):
                    vec(lamt[:, i, :], A[name][0:1, :].to_broadcast([P, DH]))
                act.wait_ge(padded, 1)
                for g in range(4):
                    r = slice(64 * (g % 2), 64 * (g % 2) + 64)
                    act.dma_start(pwb[r, g // 2, r], A["pool_w"][0, g]).then_inc(pwb_in, 16)
            nt_act(act, 0, lambda t: act.wait_ge(x_in[t], 16))
            act.wait_ge(padded, 3)
            for c in range(2):
                for half in range(2):
                    n = 6 * c + half
                    act.wait_ge(b_ready, n + 1)
                    act.activation(sig_g[:, c, half * HALF:(half + 1) * HALF], bank(n % 2), ACT.Sigmoid).then_inc(b_evac[n % 2], 1)
                for half in range(2):
                    n = 6 * c + 4 + half
                    act.wait_ge(b_ready, n + 1)
                    act.activation(p_pad[:, c, PADP + half * HALF:PADP + (half + 1) * HALF], bank(n % 2), ACT.Copy).then_inc(b_evac[n % 2], 1)
            act.drain().then_inc(p_ready, 4)
            act.wait_ge(lam_e, 1)
            act.activation(lam4[:, 2:4], lam4[:, 0:2], ACT.Exp).then_inc(lam_e, 1)
            for n in range(3 * NT):
                act.wait_ge(c_ready, n + 1)
                if n < 2 * NT:
                    if n >= 2:
                        act.wait_ge(c_qn, n - 1)
                        act.wait_ge(c_red, n - 1)
                    act.activation(qtok[:, n % 2, :], bank(n % 2), ACT.Copy)
                    act.activation(xn[:, n % 2, 0:HALF], bank(n % 2), ACT.Square).then_inc(c_evac, 1)
                else:
                    act.activation(V1[:, n - 2 * NT, :], bank(n % 2), ACT.Copy).then_inc(c_evac, 1)
            for c in range(2):
                for half in range(2):
                    n = 2 * c + half
                    act.wait_ge(pl_ready, n + 1)
                    act.activation(MIX[:, 2 + c, half * HALF:(half + 1) * HALF], bank(n), ACT.Copy, scale=vec1[:, V_PS + c:V_PS + c + 1]).then_inc(pl_evac, 1)
            for half in range(2):
                act.wait_ge(ln_xc, half + 1)
                for c in range(2):
                    sq = act.activation(sq_cv[:, c, half * HALF:(half + 1) * HALF], y_cv[:, c, half * HALF:(half + 1) * HALF], ACT.Square)
                sq.then_inc(ln_sq, 1)
            for half in range(2):
                act.wait_ge(ln_var, half + 1)
                act.activation(r_cv[:, half * HALF:(half + 1) * HALF], bank(6 + half), ACT.Sqrt, scale=1.0 / 256, bias=eps[:, 0:1]).then_inc(ln_sd, 1)
            for half in range(2):
                act.wait_ge(ln_n, half + 1)
                for c in range(2):
                    yy = y_cv[:, c, half * HALF:(half + 1) * HALF]
                    si = act.activation(yy, yy, ACT.Silu, scale=vec1[:, V_LG + c:V_LG + c + 1], bias=vec1[:, V_LB + c:V_LB + c + 1])
                si.then_inc(ln_ys, 1)
            for n in range(4):
                half, m = n // 2, n % 2
                act.wait_ge(pw_ready, n + 1)
                act.activation(MIX[:, m, half * HALF:(half + 1) * HALF], bank(n), ACT.Identity, bias=vec1[:, V_PB + m:V_PB + m + 1]).then_inc(pw_evac, 1)

            with act.Fori(0, HEADS) as h:
                g = 0
                for b in range(NT + 1):
                    if b < NT:
                        W = (b + 1) * P
                        for m in range(2):
                            act.wait_ge(s_neg, h * 2 * NT + 2 * b + m + 1)
                            act.activation(sS[:, b % 2, m, 0:W], sS[:, b % 2, m, 0:W], ACT.Exp, bias=sm[:, b % 2, 2 + m:3 + m],
                                           accum_out=sm[:, b % 2, 4 + m:5 + m]).then_inc(e_ready, 1)
                    if b >= 1:
                        q = b - 1
                        for j in range(q // 4 + 1):
                            act.wait_ge(t_ready, h * 12 + g + 1)
                            k = min(4, q + 1 - 4 * j)
                            act.activation(ATb[:, q % 2, 4 * j:4 * j + k, :], quads(4 + j)[:, 0:k, :], ACT.Copy).then_inc(at_evac, 1)
                            g += 1
                        act.wait_ge(o_ready, h * NT + q + 1)
                        act.activation(osq, bank(6, P, (q % 4) * P), ACT.Square, accum_out=sm[:, q % 2, 8:9]).then_inc(o_sq, 1)
                        act.wait_ge(o_rs, h * NT + q + 1)
                        act.activation(on[:, q % 2, :], bank(6, P, (q % 4) * P), ACT.Copy, scale=sm[:, q % 2, 9:10]).then_inc(o_n, 1)
            nt_act(act, 1, lambda t: act.wait_ge(wo_evac, NT + t + 1), stored=xn_st)
            for half in range(2):
                act.wait_ge(rt_ready, half + 1)
                act.activation(lgT[:, half * HALF:(half + 1) * HALF], bank(6 + half), ACT.Copy).then_inc(rt_cp, 1)
            act.wait_ge(rx, 1)
            act.activation(ge, ge, ACT.Exp).then_inc(rx, 1)
            act.wait_ge(rx, 3)
            act.activation(le, le, ACT.Exp).then_inc(rx, 1)
            act.wait_ge(rope_set, 1)
            act.activation(ang, ang, ACT.Sin).then_inc(rope_set, 1)

            def expert_act(t, i, p, first=False):
                act.wait_ge(m_gu, t + 3)
                act.wait_ge(m_act, t + 1)
                act.activation(sgb[:, p, :], bank(2 + p, DE), ACT.Silu).then_inc(m_sg, 1)
                act.wait_ge(m_at, t + 3)
                act.activation(actT[:, p, :, :], quads(4)[:, 0:2, :], ACT.Copy).then_inc(m_aT, 1)
                act.wait_ge(m_dn, t + 3)
                if not first:
                    act.wait_ge(m_sc[p], i * 16)
                act.activation(yb[:, p, :], psf[:, 6 * HALF:8 * HALF], ACT.Copy).then_inc(m_y, 1)
            act.sem_inc(m_aT, 1)
            act.sem_inc(m_y, 1)
            for p in range(2):
                expert_act(p, 0, p, first=True)
            with act.Fori(1, MTILES // 2) as i:
                for p in range(2):
                    expert_act(i * 2 + p, i, p)
            expert_act(MTILES - 1, MTILES // 2, 0)

            for half in range(2):
                act.sem_inc(u_evac[half], 1)
                act.sem_inc(f_evac[half], 1)
            PER = 4 * 2 + 4 + 2

            def layer(L):
                hc = Chain(act, act_chain, L * PER)
                nt_act(act, L * 2 + 2, lambda t: act.wait_ge(h_in, L * NT + t + 1))
                act.wait_ge(vl_ready, L + 1)

                def evac(kind, i):
                    u = UI[(kind, i)]
                    for half in range(2):
                        hs = slice(half * HALF, (half + 1) * HALF)
                        act.wait_ge(u_ready, L * 2 * NU + 2 * u + half + 1)
                        if kind == "lr":
                            act.wait_ge(lz_ready, L + 1)
                            o = act.activation(lrz[0:32, hs], ps[0:32, half, :], ACT.Copy)
                        if kind in ("gq", "gk"):
                            if i == 1:
                                act.wait_ge(*gla(L, "q", 1))
                            dup, scale = (q_dup, 64 ** -0.5) if kind == "gq" else (k_dup, 1.0)
                            for h in range(2):
                                for r in range(2):
                                    o = act.activation(dup[h][64 * r:64 * r + 64, hs], ps[64 * h:64 * h + 64, half, :], ACT.Copy, scale=scale)
                        if kind == "gv":
                            o = act.activation(gv[i % 2][:, hs], bank(half), ACT.Copy)
                        if kind == "gg":
                            o = act.activation(MIX[:, 4 + i, hs], bank(half), ACT.Silu)
                        if kind == "ga":
                            o = act.activation(MIX[:, i, hs], bank(half), ACT.Silu)
                        if kind in ("cq", "ckv"):
                            if (kind, i) == ("cq", 0):
                                act.wait_ge(*gla(L, "q", 3))
                            if (kind, i) == ("ckv", 1):
                                act.wait_ge(*gla(L, "done", 3))
                            to, sq = (c_q, sq_q) if kind == "cq" else (c_kv, sq_kv)
                            act.activation(to[i][:, hs], bank(half), ACT.Copy)
                            o = act.activation(sq[i][:, hs], bank(half), ACT.Square)
                        o.then_inc(u_evac[half], 1)

                def gate(h):
                    act.wait_ge(*gla(L, "z", h))
                    if h >= 1:
                        act.wait_ge(*gla(L, "k", h - 1))
                    for half in range(2):
                        hs, bias = slice(half * HALF, (half + 1) * HALF), vl[:, L_GB + h:L_GB + h + 1]
                        act.activation(la[:, hs], bank(2 + half), ACT.Identity, bias=bias)
                        o = act.activation(gt[:, hs], bank(2 + half), ACT.Abs, bias=bias)
                    hc.link(o)
                    hc.link(act.activation(gt, gt, ACT.Exp, scale=-1.0))
                    act.activation(gt, gt, ACT.Ln, bias=ones[:, 0:1]).then_inc(g_act, 1)

                def exps(h):
                    act.wait_ge(*gla(L, "d", h))
                    if h >= 1:
                        act.wait_ge(*gla(L, "a", h - 1))
                    act.activation(q_in, gt, ACT.Exp, scale=1 / 16.0)
                    act.activation(gt, gt, ACT.Exp, scale=-1 / 16.0)
                    act.activation(la, la, ACT.Exp, scale=1 / 16.0)
                    act.activation(cum, cum, ACT.Exp, scale=1 / 16.0)
                    act.activation(decay, lasts, ACT.Exp, scale=1 / 16.0).then_inc(g_act, 1)

                def ks_copy(h):
                    act.wait_ge(*gla(L, "kt", h))
                    act.wait_ge(z_ready, L + 1)
                    for half in range(2):
                        act.activation(ks_even[0:64, half * HALF:(half + 1) * HALF], ps[0:64, 6 + half, :], ACT.Copy)
                        o = act.activation(ks_odd[64:P, half * HALF:(half + 1) * HALF], ps[64:P, 6 + half, :], ACT.Copy)
                    o.then_inc(g_act, 1)

                def kv_copy(h):
                    act.wait_ge(*gla(L, "kv", h))
                    for b in range(4):
                        o = act.activation(kv[:, 4 * b:4 * b + 4, :], quads(2 + b), ACT.Copy)
                    o.then_inc(g_act, 1)

                def square(h):
                    act.wait_ge(*gla(L, "o", h))
                    if h >= 1:
                        act.wait_ge(*gla(L, "done", h - 1))
                    for half in range(2):
                        o = act.activation(sqg[:, half * HALF:(half + 1) * HALF], bank(6 + half), ACT.Square)
                    o.then_inc(g_act, 1)

                def inv_rms(to, b, width, done):
                    for half in range(2):
                        o = act.activation(to[:, half * HALF:(half + 1) * HALF], bank(b + half), ACT.Ln, scale=1.0 / width, bias=eps[:, 0:1])
                    hc.link(o)
                    act.activation(to, to, ACT.Exp, scale=-0.5).then_inc(done, 1)

                def rms(h):
                    act.wait_ge(*gla(L, "ms", h))
                    inv_rms(sqg, 4, P, g_act)

                for e in (("lr", 0), ("gq", 0), ("gk", 0)):
                    evac(*e)
                gate(0)
                evac("gv", 0)
                exps(0)
                evac("gg", 0)
                under = ((("gv", 1), ("gg", 1), ("gq", 1)), (("gk", 1), ("gv", 2), ("gg", 2)), (("gv", 3), ("gg", 3), ("cq", 0)), (("cq", 1), ("cq", 2), ("ckv", 0)))
                for h in range(4):
                    ks_copy(h)
                    evac(*under[h][0])
                    kv_copy(h)
                    if h < 3:
                        gate(h + 1)
                    evac(*under[h][1])
                    if h < 3:
                        exps(h + 1)
                    square(h)
                    evac(*under[h][2])
                    rms(h)
                evac("ckv", 1)
                act.wait_ge(l_ms, L * 2 + 1)
                inv_rms(r_q, 2, 384, l_r)
                evac("ga", 0)
                act.wait_ge(l_ms, L * 2 + 2)
                inv_rms(r_kv, 6, 256, l_r)
                for i in range(1, 4):
                    evac("ga", i)
                assert hc.n == PER, hc.n

                def fill(f):
                    kind, h, j = FILLS[f]
                    if kind != "p" or j in (2, 3):
                        return
                    act.wait_ge(f_ready, L * NF + f + 1)
                    at = (0, 0, None, None, 2, 2, 3, 3)[j]
                    act.activation(HT[:, 4 * (h % 2) + at, (j % 2) * HALF:(j % 2 + 1) * HALF], bank(f % 2), ACT.Copy).then_inc(f_evac[f % 2], 1)
                for f in range(8):
                    fill(f)
                f = 8
                for g in range(STEPS):
                    if g < 4 * NT:
                        act.wait_ge(a_neg, L * 4 * NT + g + 1)
                        if g >= 2:
                            act.wait_ge(a_t[1], L * 4 * NT + g - 1)
                        act.activation(xn[:, g % 2, :], psf[:, (2 + 2 * (g % 2)) * HALF:(4 + 2 * (g % 2)) * HALF], ACT.Exp, scale=MLA_SCALE,
                                       bias=sm[:, g % 2, 1:2], accum_out=sm[:, g % 2, 2:3]).then_inc(a_e, 1)
                    if g < 3 * NT:
                        fill(f)
                        f += 1
                    if g >= 5 and (g - 2) % 4 == 3:
                        f += 1
                    if 1 <= g <= 4 * NT:
                        q = g - 1
                        G = q // 4
                        act.wait_ge(a_t[1], L * 4 * NT + q + 1)
                        if G >= 2 and q % 4 == 0:
                            act.wait_ge(f_ready, L * NF + FI[("v", G - 2, 0)] + 1)
                        act.activation(PT[G % 2][:, 4:8, (q % 4) * P:(q % 4 + 1) * P], quads(7), ACT.Copy).then_inc(a_tev[1], 1)
                for b in range(4):
                    act.wait_ge(p_tp, L * 4 + b + 1)
                    act.activation(pT[:, b // 2, (b % 2) * HALF:(b % 2 + 1) * HALF], bank(2 + b), ACT.Copy).then_inc(p_ev, 1)
                nt_act(act, L * 2 + 3, lambda t: act.wait_ge(wo_evac, L * 2 * NT + (3 * NT + t + 1)))
                for u in range(2 * NT):
                    act.wait_ge(pg_ready, L * 2 * NT + u + 1)
                    act.wait_ge(pg_evac, L * 2 * NT + u + 1)
                    act.activation(sgp[:, u % 2, :], bank(u % 2), ACT.Sigmoid).then_inc(pg_sg, 1)
            layers(act, layer)
            for t in range(NT):
                act.wait_ge(h_in, (LAYERS + 1) * NT - NT + t + 1)
                if t >= 2:
                    act.wait_ge(f_ss, t - 1)
                act.activation(xn[:, t % 2, :], H[:, t, :], ACT.Square, accum_out=ss[:, t:t + 1]).then_inc(f_ss, 1)

        @block.tensor
        def _(pe):
            pe.sem_inc(n_tp, 2)
            pe.sem_inc(m_xt, 2)
            pe.sem_inc(m_gu, 2)
            pe.sem_inc(m_dn, 2)
            pe.sem_inc(m_at, 2)
            pe.wait_ge(idready, 4)
            nt_pe(pe, 0)
            pe.wait_ge(n_ht, 2 + NT)
            for u in range(6):
                pe.wait_ge(b_w[u % 3], 16 * (u // 3 + 1))
                for half in range(2):
                    n = 2 * u + half
                    if n >= 2:
                        pe.wait_ge(b_evac[n % 2], n // 2)
                    accumulate(pe, bank(n % 2), [(WF[:, u % 3, k, :], HT[:, k, half * HALF:(half + 1) * HALF]) for k in range(KD)]).then_inc(b_ready, 1)
            pe.wait_ge(b_evac[0], 6)
            pe.wait_ge(b_evac[1], 6)

            def turn(n):
                pe.wait_ge(c_qn, n + 1)
                if n >= 2:
                    pe.wait_ge(c_tev, n - 1)
                for h in range(4):
                    tp = pe.transpose(bank(2 + n % 2, P, h * P), qn[:, n % 2, h * P:(h + 1) * P], ident[:, :])
                tp.then_inc(c_tp, 1)
            for n in range(3 * NT):
                blk, t = n // NT, n % NT
                if t == 0:
                    pe.wait_ge(c_w[blk % 2], 16 * (blk // 2 + 1))
                if n >= 2:
                    pe.wait_ge(c_evac, n - 1)
                accumulate(pe, bank(n % 2), [(HT[:, k, t * P:(t + 1) * P], WT[:, blk % 2, k, :]) for k in range(KD)]).then_inc(c_ready, 1)
                if 2 <= n < 2 * NT + 2:
                    turn(n - 2)
            pe.wait_ge(c_evac, 3 * NT)
            pe.wait_ge(c_tev, 2 * NT)
            pe.wait_ge(pool_d, 1)
            pe.wait_ge(pwb_in, 64)
            for c in range(2):
                for half in range(2):
                    pe.matmul(bank(2 * c + half), pwb[:, c, :], p_pad[:, c, PADP + half * HALF:PADP + (half + 1) * HALF], start=True, stop=True).then_inc(pl_ready, 1)
            pe.wait_ge(cv_dve, 1)
            for half in range(2):
                accumulate(pe, bank(4 + half), [(ones[:, :], y_cv[:, c, half * HALF:(half + 1) * HALF]) for c in range(2)]).then_inc(ln_mu, 1)
            for half in range(2):
                pe.wait_ge(ln_sq, half + 1)
                accumulate(pe, bank(6 + half), [(ones[:, :], sq_cv[:, c, half * HALF:(half + 1) * HALF]) for c in range(2)]).then_inc(ln_var, 1)
            pe.wait_ge(pl_evac, 4)
            pe.wait_ge(cpw_in, 16)
            for n in range(4):
                half, m = n // 2, n % 2
                pe.wait_ge(ln_ys, half + 1)
                accumulate(pe, bank(n), [(cpw[:, c, m * P:(m + 1) * P], y_cv[:, c, half * HALF:(half + 1) * HALF]) for c in range(2)]).then_inc(pw_ready, 1)

            pe.wait_ge(pw_evac, 4)
            with pe.Fori(0, HEADS) as h:
                pe.wait_ge(qz_ready, h + 1)
                g = 0

                def scores(b):
                    W = (b + 1) * P
                    for m in range(2):
                        if 2 * b + m >= 2:
                            pe.wait_ge(s_max, h * 2 * NT + 2 * b + m - 1)
                        for j in range((W + HALF - 1) // HALF):
                            w = min(HALF, W - j * HALF)
                            mm = pe.matmul(bank(2 * m + j, w), qz[:, m, b * P:(b + 1) * P],
                                           kT[:, ds(h, 1), j * HALF:j * HALF + w].rearrange("p a t -> p (a t)"), start=True, stop=True)
                        mm.then_inc(s_ready, 1)

                def weigh(b, g):
                    pe.wait_ge(a_ready, h * NT + b + 1)
                    for j in range(b // 4 + 1):
                        if g >= 2:
                            pe.wait_ge(at_evac, h * 12 + g - 1)
                        for k in range(4 * j, min(4 * j + 4, b + 1)):
                            tp = pe.transpose(bank(4 + j, P, (k % 4) * P), sS[:, b % 2, 0, k * P:(k + 1) * P], ident[:, :])
                        tp.then_inc(t_ready, 1)
                        g += 1
                    pe.wait_ge(at_evac, h * 12 + g)
                    if b >= 1:
                        pe.wait_ge(o_n, h * NT + b)
                    accumulate(pe, bank(6, P, (b % 4) * P), [(ATb[:, b % 2, k, :], V1[:, k, ds(h * P, P)]) for k in range(b + 1)]).then_inc(o_ready, 1)
                    return g

                def turn_out(b):
                    pe.wait_ge(o_n, h * NT + b + 1)
                    if b >= 1:
                        pe.wait_ge(ot_evac, h * NT + b)
                    pe.transpose(bank(7, P, (b % 4) * P), on[:, b % 2, :], ident[:, :]).then_inc(ot_ready, 1)
                for b in range(NT + 2):
                    if b < NT:
                        scores(b)
                    if 1 <= b <= NT:
                        g = weigh(b - 1, g)
                    if b >= 2:
                        turn_out(b - 2)
                pe.wait_ge(ot_evac, h * NT + NT)
            for n in range(2):
                pe.wait_ge(wo_w[n], 16)
                for t in range(NT):
                    u = n * NT + t
                    if u >= 2:
                        pe.wait_ge(wo_evac, u - 1)
                    accumulate(pe, bank(u % 2), [(MIX[:, k, t * P:(t + 1) * P], WT[:, n, k, :]) for k in range(KD)]).then_inc(wo_ready, 1)
            nt_pe(pe, 1)
            pe.wait_ge(n_ht, 2 + 2 * NT)
            pe.wait_ge(rw_in, 64)
            for half in range(2):
                accumulate(pe, bank(6 + half), [(WF[:, 0, k, :], HT[:, k, half * HALF:(half + 1) * HALF]) for k in range(KD)]).then_inc(rt_ready, 1)
            pe.wait_ge(rt_cp, 2)
            for t in range(NT):
                tp = pe.transpose(bank(2 + t // 4, P, (t % 4) * P), lgT[:, t * P:(t + 1) * P], ident[:, :])
            tp.then_inc(rt_tp, 1)
            pe.wait_ge(rm_ready, 1)
            MMf = MM.rearrange("p t e -> p (t e)")
            pe.wait_ge(iotas, 2)
            pe.matmul(bank(6, P), tri, MMf, start=True, stop=True)
            pe.matmul(bank(7, P), ones[:, :], MMf, start=True, stop=True).then_inc(rp_ready, 1)

            def turn_rows(t, i, p):
                pe.wait_ge(m_hg[p], i * 16 + 16)
                pe.wait_ge(m_ht, t + 1)
                for c in range(KD):
                    tp = pe.transpose(bank(c // 4, P, (c % 4) * P), hg[:, p, c * P:(c + 1) * P], ident[:, :])
                tp.then_inc(m_xt, 1)

            def expert_pe(t, i, p, after):
                pe.wait_ge(m_ht, t + 2)
                pe.wait_ge(m_wgu[p], i * 32 + 32)
                pe.wait_ge(m_act, t + 1)
                accumulate(pe, bank(2 + p), [(hgT[:, p, k, :], WT[:, p, k, :]) for k in range(KD)]).then_inc(m_gu, 1)
                after()
                pe.wait_ge(m_act, t + 3)
                pe.wait_ge(m_aT, t + 1)
                for k in range(2):
                    tp = pe.transpose(bank(4, P, k * P), actb[:, p, k * P:(k + 1) * P], ident[:, :])
                tp.then_inc(m_at, 1)
                pe.wait_ge(m_aT, t + 2)
                pe.wait_ge(m_wd[p], i * 16 + 16)
                pe.wait_ge(m_y, t + 1)
                for n in range(2):
                    mm = accumulate(pe, bank(6 + n), [(actT[:, p, k, :], wd[:, p, k, n * HALF:(n + 1) * HALF]) for k in range(2)])
                mm.then_inc(m_dn, 1)
            turn_rows(0, 0, 0)
            with pe.Fori(0, MTILES // 2) as i:
                expert_pe(i * 2, i, 0, lambda: turn_rows(i * 2 + 1, i, 1))
                expert_pe(i * 2 + 1, i, 1, lambda: turn_rows(i * 2 + 2, i + 1, 0))
            expert_pe(MTILES - 1, MTILES // 2, 0, lambda: None)

            def layer(L):
                nt_pe(pe, L * 2 + 2)
                pe.wait_ge(n_ht, L * 2 * NT + 3 * NT + 2)

                def unit(kind, i):
                    u = UI[(kind, i)]
                    s = u % 2
                    pe.wait_ge(u_w[s], L * 16 * W_LAYER[s] + 16 * W_SOFAR[u])
                    for half in range(2):
                        pe.wait_ge(u_evac[half], L * NU + u + 1)
                        if kind == "gv":
                            for t in range(4):
                                mm = accumulate(pe, bank(half, P, t * P), [(HT[:, k, (4 * half + t) * P:(4 * half + t + 1) * P], WF[:, s, k, :]) for k in range(KD)])
                        else:
                            m = UNITS[u][3]
                            mm = accumulate(pe, ps[0:m, half, :], [(WF[:, s, k, 0:m], HT[:, k, half * HALF:(half + 1) * HALF]) for k in range(KD)])
                        mm.then_inc(u_ready, 1)

                def gates(h):
                    if h == 0:
                        pe.wait_ge(wg_in, L * 32 + 32)
                        for half in range(2):
                            pe.wait_ge(u_evac[half], unit_evac(L, 0, half))
                    else:
                        pe.wait_ge(*gla(L, "kvc", h - 1))
                    for half in range(2):
                        mm = pe.matmul(bank(2 + half), wgs[:, h, :], lrz[:, half * HALF:(half + 1) * HALF], start=True, stop=True)
                    mm.then_inc(g_pe, 1)

                def inner(h):
                    pe.wait_ge(*gla(L, "k", h))
                    if h >= 1:
                        pe.wait_ge(*gla(L, "r", h - 1))
                    for d, kk in enumerate((kf, kb)):
                        for t in range(NT):
                            mm = pe.matmul(bank(2 + 2 * d + t // 4, P, (t % 4) * P), kk[:, t * P:(t + 1) * P], q_in[:, t * P:(t + 1) * P], start=True, stop=True)
                    mm.then_inc(g_pe, 1)
                    if h >= 1:
                        pe.wait_ge(*gla(L, "done", h - 1))
                    for t in range(NT):
                        tp = pe.transpose(bank(6 + t // 4, P, (t % 4) * P), la[:, t * P:(t + 1) * P], ident[:, :])
                    tp.then_inc(g_pe, 1)

                def states(h):
                    pe.wait_ge(*gla(L, "ks", h))
                    pe.wait_ge(*gla(L, "am", h))
                    for half in range(2):
                        pe.wait_ge(u_evac[half], unit_evac(L, UI[("gv", h)], half))
                    for c in range(NCH):
                        t = c // 2
                        mm = pe.matmul(bank(2 + c // 4, P, (c % 4) * P), (ks_even, ks_odd)[c % 2][:, t * P:(t + 1) * P], gv[h % 2][:, t * P:(t + 1) * P], start=True, stop=True)
                    mm.then_inc(g_pe, 1)

                def outputs(h):
                    pe.wait_ge(*gla(L, "st", h))
                    for t in range(NT):
                        ts = slice(t * P, (t + 1) * P)
                        mm = accumulate(pe, bank(6 + t // 4, P, (t % 4) * P), [(gv[h % 2][:, ts], Af[:, ts]), (gv[h % 2][:, ts], Ab[:, ts]),
                                                                             (st[:, 2 * t, :], q_even[:, ts]), (st[:, 2 * t + 1, :], q_odd[:, ts])])
                    mm.then_inc(g_pe, 1)

                def squares(h):
                    pe.wait_ge(*gla(L, "sq", h))
                    for half in range(2):
                        mm = pe.matmul(bank(4 + half), ones[:, :], sqg[:, half * HALF:(half + 1) * HALF], start=True, stop=True)
                    mm.then_inc(g_pe, 1)

                unit("lr", 0)
                unit("gq", 0)
                unit("gk", 0)
                gates(0)
                unit("gv", 0)
                unit("gg", 0)
                under = ((("gv", 1), ("gg", 1), ("gq", 1)), (("gk", 1), ("gv", 2), ("gg", 2)), (("gv", 3), ("gg", 3), ("cq", 0)), (("cq", 1), ("cq", 2), ("ckv", 0)))
                for h in range(4):
                    inner(h)
                    unit(*under[h][0])
                    states(h)
                    if h < 3:
                        gates(h + 1)
                    unit(*under[h][1])
                    outputs(h)
                    unit(*under[h][2])
                    squares(h)
                unit("ckv", 1)
                for half in range(2):
                    accumulate(pe, bank(2 + half), [(ones[:, :], q[:, half * HALF:(half + 1) * HALF]) for q in sq_q])
                pe.drain().then_inc(l_ms, 1)
                unit("kr", 0)
                unit("ga", 0)
                pe.wait_ge(*gla(L, "done", 3))
                for half in range(2):
                    accumulate(pe, bank(6 + half), [(ones[:, :], q[:, half * HALF:(half + 1) * HALF]) for q in sq_kv])
                pe.drain().then_inc(l_ms, 1)
                for i in range(1, 4):
                    unit("ga", i)
                for half in range(2):
                    pe.wait_ge(u_evac[half], unit_evac(L, NU - 1, half))

                def fill(f):
                    kind, h, j = FILLS[f]
                    pe.wait_ge(f_evac[f % 2], L * (NF // 2) + f // 2 + 1)
                    o = bank(f % 2)
                    if kind == "p":
                        s, hs = h % 2, slice((j % 2) * HALF, (j % 2 + 1) * HALF)
                        if j == 0:
                            pe.wait_ge(uw[s], L * 128 + 64 * (h // 2) + 64)
                        if j < 4:
                            c = (j // 2) * P
                            mm = accumulate(pe, o, [(uq[s][:, k, c:c + P], c_q[k][:, hs]) for k in range(3)])
                        elif j < 6:
                            mm = accumulate(pe, o, [(ukv[s][:, k, 0:P], c_kv[k][:, hs]) for k in range(2)])
                        else:
                            for t in range(4):
                                ts = slice((4 * (j % 2) + t) * P, (4 * (j % 2) + t + 1) * P)
                                mm = accumulate(pe, bank(f % 2, P, t * P), [(c_kv[k][:, ts], ukv[s][:, k, P:2 * P]) for k in range(2)])
                    else:
                        G = h
                        hd = G // 2
                        for i in range(2):
                            pe.wait_ge(a_tev[i], L * 4 * NT + 4 * G + 4)
                            fv = FI[("p", hd, 6 + i)]
                            if fv % 2 != f % 2:
                                pe.wait_ge(f_evac[fv % 2], fill_evac(L, fv))
                        mm = accumulate(pe, o, [(HT[:, 4 * (hd % 2) + 3, k * P:(k + 1) * P], PT[G % 2][:, k, :]) for k in range(KD)])
                    mm.then_inc(f_ready, 1)
                pe.wait_ge(l_c, L * 2 + 2)
                pe.wait_ge(hz_ready, L + 1)
                for f in range(8):
                    fill(f)
                f = 8
                for g in range(STEPS):
                    if g < 4 * NT:
                        h, b, s = g // NT, g % NT, 4 * (g // NT % 2)
                        if b == 0:
                            for j in (4, 5):
                                fv = FI[("p", h, j)]
                                pe.wait_ge(f_evac[fv % 2], fill_evac(L, fv))
                        if g >= 2:
                            pe.wait_ge(a_e, L * 4 * NT + g - 1)
                        for half in range(2):
                            hs = slice(half * HALF, (half + 1) * HALF)
                            mm = accumulate(pe, bank(2 + 2 * (g % 2) + half), [(HT[:, s, b * P:(b + 1) * P], HT[:, s + 2, hs]),
                                                                               (HT[:, s + 1, b * P:(b + 1) * P], kr[:, hs])])
                        mm.then_inc(a_s, 1)
                    if g < 3 * NT:
                        fill(f)
                        f += 1
                    if g >= 5 and (g - 2) % 4 == 3:
                        fill(f)
                        f += 1
                    if 1 <= g <= 4 * NT:
                        q = g - 1
                        pe.wait_ge(a_p, L * 4 * NT + q + 1)
                        for half in range(2):
                            if q >= 1:
                                pe.wait_ge(a_tev[half], L * 4 * NT + q)
                            for k in range(4):
                                tp = pe.transpose(bank(6 + half, P, k * P), xn[:, q % 2, (4 * half + k) * P:(4 * half + k + 1) * P], ident[:, :])
                            tp.then_inc(a_t[half], 1)
                assert f == NF
                for i in range(2):
                    pe.wait_ge(f_evac[i], L * (NF // 2) + NF // 2 + 1)
                for n in range(2):
                    pe.wait_ge(wo_w[n], L * 32 + 32)
                    for t in range(NT):
                        u = n * NT + t
                        pe.wait_ge(wo_evac, L * 2 * NT + (2 * NT + u - 1))
                        accumulate(pe, bank(u % 2), [(MIX[:, k, t * P:(t + 1) * P], WT[:, n, k, :]) for k in range(KD)]).then_inc(wo_ready, 1)
                    if n == 0:
                        pe.wait_ge(p_in, L * 32 + 32)
                        for b in range(4):
                            for t in range(4):
                                tp = pe.transpose(bank(2 + b, P, t * P), p_tok[:, 4 * (b % 2) + t, (b // 2) * P:(b // 2 + 1) * P], ident[:, :])
                            tp.then_inc(p_tp, 1)
                pe.wait_ge(p_ev, L * 4 + 4)
                pe.wait_ge(wo_evac, L * 2 * NT + 4 * NT)
                settle(pe, settled)
                nt_pe(pe, L * 2 + 3)
                pe.wait_ge(n_ht, L * 2 * NT + 4 * NT + 2)
                for n in range(2):
                    pe.wait_ge(wo_w[n], L * 32 + 48)
                    for t in range(NT):
                        u = n * NT + t
                        pe.wait_ge(pg_evac, L * 2 * NT + u + 1)
                        accumulate(pe, bank(u % 2), [(HT[:, k, t * P:(t + 1) * P], WT[:, n, k, :]) for k in range(KD)])
                        accumulate(pe, bank(2 + u % 2), [(pT[:, c, t * P:(t + 1) * P], wpp[:, c, n * HALF:(n + 1) * HALF]) for c in range(2)]).then_inc(pg_ready, 1)
            layers(pe, layer)

        @block.vector
        def _(dve):
            chain = Chain(dve, dve_chain)
            dve.sem_inc(n_ht, 2)
            dve.sem_inc(m_ht, 1)
            dve.sem_inc(m_act, 2)
            dve.wait_ge(const_in, 16 * 19)
            chain.link(dve.tensor_scalar(vec1[:, V_QG:V_QG + 1], vec1[:, V_QG:V_QG + 1], DH ** -0.5, None, ALU.mult))
            chain.link(dve.tensor_scalar(vec1[:, V_SG:V_SG + 1], vec1[:, V_SG:V_SG + 1], 1.0 - LAM_INIT, None, ALU.mult))
            for i in range(2):
                chain.link(dve.tensor_tensor(lamt[:, 2 * i, :], lamt[:, 2 * i, :], lamt[:, 2 * i + 1, :], ALU.mult))
                chain.link(dve.tensor_reduce(lam4[:, i:i + 1], lamt[:, 2 * i, :], AX.X, ALU.add))
            dve.sem_inc(lam_e, 1)
            nt_dve(dve, 0, vec1[:, V_AG:V_AG + 8])
            dve.wait_ge(b_ready, 1)
            dve.memset(p_pad[:, :, 0:PADP], 0.0).then_inc(padded, 1)
            dve.memset(u_pad[:, :, 0:PADC], 0.0).then_inc(padded, 1)
            for c in range(2):
                for half in range(2):
                    n = 6 * c + 2 + half
                    dve.wait_ge(b_ready, n + 1)
                    dve.wait_ge(b_evac[n % 2], 3 * c + 1)
                    dve.tensor_tensor(u_pad[:, c, PADC + half * HALF:PADC + (half + 1) * HALF], bank(n % 2),
                                      sig_g[:, c, half * HALF:(half + 1) * HALF], ALU.mult).then_inc(b_evac[n % 2], 1)
            dve.wait_ge(lam_e, 2)
            chain.link(dve.tensor_tensor(lam4[:, 4:5], lam4[:, 2:3], lam4[:, 3:4], ALU.subtract))
            chain.link(dve.tensor_scalar(lam4[:, 4:5], lam4[:, 4:5], LAM_INIT, None, ALU.add))
            dve.wait_ge(padded, 3)
            tap = 0
            for n in range(2 * NT + 2):
                if n < 2 * NT:
                    dve.wait_ge(c_evac, n + 1)
                    if n >= 2:
                        dve.wait_ge(c_rs, n - 1)
                    dve.tensor_reduce(qsum[:, n % 2, :], xn[:, n % 2, 0:HALF].rearrange("p (g d) -> p g d", d=DH), AX.X, ALU.add).then_inc(c_red, 1)
                    for _ in range(2):
                        if tap < TAPS:
                            for c in range(2):
                                w = vec1[:, V_CW + TAPS * c + tap:V_CW + TAPS * c + tap + 1]
                                uu = u_pad[:, c, tap:tap + S]
                                if tap == 0:
                                    o = dve.tensor_scalar(y_cv[:, c, :], uu, w, vec1[:, V_CB + c:V_CB + c + 1], ALU.mult, ALU.add)
                                else:
                                    o = dve.scalar_tensor_tensor(out=y_cv[:, c, :], in0=uu, scalar=w, in1=y_cv[:, c, :], op0=ALU.mult, op1=ALU.add)
                            chain.link(o)
                            tap += 1
                if 1 <= n <= 2 * NT:
                    q = n - 1
                    dve.wait_ge(c_rs, q + 1)
                    if q >= 2:
                        dve.wait_ge(c_tp, q - 1)
                    dve.tensor_tensor(qn[:, q % 2, :].rearrange("p (g d) -> p g d", d=DH), qtok[:, q % 2, :].rearrange("p (g d) -> p g d", d=DH),
                                      qrs[:, q % 2, :].unsqueeze(2).to_broadcast([P, 8, DH]), ALU.mult).then_inc(c_qn, 1)
                if n >= 2:
                    q = n - 2
                    dve.wait_ge(c_tp, q + 1)
                    to, gc = (qT, V_QG) if q < NT else (kT, V_KG)
                    dve.tensor_scalar(to[:, :, (q % NT) * P:(q % NT + 1) * P], quads(2 + q % 2), vec1[:, gc:gc + 1], None, ALU.mult).then_inc(c_tev, 1)
            dve.drain().then_inc(cv_dve, 1)
            for half in range(2):
                hs = slice(half * HALF, (half + 1) * HALF)
                dve.wait_ge(ln_mu, half + 1)
                for c in range(2):
                    xc = dve.scalar_tensor_tensor(out=y_cv[:, c, hs], in0=bank(4 + half), scalar=-1.0 / 256, in1=y_cv[:, c, hs], op0=ALU.mult, op1=ALU.add)
                xc.then_inc(ln_xc, 1)
            for half in range(2):
                hs = slice(half * HALF, (half + 1) * HALF)
                dve.wait_ge(ln_sd, half + 1)
                chain.link(dve.reciprocal(r_cv[:, hs], r_cv[:, hs]))
                for c in range(2):
                    yn = dve.tensor_tensor(y_cv[:, c, hs], y_cv[:, c, hs], r_cv[:, hs], ALU.mult)
                yn.then_inc(ln_n, 1)

            dve.wait_ge(c_ready, 3 * NT)
            PER = 1 + 4 * NT
            base = chain.n
            with dve.Fori(0, HEADS) as h:
                hc = Chain(dve, dve_chain, h * PER + base)
                hc.link(dve.tensor_scalar(BH, shared[:, 0:S], kc[:, ds(h + K_SLOPE, 1)], None, ALU.mult))
                for b in range(NT + 2):
                    if b < NT:
                        W = (b + 1) * P
                        for m in range(2):
                            u = 2 * b + m
                            dve.wait_ge(s_ready, h * 2 * NT + u + 1)
                            if b >= 2:
                                dve.wait_ge(t_ready, h * 12 + sum(q // 4 + 1 for q in range(b - 1)))
                            settle(dve, settled)
                            dve.tensor_tensor_reduce(sS[:, b % 2, m, 0:W], psf[:, 2 * m * HALF:2 * m * HALF + W], BH[:, S - P - b * P:S],
                                                     1.0, NEG, ALU.add, ALU.max, sm[:, b % 2, m:m + 1]).then_inc(s_max, 1)
                            dve.wait_ge(s_max, h * 2 * NT + u + 1)
                            dve.tensor_scalar(sm[:, b % 2, 2 + m:3 + m], sm[:, b % 2, m:m + 1], -1.0, None, ALU.mult).then_inc(s_neg, 1)
                    if 1 <= b <= NT:
                        q = b - 1
                        W = (q + 1) * P
                        dve.wait_ge(e_ready, h * 2 * NT + 2 * q + 2)
                        hc.link(dve.reciprocal(sm[:, q % 2, 6:8], sm[:, q % 2, 4:6]))
                        hc.link(dve.tensor_scalar(sm[:, q % 2, 7:8], sm[:, q % 2, 7:8], lam4[:, 4:5], None, ALU.mult))
                        hc.link(dve.tensor_scalar(sS[:, q % 2, 1, 0:W], sS[:, q % 2, 1, 0:W], sm[:, q % 2, 7:8], None, ALU.mult))
                        hc.link(dve.scalar_tensor_tensor(out=sS[:, q % 2, 0, 0:W], in0=sS[:, q % 2, 0, 0:W], scalar=sm[:, q % 2, 6:7],
                                                         in1=sS[:, q % 2, 1, 0:W], op0=ALU.mult, op1=ALU.subtract))
                        dve.sem_inc(a_ready, 1)
                    if b >= 2:
                        q = b - 2
                        dve.wait_ge(ot_ready, h * NT + q + 1)
                        dve.tensor_scalar(MIX[:, ds(h + 4, 1), q * P:(q + 1) * P].rearrange("p a t -> p (a t)"), bank(7, P, (q % 4) * P),
                                          vec1[:, V_SG:V_SG + 1], None, ALU.mult).then_inc(ot_evac, 1)
                assert hc.n == PER
            chain.n = base + HEADS * PER

            for u in range(2 * NT):
                n, t = u // NT, u % NT
                dve.wait_ge(wo_ready, u + 1)
                dve.wait_ge(x_in[t], 32)
                hh = H[:, t, n * HALF:(n + 1) * HALF]
                dve.tensor_tensor(hh, bank(u % 2), hh, ALU.add).then_inc(wo_evac, 1)
            nt_dve(dve, 1, vec1[:, V_FG:V_FG + 8])
            dve.wait_ge(rt_tp, 1)
            dve.wait_ge(rw_in, 64)
            for j in range(2):
                chain.link(dve.tensor_tensor(lg[:, 4 * j:4 * j + 4, :], quads(2 + j)[:, :, 0:20], rb.unsqueeze(1).to_broadcast([P, 4, 20]), ALU.add))

            dve.wait_ge(iotas, 2)

            def col(a, n=4):
                return a.unsqueeze(2).to_broadcast([P, NT, n])

            def tt(o, a, b, op):
                chain.link(dve.tensor_tensor(o, a, b, op))

            def first_max(o, values, eq):
                chain.link(dve.tensor_reduce(m1, values, AX.X, ALU.max))
                tt(eq, values, col(m1), ALU.is_equal)
                tt(eq, eq, first4.unsqueeze(1).to_broadcast([P, NT, 4]), ALU.mult)
                chain.link(dve.tensor_reduce(m1, eq, AX.X, ALU.max))
                tt(o, eq, col(m1), ALU.is_equal)
            chain.link(dve.tensor_reduce(g_max, lg[:, :, 0:4], AX.X, ALU.max))
            tt(ge, lg[:, :, 0:4], col(g_max), ALU.subtract)
            dve.sem_inc(rx, 1)
            dve.wait_ge(rx, 2)
            chain.link(dve.tensor_reduce(g_sum, ge, AX.X, ALU.add))
            chain.link(dve.reciprocal(g_p, g_sum))
            first_max(oh, ge, geq)
            ev = lg[:, :, 4:20].rearrange("p t (g e) -> p t g e", g=GROUPS)
            tt(lsel, ev, oh.unsqueeze(3).to_broadcast([P, NT, 4, 4]), ALU.mult)
            chain.link(dve.tensor_reduce(le, lsel.rearrange("p t g e -> p t e g"), AX.X, ALU.add))
            chain.link(dve.tensor_reduce(g_max, le, AX.X, ALU.max))
            tt(le, le, col(g_max), ALU.subtract)
            dve.sem_inc(rx, 1)
            dve.wait_ge(rx, 4)
            first_max(oh1, le, leq)
            chain.link(dve.tensor_reduce(v1, le, AX.X, ALU.max))
            chain.link(dve.scalar_tensor_tensor(out=pe2, in0=oh1, scalar=-2.0, in1=le, op0=ALU.mult, op1=ALU.add))
            first_max(oh2, pe2, leq)
            chain.link(dve.tensor_reduce(v2, pe2, AX.X, ALU.max))
            tt(den, v1, v2, ALU.add)
            chain.link(dve.reciprocal(den, den))
            tt(den, den, g_p, ALU.mult)
            tt(w1, v1, den, ALU.mult)
            tt(w2, v2, den, ALU.mult)
            for o, e in ((S1, oh1), (S2, oh2)):
                tt(o.rearrange("p t (g e) -> p t g e", g=GROUPS), oh.unsqueeze(3).to_broadcast([P, NT, 4, 4]),
                   e.unsqueeze(2).to_broadcast([P, NT, 4, 4]), ALU.mult)
            tt(MM, S1, S2, ALU.add)
            dve.sem_inc(rm_ready, 1)
            dve.wait_ge(rp_ready, 1)
            within = bank(6, P).rearrange("p (t e) -> p t e", t=NT)
            intile = bank(7, P).rearrange("p (t e) -> p t e", t=NT)
            chain.link(dve.memset(toff[:, 0, :], 0.0))
            for t in range(1, NT):
                tt(toff[:, t, :], toff[:, t - 1, :], intile[:, t - 1, :], ALU.add)
            tt(cnt, toff[:, NT - 1, :], intile[:, NT - 1, :], ALU.add)
            tt(posn, toff, within, ALU.add)
            chain.link(dve.tensor_scalar(tiles_i, cnt, float(P - 1), None, ALU.add))
            chain.link(dve.tensor_single_scalar(tiles_i, tiles_i, 7, ALU.arith_shift_right))
            chain.link(dve.tensor_copy(tiles_f, tiles_i))
            chain.link(dve.tensor_tensor_scan(tend, one16, tiles_f, 0.0, ALU.mult, ALU.add))
            tt(tbase, tend, tiles_f, ALU.subtract)
            chain.link(dve.scalar_tensor_tensor(out=posn, in0=tbase.unsqueeze(1).to_broadcast([P, NT, 16]), scalar=float(P), in1=posn, op0=ALU.mult, op1=ALU.add))
            for k, (o, s, w) in enumerate(((pos1, S1, w1), (pos2, S2, w2))):
                tt(tmpe, s, posn, ALU.mult)
                chain.link(dve.tensor_reduce(o, tmpe, AX.X, ALU.add))
                chain.link(dve.tensor_copy(sidx[:, :, k:k + 1], o.unsqueeze(2)))
                chain.link(dve.tensor_copy(rows_f[:, :, k, 2:3], w.unsqueeze(2)))
            dve.sem_inc(rx_done, 1)
            tt(cmpt, iot.unsqueeze(2).to_broadcast([P, MTILES + 1, 16]), tend.unsqueeze(1).to_broadcast([P, MTILES + 1, 16]), ALU.is_ge)
            chain.link(dve.tensor_reduce(et_f, cmpt, AX.X, ALU.add))
            chain.link(dve.tensor_scalar(et_f, et_f, float(EXPERTS - 1), None, ALU.min))
            chain.link(dve.tensor_copy(et_i, et_f))
            dve.sem_inc(experts_set, 1)
            C1 = 6.28125
            C2 = float(np.float32(np.round((2 * np.pi - C1) * 2.0 ** 20) * 2.0 ** -20))
            C3 = float(2 * np.pi - C1 - C2)
            MAGIC = 1.5 * 2.0 ** 23
            dve.wait_ge(pos_in, 16)
            chain.link(dve.tensor_copy(ang, pos_i))
            chain.link(dve.tensor_scalar(ang, ang, kc[:, K_INV:K_INV + 1], None, ALU.mult))
            chain.link(dve.tensor_scalar(turns, ang, 1.0 / (2 * np.pi), kc[:, K_OFF:K_OFF + 1], ALU.mult, ALU.add))
            chain.link(dve.tensor_scalar(turns, turns, MAGIC, None, ALU.add))
            chain.link(dve.tensor_scalar(turns, turns, -MAGIC, None, ALU.add))
            for c in (C1, C2, C3):
                chain.link(dve.scalar_tensor_tensor(out=ang, in0=turns, scalar=-c, in1=ang, op0=ALU.mult, op1=ALU.add))
            chain.link(dve.tensor_scalar(ang, ang, kc[:, K_RAD:K_RAD + 1], 3.1415925, ALU.add, ALU.min))
            dve.tensor_scalar(ang, ang, -3.1415925, None, ALU.max).then_inc(rope_set, 1)
            dve.wait_ge(rope_set, 2)
            dve.tensor_scalar(rope[:, :], ang, kc[:, K_SIGN:K_SIGN + 1], None, ALU.mult).then_inc(rope_set, 1)
            dve.wait_ge(rope_set, 3)

            def rows_to_ht(t, p):
                dve.wait_ge(m_xt, t + 3)
                dve.wait_ge(m_gu, t + 1)
                for c in range(2):
                    g = vec1[:, V_FG + 4 * c:V_FG + 4 * c + 4].unsqueeze(2).to_broadcast([P, 4, P])
                    o = dve.tensor_tensor(hgT[:, p, 4 * c:4 * c + 4, :], quads(c), g, ALU.mult)
                o.then_inc(m_ht, 1)

            def expert_dve(t, p):
                dve.wait_ge(m_sg, t + 1)
                dve.wait_ge(m_at, t + 1)
                dve.scalar_tensor_tensor(out=actb[:, p, :], in0=sgb[:, p, :], scalar=tab_f[:, p, 2:3], in1=bank(2 + p, DE, DE),
                                         op0=ALU.mult, op1=ALU.mult).then_inc(m_act, 1)
            rows_to_ht(0, 0)
            with dve.Fori(0, MTILES // 2) as i:
                expert_dve(i * 2, 0)
                rows_to_ht(i * 2 + 1, 1)
                expert_dve(i * 2 + 1, 1)
                rows_to_ht(i * 2 + 2, 0)
            expert_dve(MTILES - 1, 0)
            dve.wait_ge(y_in[0], 16)
            dve.wait_ge(y_in[1], 16)
            for t in range(NT):
                dve.tensor_tensor(HT[:, t, :], HT[:, t, :], MIX[:, t, :], ALU.add).then_inc(comb, 1)
            for t in range(NT):
                dve.wait_ge(comb, t + 1)
                dve.tensor_tensor(H[:, t, :], H[:, t, :], HT[:, t, :], ALU.add).then_inc(h_in, 1)

            dve.sem_inc(pg_evac, 2)
            dve.wait_ge(masks_set, 1)
            base = chain.n
            PER = 159

            def layer(L):
                hc = Chain(dve, dve_chain, L * (PER or 0) + base)
                dve.wait_ge(vl_ready, L + 1)
                settle(dve, settled)
                nt_dve(dve, L * 2 + 2, vl[:, L_MIX:L_MIX + 8])
                dirs = ((slice(0, 64), 1), (slice(64, P), -1))

                def chunks(a):
                    return a.rearrange("p (c i) -> p c i", c=NCH)

                def gate(h):
                    dve.wait_ge(*gla(L, "t", h))
                    hc.link(dve.scalar_tensor_tensor(out=la, in0=la, scalar=0.0, in1=gt, op0=ALU.min, op1=ALU.subtract))
                    hc.link(dve.tensor_tensor_scan(cum[0:64, :], reset[0:64, :], la[0:64, :], 0.0, ALU.mult, ALU.add))
                    hc.link(dve.tensor_tensor_scan(cum[64:P, ::-1], reset[64:P, :], la[64:P, ::-1], 0.0, ALU.mult, ALU.add))
                    cc = chunks(cum)
                    for r, ref, last in ((slice(0, 64), CH // 2 - 1, CH - 1), (slice(64, P), CH // 2, 0)):
                        dve.tensor_copy(refs[r, :].unsqueeze(2), cc[r, :, ref:ref + 1])
                        o = dve.tensor_copy(lasts[r, :].unsqueeze(2), cc[r, :, last:last + 1])
                    hc.link(o)
                    dve.tensor_tensor(chunks(gt), cc, refs.unsqueeze(2).to_broadcast([P, NCH, CH]), ALU.subtract)
                    dve.tensor_tensor(chunks(la), lasts.unsqueeze(2).to_broadcast([P, NCH, CH]), cc, ALU.subtract).then_inc(g_dve, 1)

                def products(h):
                    dve.wait_ge(*gla(L, "e", h))
                    dve.wait_ge(z_ready, L + 1)
                    for half in range(2):
                        dve.wait_ge(u_evac[half], unit_evac(L, UI[("gk", h // 2)], half))
                    q, k = q_dup[h % 2], k_dup[h % 2]
                    dve.tensor_tensor(q_in, q_in, q, ALU.mult)
                    dve.tensor_tensor(kf[0:64, :], gt[0:64, :], k[0:64, :], ALU.mult)
                    dve.tensor_tensor(kb[64:P, :], gt[64:P, :], k[64:P, :], ALU.mult)
                    dve.tensor_tensor(la, la, k, ALU.mult).then_inc(g_dve, 1)
                    if h >= 1:
                        dve.wait_ge(*gla(L, "o", h - 1))
                    for par, to in ((0, q_even), (1, q_odd)):
                        v = lambda a: a.rearrange("p (t c i) -> p t c i", t=NT, c=2)[:, :, par, :]
                        o = dve.tensor_tensor(v(to), v(cum), v(q), ALU.mult)
                    o.then_inc(g_dve, 1)

                def causal(h):
                    dve.wait_ge(*gla(L, "a", h))
                    settle(dve, settled)
                    for d, (to, mask) in enumerate(((Af, mask_f), (Ab, mask_b))):
                        for b in range(2):
                            o = dve.copy_predicated(to[:, b * HALF:(b + 1) * HALF].rearrange("p (t i) -> p t i", t=4),
                                                    mask.bitcast(U32).unsqueeze(1).to_broadcast([P, 4, P]), quads(2 + 2 * d + b))
                    o.then_inc(g_dve, 1)

                def scan_states(h):
                    dve.wait_ge(*gla(L, "kvc", h))
                    if h == 0:
                        dve.memset(st[0:64, 0, :], 0.0)
                        hc.link(dve.memset(st[64:P, NCH - 1, :], 0.0))
                    for c in range(1, NCH):
                        b = NCH - 1 - c
                        dve.scalar_tensor_tensor(out=st[0:64, c, :], in0=st[0:64, c - 1, :], scalar=decay[0:64, c - 1:c], in1=kv[0:64, c - 1, :], op0=ALU.mult, op1=ALU.add)
                        o = dve.scalar_tensor_tensor(out=st[64:P, b, :], in0=st[64:P, b + 1, :], scalar=decay[64:P, b + 1:b + 2], in1=kv[64:P, b + 1, :], op0=ALU.mult, op1=ALU.add)
                        if c < NCH - 1:
                            hc.link(o)
                    o.then_inc(g_dve, 1)

                def finish(h):
                    dve.wait_ge(*gla(L, "r", h))
                    for half in range(2):
                        dve.wait_ge(u_evac[half], unit_evac(L, UI[("gg", h)], half))
                    for half in range(2):
                        hs = slice(half * HALF, (half + 1) * HALF)
                        o = dve.tensor_tensor(sqg[:, hs], bank(6 + half), sqg[:, hs], ALU.mult)
                    hc.link(o)
                    dve.scalar_tensor_tensor(out=MIX[:, 4 + h, :], in0=sqg, scalar=vl[:, L_GO:L_GO + 1], in1=MIX[:, 4 + h, :], op0=ALU.mult, op1=ALU.mult).then_inc(g_dve, 1)

                def rotate(to, src, hs, tmp):
                    dve.tensor_tensor(tmp, src[64:P, :], rope[64:P, hs], ALU.mult)
                    hc.link(dve.tensor_tensor(to[0:64, hs], src[0:64, :], rope[0:64, hs], ALU.mult))
                    return dve.tensor_tensor(to[0:64, hs], to[0:64, hs], tmp, ALU.add)

                gate(0)
                products(0)
                for h in range(4):
                    causal(h)
                    scan_states(h)
                    if h < 3:
                        gate(h + 1)
                        products(h + 1)
                    finish(h)
                for half in range(2):
                    dve.wait_ge(u_ready, L * 2 * NU + 2 * UI[("kr", 0)] + half + 1)
                    rotate(kr, ps[:, half, :], slice(half * HALF, (half + 1) * HALF), X[0:64, 7 * S + half * HALF:7 * S + (half + 1) * HALF]).then_inc(u_evac[half], 1)
                for j, (lat, g0, r) in enumerate(((c_q, L_QN, r_q), (c_kv, L_KVN, r_kv))):
                    dve.wait_ge(l_r, L * 2 + j + 1)
                    for i, c in enumerate(lat):
                        o = dve.scalar_tensor_tensor(out=c, in0=c, scalar=vl[:, g0 + i:g0 + i + 1], in1=r, op0=ALU.mult, op1=ALU.mult)
                    o.then_inc(l_c, 1)

                def fill(f):
                    kind, h, j = FILLS[f]
                    if kind == "p" and j not in (2, 3):
                        return
                    dve.wait_ge(f_ready, L * NF + f + 1)
                    if kind == "p":
                        dve.wait_ge(hz_ready, L + 1)
                        if (h, j) != (0, 2):
                            fv = FI[("p", h, 2) if j == 3 else ("p", h - 1, 3)]
                            dve.wait_ge(f_evac[fv % 2], fill_evac(L, fv))
                        o = rotate(HT[:, 4 * (h % 2) + 1, :], ps[:, f % 2, :], slice((j % 2) * HALF, (j % 2 + 1) * HALF), rtmp)
                    else:
                        mm = MIX[:, h // 2, (h % 2) * HALF:(h % 2 + 1) * HALF]
                        o = dve.tensor_tensor(mm, bank(f % 2), mm, ALU.mult)
                    o.then_inc(f_evac[f % 2], 1)
                for f in range(8):
                    fill(f)
                f = 8
                for g in range(STEPS):
                    if 1 <= g <= 4 * NT:
                        q = g - 1
                        dve.wait_ge(a_e, L * 4 * NT + q + 1)
                        hc.link(dve.reciprocal(sm[:, q % 2, 3:4], sm[:, q % 2, 2:3]))
                        dve.tensor_scalar(xn[:, q % 2, :], xn[:, q % 2, :], sm[:, q % 2, 3:4], None, ALU.mult).then_inc(a_p, 1)
                    if g < 4 * NT:
                        dve.wait_ge(a_s, L * 4 * NT + g + 1)
                        hc.link(dve.tensor_reduce(sm[:, g % 2, 0:1], psf[:, (2 + 2 * (g % 2)) * HALF:(4 + 2 * (g % 2)) * HALF], AX.X, ALU.max))
                        dve.tensor_scalar(sm[:, g % 2, 1:2], sm[:, g % 2, 0:1], -MLA_SCALE, None, ALU.mult).then_inc(a_neg, 1)
                    if g < 3 * NT:
                        fill(f)
                        f += 1
                    if g >= 5 and (g - 2) % 4 == 3:
                        fill(f)
                        f += 1
                    if 1 <= g <= 4 * NT:
                        q = g - 1
                        G = q // 4
                        dve.wait_ge(a_t[0], L * 4 * NT + q + 1)
                        if G >= 2 and q % 4 == 0:
                            dve.wait_ge(f_ready, L * NF + FI[("v", G - 2, 0)] + 1)
                        dve.tensor_copy(PT[G % 2][:, 0:4, (q % 4) * P:(q % 4 + 1) * P], quads(6)).then_inc(a_tev[0], 1)
                for u in range(2 * NT):
                    n, t = u // NT, u % NT
                    dve.wait_ge(wo_ready, L * 2 * NT + (2 * NT + u + 1))
                    hh = H[:, t, n * HALF:(n + 1) * HALF]
                    dve.tensor_tensor(hh, bank(u % 2), hh, ALU.add).then_inc(wo_evac, 1)
                nt_dve(dve, L * 2 + 3, vl[:, L_PLE:L_PLE + 8])
                for u in range(2 * NT):
                    n, t = u // NT, u % NT
                    dve.wait_ge(pg_sg, L * 2 * NT + u + 1)
                    if n == 1 and t >= 1:
                        dve.wait_ge(h_in, L * NT + NT + t)
                    dve.tensor_tensor(gp, sgp[:, u % 2, :], bank(2 + u % 2), ALU.mult).then_inc(pg_evac, 1)
                    dve.wait_ge(pg_evac, L * 2 * NT + u + 3)
                    hh = H[:, t, n * HALF:(n + 1) * HALF]
                    o = dve.tensor_tensor(hh, gp, hh, ALU.add)
                    if n == 0:
                        hc.link(o)
                    else:
                        o.then_inc(h_in, 1)
                assert PER is None or hc.n == PER, (hc.n, PER)
            layers(dve, layer)
            dve.wait_ge(f_rs, 1)
            dve.wait_ge(fg_in, 16)
            for t in range(NT):
                dve.scalar_tensor_tensor(out=HT[:, t, :], in0=H[:, t, :], scalar=rs[:, t:t + 1], in1=fgain, op0=ALU.mult, op1=ALU.mult).then_inc(f_out, 1)


def kernel(**inputs):
    import concourse.bacc as bacc
    from concourse.bass_utils import run_bass_kernel_spmd

    nc = bacc.Bacc("TRN2", target_bir_lowering=False, num_devices=1)
    arrays, A = {}, {}
    for name, a in list(inputs.items()) + [("kc", shape_constants())]:
        a = np.ascontiguousarray(a)
        arrays["in_" + name] = a
        A[name] = nc.dram_tensor("in_" + name, a.shape, mybir.dt.from_np(a.dtype), kind="ExternalInput").ap()
    out = nc.dram_tensor("out", (1, S, D), F32, kind="ExternalOutput").ap()
    program(nc, A, out)
    return run_bass_kernel_spmd(nc, [arrays], core_ids=[0]).results[0]["out"]
```

```python
from contextlib import ExitStack

import numpy as np
import concourse.bass as bass
from concourse import mybir

F32 = mybir.dt.float32
I32 = mybir.dt.int32
U32 = mybir.dt.uint32
ALU = mybir.AluOpType
ACT = mybir.ActivationFunctionType
AX = mybir.AxisListType
ds = bass.ds

P = 128
S = 1024
D = 1024
NT = S // P
KD = D // P
HALF = 512
EPS = 1e-6

TAPS = 31
PADC = TAPS - 1
HEADS = 4
DH = 64
C_POOL0, C_Q, C_K, C_V = 512, 768, 1280, 1792
WINDOWS = (2, 4, 8, 16)
PADP = 16
LAM_INIT = 0.8 - 0.6 * np.exp(-0.3 * 0)
GROUPS, PER_GROUP, EXPERTS = 4, 4, 16
DE = 256
MTILES = EXPERTS + 2 * S // P - 1
NEG = -3.0e38

LAYERS = 2
C_CQ, C_CKV, C_KR, C_GA, C_GQ, C_GK, C_GV, C_LR, C_GG = 0, 384, 640, 704, 1216, 1472, 1728, 2240, 2272
CH = 64
NCH = S // CH
MLA_SCALE = float(np.float32(192) ** np.float32(-0.5))
PLE = 256

V_AG, V_FG, V_CB, V_LG, V_LB, V_PB, V_PS, V_QG, V_KG, V_SG, V_CW = 0, 8, 16, 18, 20, 22, 24, 26, 27, 28, 29
NV1 = V_CW + 2 * TAPS
L_MIX, L_PLE, L_QN, L_KVN, L_GB, L_GO = 0, 8, 16, 19, 21, 25
NV2 = 26
K_INV, K_OFF, K_RAD, K_SIGN, K_SLOPE, K_POOLW, K_POOL16 = 0, 1, 2, 3, 4, 8, 10
NK = K_POOL16 + 2 * 16


def shape_constants():
    c = np.zeros((P, NK), np.float32)
    p = np.arange(P)
    c[:, K_INV] = 10000.0 ** (-(p % 32) / 32.0)
    c[:, K_OFF] = np.where(p < 64, 0.25, 0.0)
    c[:, K_RAD] = np.where(p < 64, np.pi / 2, 0.0)
    c[:, K_SIGN] = np.where((p >= 64) & (p < 96), -1.0, 1.0)
    for h in range(HEADS):
        c[:, K_SLOPE + h] = (2.0 ** (-8.0 / HEADS)) ** (h + 1)
    for i in range(2):
        w = np.where(p < 64, WINDOWS[2 * i], WINDOWS[2 * i + 1])
        c[:, K_POOLW + i] = 1.0 / w
        c[:, K_POOL16 + 16 * i:K_POOL16 + 16 * i + 16] = 1.0 / np.minimum(np.arange(16)[None, :] + 1, w[:, None])
    return c



class Chain:

    def __init__(self, eng, semaphore, base=0):
        self.eng, self.semaphore, self.base, self.n = eng, semaphore, base, 0

    def link(self, ins):
        self.n += 1
        ins.then_inc(self.semaphore, 1)
        self.eng.wait_ge(self.semaphore, self.base + self.n)


def settle(eng, semaphore):
    eng.sem_inc(semaphore, 1)


def accumulate(pe, o, pairs):
    last = len(pairs) - 1
    for i, (l, r) in enumerate(pairs):
        mm = pe.matmul(o, l, r, start=(i == 0), stop=(i == last))
    return mm


def program(nc, A, out):
    ctx = ExitStack()
    with ctx:
        def sb(name, shape, dt=F32):
            return ctx.enter_context(nc.sbuf_tensor(name, shape, dt))

        def sem(name):
            return ctx.enter_context(nc.semaphore(name))

        def sems(name, n):
            return [sem(f"{name}{i}") for i in range(n)]

        H = sb("H", [P, NT, D])
        HT = sb("HT", [P, KD, S])
        MIX = sb("MIX", [P, KD, S])
        WF = sb("WF", [P, 4, KD, P])
        WT = sb("WT", [P, 2, KD, HALF])
        X = sb("X", [P, 10240])
        ident = sb("ident", [P, P])
        ones = sb("ones", [P, P])
        vec1 = sb("vec1", [P, NV1])
        vec2 = sb("vec2", [P, LAYERS, NV2])
        vl = sb("vl", [P, NV2])
        kc = sb("kc", [P, NK])
        eps = sb("eps", [P, 1])
        mhalf = sb("mhalf", [P, 8])
        ss = sb("ss", [P, 8])
        rs = sb("rs", [P, 8])
        stat = sb("stat", [P, 64])
        xn = sb("xn", [P, 2, D])
        rope = sb("rope", [P, S])
        shared = sb("shared", [P, 1280])
        lamt = sb("lamt", [P, 4, DH])
        pwb = sb("pwb", [P, 2, P])
        ps = ctx.enter_context(nc.psum_tensor("ps", [P, 8, HALF], F32))
        psf = ps[:, :, :].rearrange("p b n -> p (b n)")

        def bank(b, n=HALF, at=0):
            return ps[:, b, at:at + n]

        def quads(b):
            return ps[:, b, :].rearrange("p (c n) -> p c n", n=P)

        xn_dram = nc.dram_tensor("xn_dram", (S, D), F32).ap()
        y_dram = nc.dram_tensor("y_dram", (2 * S, D), F32).ap()
        slot_dram = nc.dram_tensor("slot_dram", (MTILES * P, 4), I32).ap()

        Hf = H[:, :, :].rearrange("p t d -> p (t d)")
        HTf = HT[:, :, :].rearrange("p k t -> p (k t)")
        MXf = MIX[:, :, :].rearrange("p k t -> p (k t)")
        WTf = WT[:, :, :, :].rearrange("p s k n -> p (s k n)")
        WFf = WF[:, :, :, :].rearrange("p s k n -> p (s k n)")

        def slot(flat, i, n=1):
            return flat[:, i * S:(i + n) * S]

        u_pad = Hf[:, 0:2108].rearrange("p (c t) -> p c t", c=2)
        y_cv = Hf[:, 2108:4156].rearrange("p (c t) -> p c t", c=2)
        sq_cv = Hf[:, 4156:6204].rearrange("p (c t) -> p c t", c=2)
        wB = Hf[:, 6204:7244]
        sig_g = MXf[:, 0:2048].rearrange("p (c t) -> p c t", c=2)
        r_cv = MXf[:, 0:1024]
        p_pad = MXf[:, 4096:6176].rearrange("p (c t) -> p c t", c=2)
        wA = MXf[:, 6176:7216]
        fix16 = MXf[:, 7216:7232]
        qT = X[:, 0:4096].rearrange("p (h t) -> p h t", h=4)
        kT = X[:, 4096:8192].rearrange("p (h t) -> p h t", h=4)
        qtok = X[:, 8192:9216].rearrange("p (b n) -> p b n", b=2)
        qn = X[:, 9216:10240].rearrange("p (b n) -> p b n", b=2)
        V1 = WFf.rearrange("p (t n) -> p t n", t=NT)
        qz = [[X[:, 8192:9216], X[:, 9216:10240]], [rope[:, :], xn[:, 1, :]]]
        sS = [[slot(HTf, i) for i in range(3)], [slot(HTf, i) for i in (3, 4)]]
        ATb = slot(HTf, 5, 2).rearrange("p (b k q) -> p b k q", b=2, k=8)
        BH = slot(HTf, 7)
        on = xn[:, 0, 0:384].rearrange("p (b q) -> p b q", b=3)
        osq = xn[:, 0, 384:512]
        ORDER = [b for i in range(NT // 2) for b in (NT - 1 - i, i)]
        BLOCKS = [(h, b) for h in range(HEADS) for b in ORDER]
        NB = len(BLOCKS)
        TURNS = [sum(b // 4 + 1 for _, b in BLOCKS[:g]) for g in range(NB + 1)]
        qsum = stat[:, 0:16].rearrange("p (b g) -> p b g", b=2)
        qrs = stat[:, 16:32].rearrange("p (b g) -> p b g", b=2)
        lam4 = stat[:, 32:40]
        sm = sb("sm", [P, 4, 16])
        cpw = xn[:, 0, 512:1024].rearrange("p (k n) -> p k n", k=2)
        lgT = X[:, 0:1024]
        rb = X[:, 1024:1044]
        R0 = 1056

        def rbuf(at, *shape):
            n = int(np.prod(shape))
            v = X[:, R0 + at:R0 + at + n]
            if len(shape) == 2:
                v = v.rearrange("p (a b) -> p a b", a=shape[0])
            if len(shape) == 3:
                v = v.rearrange("p (a b c) -> p a b c", a=shape[0], b=shape[1])
            return v
        lg = rbuf(0, NT, 20)
        first4 = rbuf(160, 4)
        g_max, g_sum, g_p, m1, v1, v2, w1, w2, den, pos1, pos2 = (rbuf(176 + 8 * i, NT) for i in range(11))
        ge, geq, oh, le, leq, oh1, oh2, pe2 = (rbuf(272 + 32 * i, NT, 4) for i in range(8))
        lsel = rbuf(544, NT, 4, 4)
        S1, S2, MM = rbuf(672, NT, 16), rbuf(800, NT, 16), rbuf(928, NT, 16)
        posn, toff, tmpe = rbuf(1056, NT, 16), rbuf(1184, NT, 16), rbuf(1312, NT, 16)
        cnt, tiles_f, tend, tbase, one16 = (rbuf(1440 + 16 * i, 16) for i in range(5))
        tiles_i = rbuf(1520, 16).bitcast(I32)
        cmpt = rbuf(1552, MTILES + 1, 16)
        iot = rbuf(2064, MTILES + 1)
        et_f = rbuf(2096, MTILES + 1)
        et_i = rbuf(2128, MTILES + 1).bitcast(I32)
        rows = rbuf(2160, NT, 2, 4).bitcast(I32)
        rows_f = rbuf(2160, NT, 2, 4)
        sidx = rbuf(2224, NT, 2).bitcast(I32)
        initrow = rbuf(2240, MTILES, 4).bitcast(I32)
        initrow_f = rbuf(2240, MTILES, 4)
        tri = rbuf(2368, P)
        tokid = rbuf(2496, NT)
        tabs = rbuf(2512, MTILES, 4).bitcast(I32)
        tabs_f = rbuf(2512, MTILES, 4)
        tok_of = rbuf(2512 + 4 * MTILES, 2, 2).bitcast(I32)
        dst_of = rbuf(2512 + 4 * MTILES + 4, 2, 2).bitcast(I32)
        M0 = R0 + 2512 + 4 * MTILES + 12
        sgb = X[:, M0:M0 + 512].rearrange("p (b n) -> p b n", b=2)
        actb = X[:, M0 + 512:M0 + 1024].rearrange("p (b n) -> p b n", b=2)
        actT = X[:, M0 + 1024:M0 + 1536].rearrange("p (b k n) -> p b k n", b=2, k=2)
        yb = X[:, M0 + 1536:M0 + 3584].rearrange("p (b n) -> p b n", b=2)
        wd = MXf[:, 0:4096].rearrange("p (b k n) -> p b k n", b=2, k=2)
        hg = MXf[:, 4096:6144].rearrange("p (b n) -> p b n", b=2)
        hgT = MXf[:, 6144:8192].rearrange("p (b k n) -> p b k n", b=2, k=KD)

        q_dup = [slot(X, 0), slot(X, 1)]
        k_dup = [slot(X, 2), slot(X, 3)]
        cum, la, gt, q_in, sqg = (slot(X, i) for i in range(4, 9))
        wgs = X[:, 9 * S:9 * S + 4 * P].rearrange("p (h n) -> p h n", h=4)
        refs, lasts, decay = (X[:, 9 * S + 512 + 16 * i:9 * S + 528 + 16 * i] for i in range(3))
        kf, kb = slot(WTf, 0), slot(WTf, 1)
        q_even, q_odd = slot(WTf, 2), slot(WTf, 3)
        kv = slot(WTf, 4, 2).rearrange("p (c v) -> p c v", c=NCH)
        st = slot(WTf, 6, 2).rearrange("p (c v) -> p c v", c=NCH)
        ks_even, ks_odd, Af, Ab = (MIX[:, i, :] for i in range(4))
        gv = [slot(WFf, 2), slot(WFf, 3)]
        lrz = xn[:, 0, :]
        reset = shared[:, 0:S]
        mask_f, mask_b = shared[:, S:S + P], shared[:, S + P:S + 2 * P]
        c_q = [slot(X, i) for i in range(3)]
        c_kv = [slot(X, 3), slot(X, 4)]
        kr = slot(X, 5)
        sq_q = [slot(X, 6), slot(X, 7), xn[:, 0, :]]
        sq_kv = [xn[:, 1, :], slot(X, 8)]
        r_q, r_kv = slot(X, 9), slot(X, 6)
        PT = [WTf[:, 4 * S:8 * S].rearrange("p (k q) -> p k q", k=KD), X[:, 6 * S:10 * S].rearrange("p (k q) -> p k q", k=KD)]
        uq = [WFf[:, o:o + 768].rearrange("p (k n) -> p k n", k=3) for o in (2048, 0)]
        ukv = [WFf[:, o + 768:o + 1280].rearrange("p (k n) -> p k n", k=2) for o in (2048, 0)]
        rtmp = WFf[0:64, 1280:1792]
        p_tok = slot(X, 0, 2).rearrange("p (t c) -> p t c", t=NT)
        pT = slot(X, 2, 2).rearrange("p (c t) -> p c t", c=2)
        wpp = slot(X, 4, 2).rearrange("p (c n) -> p c n", c=2)
        sgp = slot(X, 6).rearrange("p (b n) -> p b n", b=2)
        gp = X[:, 7 * S:7 * S + HALF]
        fgain = MIX[:, 0, :]
        pos_i = X[:, 7 * S:8 * S].bitcast(I32)
        ang, turns = slot(X, 8), slot(X, 9)

        UNITS = [("lr", 0, C_LR, 32)]
        for pair in range(2):
            UNITS += [("gq", pair, C_GQ + pair * P, P), ("gk", pair, C_GK + pair * P, P)]
            for h in (2 * pair, 2 * pair + 1):
                UNITS += [("gv", h, C_GV + h * P, P), ("gg", h, C_GG + h * P, P)]
        UNITS += [("cq", i, C_CQ + i * P, P) for i in range(3)] + [("ckv", i, C_CKV + i * P, P) for i in range(2)]
        UNITS += [("kr", 0, C_KR, P)] + [("ga", i, C_GA + i * P, P) for i in range(4)]
        NU = len(UNITS)
        UI = {(k, i): u for u, (k, i, _, _) in enumerate(UNITS)}
        W_DMAS = [3 if k == "kr" else 1 for k, _, _, _ in UNITS]
        W_SOFAR = [sum(W_DMAS[v] for v in range(u % 2, u + 1, 2)) for u in range(NU)]
        W_LAYER = [sum(W_DMAS[s::2]) for s in range(2)]
        FILLS = [("p", 0, j) for j in range(8)]
        STEPS = 4 * NT + 2
        for g in range(STEPS):
            if g // NT + 1 < 4 and g < 4 * NT:
                FILLS.append(("p", g // NT + 1, g % NT))
            if g >= 5 and (g - 2) % 4 == 3:
                FILLS.append(("v", (g - 2) // 4, 0))
        NF = len(FILLS)
        FI = {f: i for i, f in enumerate(FILLS)}

        x_in = sems("x_in", NT)
        const_in, idready = sem("const_in"), sem("idready")
        n_ss, n_rs, n_xn = sem("n_ss"), sem("n_rs"), sem("n_xn")
        n_tp, n_ht = sem("n_tp"), sem("n_ht")
        pool_chain, dve_chain, act_chain = sem("pool_chain"), sem("dve_chain"), sem("act_chain")
        b_w, b_ready, b_evac = sems("b_w", 3), sem("b_ready"), sems("b_evac", 2)
        p_ready = sem("p_ready")
        c_w, c_ready, c_evac = sems("c_w", 2), sem("c_ready"), sem("c_evac")
        c_red, c_rs, c_qn, c_tp, c_tev = (sem(n) for n in ("c_red", "c_rs", "c_qn", "c_tp", "c_tev"))
        cv_dve, pool_d = sem("cv_dve"), sem("pool_d")
        pl_ready, pl_evac = sem("pl_ready"), sem("pl_evac")
        ln_mu, ln_xc, ln_sq, ln_var, ln_sd, ln_n, ln_ys, pw_ready, pw_evac = (
            sem(n) for n in ("ln_mu", "ln_xc", "ln_sq", "ln_var", "ln_sd", "ln_n", "ln_ys", "pw_ready", "pw_evac"))
        lam_e, padded = sem("lam_e"), sem("padded")
        cpw_in, pwb_in = sem("cpw_in"), sem("pwb_in")
        qz_ready, s_ready, s_max, s_neg, e_ready, a_ready, t_ready, at_evac, o_ready, o_cp, o_n, ot_ready, ot_evac, qz_zero = (
            sem(n) for n in ("qz_ready", "s_ready", "s_max", "s_neg", "e_ready", "a_ready", "t_ready", "at_evac",
                             "o_ready", "o_cp", "o_n", "ot_ready", "ot_evac", "qz_zero"))
        wo_w, wo_ready, wo_evac = sems("wo_w", 2), sem("wo_ready"), sem("wo_evac")
        xn_st = sems("xn_st", 2)
        rw_zero, rw_in, rt_ready, rt_cp, rt_tp = (
            sem(n) for n in ("rw_zero", "rw_in", "rt_ready", "rt_cp", "rt_tp"))
        rx, rx_done, rm_ready, rp_ready, slots_set, slots_init, slots_in, experts_set = (
            sem(n) for n in ("rx", "rx_done", "rm_ready", "rp_ready", "slots_set", "slots_init", "slots_in", "experts_set"))
        iotas = sem("iotas")
        m_wgu, m_wd, m_hg, m_sc = (sems(n, 2) for n in ("m_wgu", "m_wd", "m_hg", "m_sc"))
        m_tab, m_tok, m_dst = sem("m_tab"), sem("m_tok"), sem("m_dst")
        m_xt, m_ht, m_gu, m_sg, m_act, m_at, m_aT, m_dn, m_y = (
            sem(n) for n in ("m_xt", "m_ht", "m_gu", "m_sg", "m_act", "m_at", "m_aT", "m_dn", "m_y"))
        y_in, h_in = sems("y_in", 2), sem("h_in")
        comb = sem("comb")
        v2_in, vl_ready, pos_in, rope_set, masks_set = (
            sem(n) for n in ("v2_in", "vl_ready", "pos_in", "rope_set", "masks_set"))
        z_ready, lz_ready, hz_ready, wg_in = (sem(n) for n in ("z_ready", "lz_ready", "hz_ready", "wg_in"))
        u_w, u_ready, u_evac = sems("u_w", 2), sem("u_ready"), sems("u_evac", 2)
        g_pe, g_act, g_dve = sem("g_pe"), sem("g_act"), sem("g_dve")
        GLA_STEPS = {g_pe: [("z", 0)], g_act: [("t", 0), ("e", 0)], g_dve: [("d", 0), ("k", 0), ("q", 0)]}
        for h in range(4):
            more = h < 3
            GLA_STEPS[g_pe] += [("a", h), ("kt", h), ("kv", h)] + [("z", h + 1)] * more + [("o", h), ("ms", h)]
            GLA_STEPS[g_act] += [("ks", h), ("kvc", h)] + [("t", h + 1), ("e", h + 1)] * more + [("sq", h), ("r", h)]
            GLA_STEPS[g_dve] += [("am", h), ("st", h)] + [("d", h + 1), ("k", h + 1), ("q", h + 1)] * more + [("done", h)]
        GLA_AT = {step: (s, i) for s, steps in GLA_STEPS.items() for i, step in enumerate(steps)}

        def gla(L, step, h):
            s, i = GLA_AT[(step, h)]
            return s, L * len(GLA_STEPS[s]) + i + 1

        l_ms, l_r, l_c = sem("l_ms"), sem("l_r"), sem("l_c")
        uw, f_ready, f_evac = sems("uw", 2), sem("f_ready"), sems("f_evac", 2)
        a_s, a_neg, a_e, a_p, a_t, a_tev = sem("a_s"), sem("a_neg"), sem("a_e"), sem("a_p"), sems("a_t", 2), sems("a_tev", 2)
        p_in, p_tp, p_ev, pg_ready, pg_sg, pg_evac = sem("p_in"), sem("p_tp"), sem("p_ev"), sem("pg_ready"), sem("pg_sg"), sem("pg_evac")
        fg_in, f_ss, f_rs, f_out, out_st = sem("fg_in"), sem("f_ss"), sem("f_rs"), sem("f_out"), sem("out_st")


        settled = sem("settled")

        block = ctx.enter_context(nc.Block())

        def nt_act(act, N, ready, stored=None):
            for t in range(NT):
                ready(t)
                if t >= 2:
                    act.wait_ge(n_ss, N * NT + t - 1)
                act.activation(xn[:, t % 2, :], H[:, t, :], ACT.Square, accum_out=ss[:, t:t + 1]).then_inc(n_ss, 1)
            act.wait_ge(n_rs, N + 1)
            act.wait_ge(n_ss, N * NT + NT)
            with act.Fori(0, NT // 2) as i:
                for p in range(2):
                    act.wait_ge(n_tp, N * NT + i * 2 + p + 1)
                    if stored is not None:
                        act.wait_ge(stored[p], i * 16 + 16)
                    act.activation(xn[:, p, :], H[:, ds(i * 2 + p, 1), :].rearrange("p a d -> p (a d)"), ACT.Copy,
                                   scale=rs[:, ds(i * 2 + p, 1)]).then_inc(n_xn, 1)

        def nt_pool(pool, chain, N):
            pool.wait_ge(n_ss, N * NT + NT)
            settle(pool, settled)
            chain.link(pool.tensor_scalar(ss[:, :], ss[:, :], 1.0 / D, EPS, ALU.mult, ALU.add))
            pool.tensor_tensor(rs[:, :], ss[:, :], mhalf[:, :], ALU.pow).then_inc(n_rs, 1)

        def nt_pe(pe, N):
            with pe.Fori(0, NT // 2) as i:
                for p in range(2):
                    pe.wait_ge(n_xn, N * NT + i * 2 + p + 1)
                    pe.wait_ge(n_ht, N * NT + i * 2 + p + 1)
                    for c in range(KD):
                        tp = pe.transpose(bank(2 + 2 * p + c // 4, P, (c % 4) * P), xn[:, p, c * P:(c + 1) * P], ident[:, :])
                    tp.then_inc(n_tp, 1)

        def nt_dve(dve, N, gain):
            with dve.Fori(0, NT // 2) as i:
                for p in range(2):
                    dve.wait_ge(n_tp, N * NT + i * 2 + p + 3)
                    for c in range(2):
                        g = gain[:, 4 * c:4 * c + 4].unsqueeze(2).to_broadcast([P, 4, P])
                        tt = dve.tensor_tensor(HT[:, 4 * c:4 * c + 4, ds((i * 2 + p) * P, P)], quads(2 + 2 * p + c), g, ALU.mult)
                    tt.then_inc(n_ht, 1)

        def experts(eng, step):
            for o in range(3):
                step(0, o)
            with eng.Fori(1, (MTILES - 5) // 2) as i:
                for o in (1, 2):
                    step(i, o)
            for o in range(MTILES - 4, MTILES + 1):
                step(0, o)

        def has(i, o):
            return not isinstance(i, int) or 0 <= 2 * i + o < MTILES

        def wait_past(eng, semaphore, value):
            if not isinstance(value, int) or value > 0:
                eng.wait_ge(semaphore, value)

        def layers(eng, layer):
            with eng.Fori(0, LAYERS) as L:
                layer(L)

        def unit_evac(L, u, half):
            return L * NU + (u + 2)

        def fill_evac(L, f):
            return L * (NF // 2) + (f // 2 + 2)

        @block.sync
        def _(sp):
            for p in range(2):
                sp.sem_inc(xn_st[p], 16)
            for t in range(NT):
                sp.dma_start(H[:, t, :], A["x"][0, t * P:(t + 1) * P, :]).then_inc(x_in[t], 16)
            for u in range(6):
                c, kind = u // 3, u % 3
                c0 = (256, 0, C_POOL0)[kind] + c * P
                if u >= 3:
                    sp.wait_ge(b_ready, 2 * (u - 3) + 2)
                sp.dma_start(WF[:, kind, :, :], A["w_in"][0, :, c0:c0 + P].rearrange("(k p) c -> p k c", p=P)).then_inc(b_w[kind], 16)
            for b in range(3):
                if b == 2:
                    sp.wait_ge(c_ready, NT)
                sp.dma_start(WT[:, b % 2, :, :], A["w_in"][0, :, C_Q + b * HALF:C_Q + (b + 1) * HALF]
                             .rearrange("(k p) c -> p k c", p=P)).then_inc(c_w[b % 2], 16)
                if b == 1:
                    sp.wait_ge(b_ready, 1)
                    sp.dma_start(cpw, A["conv_pw_w"][0].rearrange("(k p) n -> p k n", p=P)).then_inc(cpw_in, 16)
            for n in (1, 0):
                sp.wait_ge(c_ready, (3 - n) * NT)
                sp.dma_start(WT[:, n, :, :], A["w_out"][0, :, n * HALF:(n + 1) * HALF].rearrange("(k p) c -> p k c", p=P)).then_inc(wo_w[n], 16)
            sp.wait_ge(pw_ready, 4)
            sp.wait_ge(pl_ready, 4)
            for t in range(NT):
                sp.dma_start(H[:, t, :], A["x"][0, t * P:(t + 1) * P, :]).then_inc(x_in[t], 16)
            sp.wait_ge(o_ready, HEADS * NT)
            sp.wait_ge(ot_evac, HEADS * NT)
            sp.dma_start(pos_i, A["positions_2"][0:1, :].to_broadcast([P, S])).then_inc(pos_in, 16)
            with nc.allow_non_contiguous_dma(reason="gains and biases, one value a partition"):
                for l in range(LAYERS):
                    for at, n, name in ((L_MIX, 8, "ln_mix_2"), (L_PLE, 8, "ple_norm_2"), (L_QN, 3, "mla_q_norm_2"),
                                        (L_KVN, 2, "mla_kv_norm_2"), (L_GO, 1, "gla_out_norm_2")):
                        sp.dma_start(vec2[:, l, at:at + n], A[name][l].rearrange("(c p) -> p c", p=P)).then_inc(v2_in, 16)
                    for r, name in ((slice(0, 64), "gla_b_gate_fwd_2"), (slice(64, P), "gla_b_gate_bwd_2")):
                        sp.dma_start(vec2[r, l, L_GB:L_GB + 4], A[name][l].rearrange("(h p) -> p h", h=4)).then_inc(v2_in, 16)
            sp.dma_start(rb[:, 0:4], A["router_g_b"][0:1, :].to_broadcast([P, 4])).then_inc(rw_in, 16)
            sp.dma_start(rb[:, 4:20], A["router_e_b"][0:1, :].to_broadcast([P, 16])).then_inc(rw_in, 16)
            sp.wait_ge(rw_zero, 1)
            sp.dma_start(WF[:, 0, :, 0:4], A["router_g_w"][0].rearrange("(k p) c -> p k c", p=P)).then_inc(rw_in, 16)
            sp.dma_start(WF[:, 0, :, 4:20], A["router_e_w"][0].rearrange("(k p) c -> p k c", p=P)).then_inc(rw_in, 16)
            with sp.Fori(0, NT // 2) as i:
                for p in range(2):
                    sp.wait_ge(n_xn, i * 2 + (NT + p + 1))
                    sp.dma_start(xn_dram[ds((i * 2 + p) * P, P), :], xn[:, p, :]).then_inc(xn_st[p], 16)
            sp.wait_ge(slots_init, 1)
            sp.dma_start(slot_dram.rearrange("(a p) c -> p a c", p=P), initrow).then_inc(slots_in, 16)
            sp.wait_ge(slots_set, 16 * 2 * NT)
            sp.wait_ge(experts_set, 1)
            sp.wait_ge(wo_ready, 2 * NT)

            sp.dma_start(tabs, slot_dram.rearrange("(a p) c -> p a c", p=P)).then_inc(m_tab, 16)

            def expert(i, o):
                return sp.value_load(et_i[0:1, ds(i * 2 + o, 1)], min_val=0, max_val=EXPERTS - 1)

            def load_gu(i, o):
                e, p = expert(i, o), o % 2
                wait_past(sp, m_gu, i * 2 + (o - 1))
                sp.dma_start(WT[:, p, :, 0:DE], A["w_gate"][0, ds(e, 1)].rearrange("a (k p) c -> p (a k) c", p=P)).then_inc(m_wgu[p], 16)
                sp.dma_start(WT[:, p, :, DE:2 * DE], A["w_up"][0, ds(e, 1)].rearrange("a (k p) c -> p (a k) c", p=P)).then_inc(m_wgu[p], 16)

            def load_d(i, o):
                e, p = expert(i, o), o % 2
                wait_past(sp, m_dn, i * 2 + (o - 1))
                sp.dma_start(wd[:, p, :, :], A["w_down"][0, ds(e, 1)].rearrange("a (k p) c -> p (a k) c", p=P)).then_inc(m_wd[p], 16)

            def expert_sp(i, o):
                if has(i, o + 2):
                    load_gu(i, o + 2)
                if has(i, o + 1) and o != 0:
                    load_d(i, o + 1)
            for o in range(2):
                load_gu(0, o)
                load_d(0, o)
            experts(sp, expert_sp)
            sp.wait_ge(m_sc[0], 16 * (MTILES // 2 + 1))
            sp.wait_ge(m_sc[1], 16 * (MTILES // 2))
            sp.dma_start(HT[:, :, :], y_dram[0:S, :].rearrange("(t p) d -> p t d", p=P)).then_inc(y_in[0], 16)
            sp.wait_ge(m_dn, MTILES)
            sp.dma_start(MIX[:, :, :], y_dram[S:2 * S, :].rearrange("(t p) d -> p t d", p=P)).then_inc(y_in[1], 16)
            def layer(L):
                win = A["w_in_2"][ds(L, 1)].rearrange("a (k p) c -> p (a k) c", p=P)

                def up_weights(h):
                    s = h % 2
                    wq = A["w_uq_2"][ds(L, 1)].rearrange("a (k p) c -> p (a k) c", p=P)
                    sp.dma_start(uq[s][:, :, 0:192], wq[:, :, h * 192:h * 192 + 192]).then_inc(uw[s], 16)
                    sp.dma_start(uq[s][:, :, 192:224], wq[:, :, h * 192 + 160:h * 192 + 192]).then_inc(uw[s], 16)
                    sp.dma_start(uq[s][:, :, 224:256], wq[:, :, h * 192 + 128:h * 192 + 160]).then_inc(uw[s], 16)
                    sp.dma_start(ukv[s], A["w_ukv_2"][ds(L, 1), :, h * 256:h * 256 + 256].rearrange("a (k p) c -> p (a k) c", p=P)).then_inc(uw[s], 16)
                for u, (kind, i, c0, n) in enumerate(UNITS):
                    if u >= 2:
                        sp.wait_ge(u_ready, L * 2 * NU + 2 * (u - 1))
                        settle(sp, settled)
                    if kind == "kr":
                        for to, c, m in ((0, c0, 64), (64, c0 + 32, 32), (96, c0, 32)):
                            sp.dma_start(WF[:, u % 2, :, to:to + m], win[:, :, c:c + m]).then_inc(u_w[u % 2], 16)
                        up_weights(0)
                    else:
                        sp.dma_start(WF[:, u % 2, :, 0:n], win[:, :, c0:c0 + n]).then_inc(u_w[u % 2], 16)
                    if u == 1:
                        sp.wait_ge(z_ready, L + 1)
                        for r, name in ((0, "gla_w_gate_fwd_2"), (1, "gla_w_gate_bwd_2")):
                            sp.dma_start(wgs[16 * r:16 * r + 16, :, 64 * r:64 * r + 64],
                                         A[name][ds(L, 1)].rearrange("a r (h d) -> r (a h) d", h=4)).then_inc(wg_in, 16)
                sp.dma_start(WT[:, 0, :, :], A["w_out_2"][ds(L, 1), :, 0:HALF].rearrange("a (k p) c -> p (a k) c", p=P)).then_inc(wo_w[0], 16)
                sp.wait_ge(u_ready, L * 2 * NU + 2 * NU)
                up_weights(1)
                for h in (2, 3):
                    sp.wait_ge(f_ready, L * NF + FI[("p", h - 2, 7)] + 1)
                    up_weights(h)
                sp.wait_ge(f_ready, L * NF + FI[("v", 6, 0)] + 1)
                sp.dma_start(WT[:, 1, :, :], A["w_out_2"][ds(L, 1), :, HALF:D].rearrange("a (k p) c -> p (a k) c", p=P)).then_inc(wo_w[1], 16)
                sp.wait_ge(f_ready, L * NF + NF)
                sp.dma_start(p_tok, A["p_2"][ds(L, 1), 0].rearrange("a (t p) c -> p (a t) c", p=P)).then_inc(p_in, 16)
                sp.dma_start(wpp, A["w_ple_proj_2"][ds(L, 1)].rearrange("a (k p) c -> p (a k) c", p=P)).then_inc(p_in, 16)
                for n in range(2):
                    sp.wait_ge(wo_ready, L * 2 * NT + (n + 3) * NT)
                    sp.dma_start(WT[:, n, :, :], A["w_ple_gate_2"][ds(L, 1), :, n * HALF:(n + 1) * HALF]
                                 .rearrange("a (k p) c -> p (a k) c", p=P)).then_inc(wo_w[n], 16)
            layers(sp, layer)
            sp.dma_start(fgain, A["final_norm_2"].rearrange("(a d) -> a d", a=1).to_broadcast([P, D])).then_inc(fg_in, 16)
            for t in range(NT):
                sp.wait_ge(f_out, t + 1)
                sp.dma_start(out[0, t * P:(t + 1) * P, :], HT[:, t, :]).then_inc(out_st, 16)
            sp.wait_ge(out_st, 16 * NT)

        @block.gpsimd
        def _(pool):
            chain = Chain(pool, pool_chain)
            chain.link(pool.memset(ident[:, :], 0.0))
            pool.affine_select(out=ident[:, :], in_=ident[:, :], pattern=[[-1, P]], compare_op=ALU.not_equal, fill=1.0,
                               base=0, channel_multiplier=1).then_inc(idready, 1)
            pool.memset(ones[:, :], 1.0).then_inc(idready, 1)
            pool.memset(mhalf[:, :], -0.5)
            pool.memset(eps[:, :], EPS).then_inc(idready, 1)
            pool.memset(pwb[:, :, :], 0.0).then_inc(padded, 1)
            chain.link(pool.iota(shared[:, 0:S], pattern=[[1, S]], base=-(S - P), channel_multiplier=-1, allow_small_or_imprecise_dtypes=True))
            pool.affine_select(out=shared[:, 0:S], in_=shared[:, 0:S], pattern=[[-1, S]], compare_op=ALU.is_ge, fill=NEG,
                               base=S - P, channel_multiplier=1).then_inc(idready, 1)
            nt_pool(pool, chain, 0)

            for n in range(2 * NT):
                pool.wait_ge(c_red, n + 1)
                if n >= 2:
                    pool.wait_ge(c_qn, n - 1)
                chain.link(pool.tensor_scalar(qsum[:, n % 2, :], qsum[:, n % 2, :], 1.0 / DH, EPS, ALU.mult, ALU.add))
                pool.tensor_tensor(qrs[:, n % 2, :], qsum[:, n % 2, :], mhalf[:, :], ALU.pow).then_inc(c_rs, 1)
            pool.wait_ge(p_ready, 4)
            W0 = S + PADP
            for c in range(2):
                pp = p_pad[:, c, :]
                chain.link(pool.tensor_tensor(wA[:, 1:W0], pp[:, 1:W0], pp[:, 0:W0 - 1], ALU.add))
                if c == 0:
                    chain.link(pool.tensor_tensor(wB[64:P, 3:W0], wA[64:P, 3:W0], wA[64:P, 1:W0 - 2], ALU.add))
                else:
                    chain.link(pool.tensor_tensor(wB[:, 3:W0], wA[:, 3:W0], wA[:, 1:W0 - 2], ALU.add))
                    chain.link(pool.tensor_tensor(wA[:, 7:W0], wB[:, 7:W0], wB[:, 3:W0 - 4], ALU.add))
                    chain.link(pool.tensor_tensor(wB[64:P, 15:W0], wA[64:P, 15:W0], wA[64:P, 7:W0 - 8], ALU.add))
                for lo, ww in ((0, wA), (64, wB)):
                    r = slice(lo, lo + 64)
                    k16 = kc[r, K_POOL16 + 16 * c:K_POOL16 + 16 * c + 16]
                    chain.link(pool.tensor_tensor(fix16[r, :], ww[r, PADP:2 * PADP], k16, ALU.mult))
                    pool.tensor_tensor(pp[r, PADP:2 * PADP], fix16[r, :], pp[r, PADP:2 * PADP], ALU.subtract)
                    chain.link(pool.tensor_scalar(ww[r, 2 * PADP:W0], ww[r, 2 * PADP:W0], kc[r, K_POOLW + c:K_POOLW + c + 1], None, ALU.mult))
                    last = pool.tensor_tensor(pp[r, 2 * PADP:W0], ww[r, 2 * PADP:W0], pp[r, 2 * PADP:W0], ALU.subtract)
                    chain.link(last)
            pool.sem_inc(pool_d, 1)

            pool.wait_ge(c_tp, 2 * NT)
            pool.wait_ge(c_tev, 2 * NT)
            for s in range(2):
                for m in range(2):
                    z = pool.memset(qz[s][m], 0.0)
            z.then_inc(qz_zero, 1)
            for q in range(NB):
                o, ssq, rsq = on[:, q % 3, :], sm[:, q % 4, 8:9], sm[:, q % 4, 9:10]
                pool.wait_ge(o_cp, q + 1)
                chain.link(pool.tensor_scalar(ssq, ssq, 1.0 / P, EPS, ALU.mult, ALU.add))
                chain.link(pool.tensor_tensor(rsq, ssq, mhalf[:, 0:1], ALU.pow))
                pool.tensor_scalar(o, o, rsq, None, ALU.mult).then_inc(o_n, 1)

            pool.wait_ge(ot_evac, HEADS * NT)
            chain.link(pool.memset(shared[:, :], 1.0))
            pool.memset(reset.rearrange("p (c i) -> p c i", c=NCH)[:, :, 0:1], 0.0)
            pool.affine_select(out=mask_f, in_=mask_f, pattern=[[1, P]], compare_op=ALU.is_ge, fill=0.0, base=0, channel_multiplier=-1)
            chain.link(pool.affine_select(out=mask_b, in_=mask_b, pattern=[[-1, P]], compare_op=ALU.is_ge, fill=0.0, base=0, channel_multiplier=1))
            chain.link(pool.memset(mask_f[0:64, CH:P], 0.0))
            chain.link(pool.memset(mask_b[64:P, 0:CH], 0.0))
            pool.sem_inc(masks_set, 1)
            pool.wait_ge(o_ready, HEADS * NT)
            pool.wait_ge(ot_evac, HEADS * NT)
            pool.memset(WF[:, 0, :, :], 0.0).then_inc(rw_zero, 1)
            chain.link(pool.memset(tri, 1.0))
            pool.affine_select(out=tri, in_=tri, pattern=[[1, P]], compare_op=ALU.is_gt, fill=0.0, base=0, channel_multiplier=-1).then_inc(iotas, 1)
            pool.iota(first4, pattern=[[-1, 4]], base=4, channel_multiplier=0, allow_small_or_imprecise_dtypes=True)
            pool.iota(iot, pattern=[[1, MTILES + 1]], base=0, channel_multiplier=0, allow_small_or_imprecise_dtypes=True)
            pool.iota(tokid, pattern=[[P, NT]], base=0, channel_multiplier=1, allow_small_or_imprecise_dtypes=True)
            pool.memset(one16, 1.0)
            pool.iota(initrow[:, :, 0:2], pattern=[[0, MTILES], [0, 2]], base=1 << 20, channel_multiplier=0)
            pool.memset(initrow_f[:, :, 2:4], 0.0).then_inc(slots_init, 1)
            pool.iota(rows[:, :, 0, 0:1], pattern=[[P, NT]], base=0, channel_multiplier=1)
            pool.iota(rows[:, :, 1, 0:1], pattern=[[P, NT]], base=0, channel_multiplier=1)
            pool.iota(rows[:, :, 0, 1:2], pattern=[[P, NT]], base=0, channel_multiplier=1)
            pool.iota(rows[:, :, 1, 1:2], pattern=[[P, NT]], base=S, channel_multiplier=1)
            pool.memset(rows_f[:, :, :, 3:4], 0.0).then_inc(iotas, 1)
            nt_pool(pool, chain, 1)
            pool.wait_ge(slots_in, 16)
            pool.wait_ge(rx_done, 1)
            for t in range(NT):
                for k in range(2):
                    pool.indirect_dma_start(out=slot_dram[:, :], out_offset=bass.IndirectOffsetOnAxis(ap=sidx[:, t, k:k + 1].bitcast(U32), axis=0),
                                            in_=rows[:, t, k, :], in_offset=None).then_inc(slots_set, 16)
            pool.wait_ge(xn_st[0], 16 * 5)
            pool.wait_ge(xn_st[1], 16 * 5)

            pool.wait_ge(wo_ready, 2 * NT)
            chain.link(pool.memset(hg, 0.0))
            pool.wait_ge(m_tab, 16)
            base = chain.n

            def gather(i, o):
                p = o % 2
                wait_past(pool, m_hg[p], i * 16 + 16 * (o // 2))
                settle(pool, settled)
                pool.tensor_copy(tok_of[:, p, 0:1], tabs[:, ds(i * 2 + o, 1), 0:1].rearrange("p a c -> p (a c)")).then_inc(m_tok, 1)
                pool.wait_ge(m_tok, i * 2 + (o + 1))
                wait_past(pool, m_xt, i * 2 + (o - 1))
                settle(pool, settled)
                pool.indirect_dma_start(out=hg[:, p, :], out_offset=None, in_=xn_dram[:, :],
                                        in_offset=bass.IndirectOffsetOnAxis(ap=tok_of[:, p, 0:1].bitcast(U32), axis=0),
                                        bounds_check=S - 1, oob_is_err=False).then_inc(m_hg[p], 16)

            def scatter(i, o):
                p = o % 2
                wait_past(pool, m_sc[p], i * 16 + 16 * (o // 2))
                settle(pool, settled)
                pool.tensor_copy(dst_of[:, p, 0:1], tabs[:, ds(i * 2 + o, 1), 1:2].rearrange("p a c -> p (a c)")).then_inc(m_dst, 1)
                pool.wait_ge(m_dst, i * 2 + (o + 1))
                pool.wait_ge(m_y, i * 2 + (o + 1))
                settle(pool, settled)
                pool.indirect_dma_start(out=y_dram[:, :], out_offset=bass.IndirectOffsetOnAxis(ap=dst_of[:, p, 0:1].bitcast(U32), axis=0),
                                        in_=yb[:, p, :], in_offset=None, bounds_check=2 * S - 1, oob_is_err=False).then_inc(m_sc[p], 16)

            def expert_pool(i, o):
                if has(i, o + 3):
                    gather(i, o + 3)
                if has(i, o - 1):
                    scatter(i, o - 1)
            for o in range(3):
                gather(0, o)
            experts(pool, expert_pool)
            pool.wait_ge(v2_in, 16 * 14)
            base = chain.n

            def layer(L):
                hc = Chain(pool, pool_chain, L * 2 + base)
                pool.wait_ge(h_in, L * NT + NT)
                pool.tensor_copy(vl[:, :], vec2[:, ds(L, 1), :].rearrange("p a n -> p (a n)")).then_inc(vl_ready, 1)
                nt_pool(pool, hc, L * 2 + 2)
                pool.memset(wgs, 0.0)
                pool.memset(WT[:, 0, :, :], 0.0)
                pool.memset(MIX[:, 0:4, :], 0.0).then_inc(z_ready, 1)
                pool.wait_ge(n_tp, L * 2 * NT + 3 * NT + 2)
                settle(pool, settled)
                pool.memset(lrz, 0.0).then_inc(lz_ready, 1)
                pool.wait_ge(*gla(L, "kt", 3))
                settle(pool, settled)
                pool.memset(kr[64:P, :], 0.0)
                pool.wait_ge(u_ready, L * 2 * NU + 2 * NU)
                settle(pool, settled)
                pool.memset(HT[64:P, 1, :], 0.0)
                pool.memset(HT[64:P, 5, :], 0.0).then_inc(hz_ready, 1)
                nt_pool(pool, hc, L * 2 + 3)
                assert hc.n == 2
            layers(pool, layer)
            chain.n = base + 2 * LAYERS
            pool.wait_ge(f_ss, NT)
            chain.link(pool.tensor_scalar(ss[:, :], ss[:, :], 1.0 / D, EPS, ALU.mult, ALU.add))
            pool.tensor_tensor(rs[:, :], ss[:, :], mhalf[:, :], ALU.pow).then_inc(f_rs, 1)

        @block.scalar
        def _(act):
            def vec(dst, src):
                act.dma_start(dst, src).then_inc(const_in, 16)
            with nc.allow_non_contiguous_dma(reason="gains and biases, one value a partition"):
                for at, n, name in ((V_AG, 8, "attn_norm_g"), (V_FG, 8, "ffn_norm_g"), (V_CB, 2, "conv_b"), (V_LG, 2, "conv_ln_g"),
                                    (V_LB, 2, "conv_ln_b"), (V_PB, 2, "conv_pw_b"), (V_PS, 2, "pool_scale"), (V_SG, 1, "attn_sub_norm_g")):
                    vec(vec1[:, at:at + n], A[name][0].rearrange("(c p) -> p c", p=P))
                vec(kc[:, :], A["kc"])
                for m in range(2):
                    vec(vec1[64 * m:64 * m + 64, V_QG:V_QG + 1], A["q_norm_g"][0].rearrange("(p c) -> p c", c=1))
                    vec(vec1[64 * m:64 * m + 64, V_KG:V_KG + 1], A["k_norm_g"][0].rearrange("(p c) -> p c", c=1))
                for c in range(2):
                    vec(vec1[:, V_CW + TAPS * c:V_CW + TAPS * (c + 1)], A["conv_w"][0, :, c * P:(c + 1) * P].rearrange("j p -> p j"))
                for i, name in enumerate(("lambda_q1", "lambda_k1", "lambda_q2", "lambda_k2")):
                    vec(lamt[:, i, :], A[name][0:1, :].to_broadcast([P, DH]))
                act.wait_ge(padded, 1)
                for g in range(4):
                    r = slice(64 * (g % 2), 64 * (g % 2) + 64)
                    act.dma_start(pwb[r, g // 2, r], A["pool_w"][0, g]).then_inc(pwb_in, 16)
            nt_act(act, 0, lambda t: act.wait_ge(x_in[t], 16))
            act.wait_ge(padded, 3)
            for c in range(2):
                for half in range(2):
                    n = 6 * c + half
                    act.wait_ge(b_ready, n + 1)
                    act.activation(sig_g[:, c, half * HALF:(half + 1) * HALF], bank(n % 2), ACT.Sigmoid).then_inc(b_evac[n % 2], 1)
                for half in range(2):
                    n = 6 * c + 4 + half
                    act.wait_ge(b_ready, n + 1)
                    act.activation(p_pad[:, c, PADP + half * HALF:PADP + (half + 1) * HALF], bank(n % 2), ACT.Copy).then_inc(b_evac[n % 2], 1)
            act.drain().then_inc(p_ready, 4)
            act.wait_ge(lam_e, 1)
            act.activation(lam4[:, 2:4], lam4[:, 0:2], ACT.Exp).then_inc(lam_e, 1)
            for n in range(3 * NT):
                act.wait_ge(c_ready, n + 1)
                if n < 2 * NT:
                    if n >= 2:
                        act.wait_ge(c_qn, n - 1)
                        act.wait_ge(c_red, n - 1)
                    act.activation(qtok[:, n % 2, :], bank(n % 2), ACT.Copy)
                    act.activation(xn[:, n % 2, 0:HALF], bank(n % 2), ACT.Square).then_inc(c_evac, 1)
                else:
                    act.activation(V1[:, n - 2 * NT, :], bank(n % 2), ACT.Copy).then_inc(c_evac, 1)
            for c in range(2):
                for half in range(2):
                    n = 2 * c + half
                    act.wait_ge(pl_ready, n + 1)
                    act.activation(MIX[:, 2 + c, half * HALF:(half + 1) * HALF], bank(n), ACT.Copy, scale=vec1[:, V_PS + c:V_PS + c + 1]).then_inc(pl_evac, 1)
            for half in range(2):
                act.wait_ge(ln_xc, half + 1)
                for c in range(2):
                    sq = act.activation(sq_cv[:, c, half * HALF:(half + 1) * HALF], y_cv[:, c, half * HALF:(half + 1) * HALF], ACT.Square)
                sq.then_inc(ln_sq, 1)
            for half in range(2):
                act.wait_ge(ln_var, half + 1)
                act.activation(r_cv[:, half * HALF:(half + 1) * HALF], bank(6 + half), ACT.Sqrt, scale=1.0 / 256, bias=eps[:, 0:1]).then_inc(ln_sd, 1)
            for half in range(2):
                act.wait_ge(ln_n, half + 1)
                for c in range(2):
                    yy = y_cv[:, c, half * HALF:(half + 1) * HALF]
                    si = act.activation(yy, yy, ACT.Silu, scale=vec1[:, V_LG + c:V_LG + c + 1], bias=vec1[:, V_LB + c:V_LB + c + 1])
                si.then_inc(ln_ys, 1)
            for n in range(4):
                half, m = n // 2, n % 2
                act.wait_ge(pw_ready, n + 1)
                act.activation(MIX[:, m, half * HALF:(half + 1) * HALF], bank(n), ACT.Identity, bias=vec1[:, V_PB + m:V_PB + m + 1]).then_inc(pw_evac, 1)

            def stage(h):
                if h >= 2:
                    act.wait_ge(s_ready, 2 * NT * (h - 1))
                act.activation(qz[h % 2][0][0:64, :], qT[0:64, h, :], ACT.Copy)
                act.activation(qz[h % 2][1][64:P, :], qT[64:P, h, :], ACT.Copy).then_inc(qz_ready, 1)
            act.wait_ge(c_tev, 2 * NT)
            act.wait_ge(qz_zero, 1)
            stage(0)
            for g in range(NB + 3):
                if 2 <= g < NB + 2:
                    q = g - 2
                    b = BLOCKS[q][1]
                    for j in range(b // 4 + 1):
                        act.wait_ge(t_ready, TURNS[q] + j + 1)
                        if q >= 2:
                            act.wait_ge(o_ready, q - 1)
                        k = min(4, b + 1 - 4 * j)
                        act.activation(ATb[:, q % 2, 4 * j:4 * j + k, :], quads(4 + j)[:, 0:k, :], ACT.Copy).then_inc(at_evac, 1)
                if g < NB:
                    W = (BLOCKS[g][1] + 1) * P
                    for m in range(2):
                        act.wait_ge(s_neg, 2 * g + m + 1)
                        w = sS[m][g % (3 - m)][:, 0:W]
                        act.activation(w, w, ACT.Exp, bias=sm[:, g % 4, 2 + m:3 + m], accum_out=sm[:, g % 4, 4 + m:5 + m]).then_inc(e_ready, 1)
                if g >= 3:
                    q = g - 3
                    act.wait_ge(o_ready, q + 1)
                    if q >= 3:
                        act.wait_ge(ot_ready, q - 2)
                    act.activation(on[:, q % 3, :], bank(6, P, (q % 4) * P), ACT.Copy, scale=sm[:, q % 4, 6:7])
                    if q >= 1:
                        act.wait_ge(o_cp, q)
                    act.activation(osq, bank(6, P, (q % 4) * P), ACT.Square, scale=sm[:, q % 4, 6:7], accum_out=sm[:, q % 4, 8:9]).then_inc(o_cp, 1)
                if g < NB and g % NT == 2 and BLOCKS[g][0] + 1 < HEADS:
                    stage(BLOCKS[g][0] + 1)
            nt_act(act, 1, lambda t: act.wait_ge(wo_evac, NT + t + 1), stored=xn_st)
            for half in range(2):
                act.wait_ge(rt_ready, half + 1)
                act.activation(lgT[:, half * HALF:(half + 1) * HALF], bank(6 + half), ACT.Copy).then_inc(rt_cp, 1)
            act.wait_ge(rx, 1)
            act.activation(ge, ge, ACT.Exp).then_inc(rx, 1)
            act.wait_ge(rx, 3)
            act.activation(le, le, ACT.Exp).then_inc(rx, 1)
            act.wait_ge(rope_set, 1)
            act.activation(ang, ang, ACT.Sin).then_inc(rope_set, 1)

            def expert_act(i, o):
                t = i * 2 + o
                if has(i, o - 1):
                    p = (o - 1) % 2
                    act.wait_ge(m_at, t)
                    wait_past(act, m_dn, i * 2 + (o - 2))
                    act.activation(actT[:, p, :, :], quads(4)[:, 0:2, :], ACT.Copy).then_inc(m_aT, 1)
                if has(i, o):
                    act.wait_ge(m_gu, i * 2 + (o + 1))
                    wait_past(act, m_act, i * 2 + (o - 1))
                    act.activation(sgb[:, o % 2, :], bank(2 + o % 2, DE), ACT.Silu).then_inc(m_sg, 1)
                if has(i, o - 1):
                    act.wait_ge(m_dn, t)
                    wait_past(act, m_sc[p], i * 16 + 16 * ((o - 1) // 2))
                    act.activation(yb[:, p, :], psf[:, 6 * HALF:8 * HALF], ACT.Copy).then_inc(m_y, 1)
            experts(act, expert_act)

            for half in range(2):
                act.sem_inc(u_evac[half], 1)
                act.sem_inc(f_evac[half], 1)
            PER = 4 * 2 + 4 + 2

            def layer(L):
                hc = Chain(act, act_chain, L * PER)
                nt_act(act, L * 2 + 2, lambda t: act.wait_ge(h_in, L * NT + t + 1))
                act.wait_ge(vl_ready, L + 1)

                def evac(kind, i):
                    u = UI[(kind, i)]
                    for half in range(2):
                        hs = slice(half * HALF, (half + 1) * HALF)
                        act.wait_ge(u_ready, L * 2 * NU + 2 * u + half + 1)
                        if kind == "lr":
                            act.wait_ge(lz_ready, L + 1)
                            o = act.activation(lrz[0:32, hs], ps[0:32, half, :], ACT.Copy)
                        if kind in ("gq", "gk"):
                            if i == 1:
                                act.wait_ge(*gla(L, "q", 1))
                            dup, scale = (q_dup, 64 ** -0.5) if kind == "gq" else (k_dup, 1.0)
                            for h in range(2):
                                for r in range(2):
                                    o = act.activation(dup[h][64 * r:64 * r + 64, hs], ps[64 * h:64 * h + 64, half, :], ACT.Copy, scale=scale)
                        if kind == "gv":
                            o = act.activation(gv[i % 2][:, hs], bank(half), ACT.Copy)
                        if kind == "gg":
                            o = act.activation(MIX[:, 4 + i, hs], bank(half), ACT.Silu)
                        if kind == "ga":
                            o = act.activation(MIX[:, i, hs], bank(half), ACT.Silu)
                        if kind in ("cq", "ckv"):
                            if (kind, i) == ("cq", 0):
                                act.wait_ge(*gla(L, "q", 3))
                            if (kind, i) == ("ckv", 1):
                                act.wait_ge(*gla(L, "done", 3))
                            to, sq = (c_q, sq_q) if kind == "cq" else (c_kv, sq_kv)
                            act.activation(to[i][:, hs], bank(half), ACT.Copy)
                            o = act.activation(sq[i][:, hs], bank(half), ACT.Square)
                        o.then_inc(u_evac[half], 1)

                def gate(h):
                    act.wait_ge(*gla(L, "z", h))
                    if h >= 1:
                        act.wait_ge(*gla(L, "k", h - 1))
                    for half in range(2):
                        hs, bias = slice(half * HALF, (half + 1) * HALF), vl[:, L_GB + h:L_GB + h + 1]
                        act.activation(la[:, hs], bank(2 + half), ACT.Identity, bias=bias)
                        o = act.activation(gt[:, hs], bank(2 + half), ACT.Abs, bias=bias)
                    hc.link(o)
                    hc.link(act.activation(gt, gt, ACT.Exp, scale=-1.0))
                    act.activation(gt, gt, ACT.Ln, bias=ones[:, 0:1]).then_inc(g_act, 1)

                def exps(h):
                    act.wait_ge(*gla(L, "d", h))
                    if h >= 1:
                        act.wait_ge(*gla(L, "a", h - 1))
                    act.activation(q_in, gt, ACT.Exp, scale=1 / 16.0)
                    act.activation(gt, gt, ACT.Exp, scale=-1 / 16.0)
                    act.activation(la, la, ACT.Exp, scale=1 / 16.0)
                    act.activation(cum, cum, ACT.Exp, scale=1 / 16.0)
                    act.activation(decay, lasts, ACT.Exp, scale=1 / 16.0).then_inc(g_act, 1)

                def ks_copy(h):
                    act.wait_ge(*gla(L, "kt", h))
                    act.wait_ge(z_ready, L + 1)
                    for half in range(2):
                        act.activation(ks_even[0:64, half * HALF:(half + 1) * HALF], ps[0:64, 6 + half, :], ACT.Copy)
                        o = act.activation(ks_odd[64:P, half * HALF:(half + 1) * HALF], ps[64:P, 6 + half, :], ACT.Copy)
                    o.then_inc(g_act, 1)

                def kv_copy(h):
                    act.wait_ge(*gla(L, "kv", h))
                    for b in range(4):
                        o = act.activation(kv[:, 4 * b:4 * b + 4, :], quads(2 + b), ACT.Copy)
                    o.then_inc(g_act, 1)

                def square(h):
                    act.wait_ge(*gla(L, "o", h))
                    if h >= 1:
                        act.wait_ge(*gla(L, "done", h - 1))
                    for half in range(2):
                        o = act.activation(sqg[:, half * HALF:(half + 1) * HALF], bank(6 + half), ACT.Square)
                    o.then_inc(g_act, 1)

                def inv_rms(to, b, width, done):
                    for half in range(2):
                        o = act.activation(to[:, half * HALF:(half + 1) * HALF], bank(b + half), ACT.Ln, scale=1.0 / width, bias=eps[:, 0:1])
                    hc.link(o)
                    act.activation(to, to, ACT.Exp, scale=-0.5).then_inc(done, 1)

                def rms(h):
                    act.wait_ge(*gla(L, "ms", h))
                    inv_rms(sqg, 4, P, g_act)

                for e in (("lr", 0), ("gq", 0), ("gk", 0)):
                    evac(*e)
                gate(0)
                evac("gv", 0)
                exps(0)
                evac("gg", 0)
                under = ((("gv", 1), ("gg", 1), ("gq", 1)), (("gk", 1), ("gv", 2), ("gg", 2)), (("gv", 3), ("gg", 3), ("cq", 0)), (("cq", 1), ("cq", 2), ("ckv", 0)))
                for h in range(4):
                    ks_copy(h)
                    evac(*under[h][0])
                    kv_copy(h)
                    if h < 3:
                        gate(h + 1)
                    evac(*under[h][1])
                    if h < 3:
                        exps(h + 1)
                    square(h)
                    evac(*under[h][2])
                    rms(h)
                evac("ckv", 1)
                act.wait_ge(l_ms, L * 2 + 1)
                inv_rms(r_q, 2, 384, l_r)
                evac("ga", 0)
                act.wait_ge(l_ms, L * 2 + 2)
                inv_rms(r_kv, 6, 256, l_r)
                for i in range(1, 4):
                    evac("ga", i)
                assert hc.n == PER, hc.n

                def fill(f):
                    kind, h, j = FILLS[f]
                    if kind != "p" or j in (2, 3):
                        return
                    act.wait_ge(f_ready, L * NF + f + 1)
                    at = (0, 0, None, None, 2, 2, 3, 3)[j]
                    act.activation(HT[:, 4 * (h % 2) + at, (j % 2) * HALF:(j % 2 + 1) * HALF], bank(f % 2), ACT.Copy).then_inc(f_evac[f % 2], 1)
                for f in range(8):
                    fill(f)
                f = 8
                for g in range(STEPS):
                    if g < 4 * NT:
                        act.wait_ge(a_neg, L * 4 * NT + g + 1)
                        if g >= 2:
                            act.wait_ge(a_t[1], L * 4 * NT + g - 1)
                        act.activation(xn[:, g % 2, :], psf[:, (2 + 2 * (g % 2)) * HALF:(4 + 2 * (g % 2)) * HALF], ACT.Exp, scale=MLA_SCALE,
                                       bias=sm[:, g % 2, 1:2], accum_out=sm[:, g % 2, 2:3]).then_inc(a_e, 1)
                    if g < 3 * NT:
                        fill(f)
                        f += 1
                    if g >= 5 and (g - 2) % 4 == 3:
                        f += 1
                    if 1 <= g <= 4 * NT:
                        q = g - 1
                        G = q // 4
                        act.wait_ge(a_t[1], L * 4 * NT + q + 1)
                        if G >= 2 and q % 4 == 0:
                            act.wait_ge(f_ready, L * NF + FI[("v", G - 2, 0)] + 1)
                        act.activation(PT[G % 2][:, 4:8, (q % 4) * P:(q % 4 + 1) * P], quads(7), ACT.Copy).then_inc(a_tev[1], 1)
                for b in range(4):
                    act.wait_ge(p_tp, L * 4 + b + 1)
                    act.activation(pT[:, b // 2, (b % 2) * HALF:(b % 2 + 1) * HALF], bank(2 + b), ACT.Copy).then_inc(p_ev, 1)
                nt_act(act, L * 2 + 3, lambda t: act.wait_ge(wo_evac, L * 2 * NT + (3 * NT + t + 1)))
                for u in range(2 * NT):
                    act.wait_ge(pg_ready, L * 2 * NT + u + 1)
                    act.wait_ge(pg_evac, L * 2 * NT + u + 1)
                    act.activation(sgp[:, u % 2, :], bank(u % 2), ACT.Sigmoid).then_inc(pg_sg, 1)
            layers(act, layer)
            for t in range(NT):
                act.wait_ge(h_in, (LAYERS + 1) * NT - NT + t + 1)
                if t >= 2:
                    act.wait_ge(f_ss, t - 1)
                act.activation(xn[:, t % 2, :], H[:, t, :], ACT.Square, accum_out=ss[:, t:t + 1]).then_inc(f_ss, 1)

        @block.tensor
        def _(pe):
            pe.sem_inc(n_tp, 2)
            pe.wait_ge(idready, 4)
            nt_pe(pe, 0)
            pe.wait_ge(n_ht, 2 + NT)
            for u in range(6):
                pe.wait_ge(b_w[u % 3], 16 * (u // 3 + 1))
                for half in range(2):
                    n = 2 * u + half
                    if n >= 2:
                        pe.wait_ge(b_evac[n % 2], n // 2)
                    accumulate(pe, bank(n % 2), [(WF[:, u % 3, k, :], HT[:, k, half * HALF:(half + 1) * HALF]) for k in range(KD)]).then_inc(b_ready, 1)
            pe.wait_ge(b_evac[0], 6)
            pe.wait_ge(b_evac[1], 6)

            def turn(n):
                pe.wait_ge(c_qn, n + 1)
                if n >= 2:
                    pe.wait_ge(c_tev, n - 1)
                for h in range(4):
                    tp = pe.transpose(bank(2 + n % 2, P, h * P), qn[:, n % 2, h * P:(h + 1) * P], ident[:, :])
                tp.then_inc(c_tp, 1)
            for n in range(3 * NT):
                blk, t = n // NT, n % NT
                if t == 0:
                    pe.wait_ge(c_w[blk % 2], 16 * (blk // 2 + 1))
                if n >= 2:
                    pe.wait_ge(c_evac, n - 1)
                accumulate(pe, bank(n % 2), [(HT[:, k, t * P:(t + 1) * P], WT[:, blk % 2, k, :]) for k in range(KD)]).then_inc(c_ready, 1)
                if 2 <= n < 2 * NT + 2:
                    turn(n - 2)
            pe.wait_ge(c_evac, 3 * NT)
            pe.wait_ge(c_tev, 2 * NT)
            pe.wait_ge(pool_d, 1)
            pe.wait_ge(pwb_in, 64)
            for c in range(2):
                for half in range(2):
                    pe.matmul(bank(2 * c + half), pwb[:, c, :], p_pad[:, c, PADP + half * HALF:PADP + (half + 1) * HALF], start=True, stop=True).then_inc(pl_ready, 1)
            pe.wait_ge(cv_dve, 1)
            for half in range(2):
                accumulate(pe, bank(4 + half), [(ones[:, :], y_cv[:, c, half * HALF:(half + 1) * HALF]) for c in range(2)]).then_inc(ln_mu, 1)
            for half in range(2):
                pe.wait_ge(ln_sq, half + 1)
                accumulate(pe, bank(6 + half), [(ones[:, :], sq_cv[:, c, half * HALF:(half + 1) * HALF]) for c in range(2)]).then_inc(ln_var, 1)
            pe.wait_ge(pl_evac, 4)
            pe.wait_ge(cpw_in, 16)
            for n in range(4):
                half, m = n // 2, n % 2
                pe.wait_ge(ln_ys, half + 1)
                accumulate(pe, bank(n), [(cpw[:, c, m * P:(m + 1) * P], y_cv[:, c, half * HALF:(half + 1) * HALF]) for c in range(2)]).then_inc(pw_ready, 1)

            pe.wait_ge(pw_evac, 4)
            for g in range(NB + 5):
                if g < NB:
                    h, b = BLOCKS[g]
                    W = (b + 1) * P
                    if g % NT == 0:
                        pe.wait_ge(qz_ready, h + 1)
                    for m in range(2):
                        if g >= 1:
                            pe.wait_ge(s_max, 2 * g + m - 1)
                        for j in range((W + HALF - 1) // HALF):
                            w = min(HALF, W - j * HALF)
                            mm = pe.matmul(bank(2 * m + j, w), qz[h % 2][m][:, b * P:(b + 1) * P], kT[:, h, j * HALF:j * HALF + w], start=True, stop=True)
                        mm.then_inc(s_ready, 1)
                if 2 <= g < NB + 2:
                    q = g - 2
                    b = BLOCKS[q][1]
                    pe.wait_ge(a_ready, q + 1)
                    if q >= 1:
                        pe.wait_ge(at_evac, TURNS[q])
                    for j in range(b // 4 + 1):
                        for k in range(4 * j, min(4 * j + 4, b + 1)):
                            tp = pe.transpose(bank(4 + j, P, (k % 4) * P), sS[0][q % 3][:, k * P:(k + 1) * P], ident[:, :])
                        tp.then_inc(t_ready, 1)
                if 3 <= g < NB + 3:
                    q = g - 3
                    h, b = BLOCKS[q]
                    pe.wait_ge(at_evac, TURNS[q + 1])
                    if q >= 1:
                        pe.wait_ge(o_cp, q)
                    accumulate(pe, bank(6, P, (q % 4) * P), [(ATb[:, q % 2, k, :], V1[:, k, h * P:(h + 1) * P]) for k in range(b + 1)]).then_inc(o_ready, 1)
                if g >= 5:
                    q = g - 5
                    pe.wait_ge(o_n, q + 1)
                    if q >= 1:
                        pe.wait_ge(ot_evac, q)
                    pe.transpose(bank(7, P, (q % 4) * P), on[:, q % 3, :], ident[:, :]).then_inc(ot_ready, 1)
            pe.wait_ge(ot_evac, NB)
            for n in range(2):
                pe.wait_ge(wo_w[n], 16)
                for t in range(NT):
                    u = n * NT + t
                    if u >= 2:
                        pe.wait_ge(wo_evac, u - 1)
                    accumulate(pe, bank(u % 2), [(MIX[:, k, t * P:(t + 1) * P], WT[:, n, k, :]) for k in range(KD)]).then_inc(wo_ready, 1)
            nt_pe(pe, 1)
            pe.wait_ge(n_ht, 2 + 2 * NT)
            pe.wait_ge(rw_in, 64)
            for half in range(2):
                accumulate(pe, bank(6 + half), [(WF[:, 0, k, :], HT[:, k, half * HALF:(half + 1) * HALF]) for k in range(KD)]).then_inc(rt_ready, 1)
            pe.wait_ge(rt_cp, 2)
            for t in range(NT):
                tp = pe.transpose(bank(2 + t // 4, P, (t % 4) * P), lgT[:, t * P:(t + 1) * P], ident[:, :])
            tp.then_inc(rt_tp, 1)
            pe.wait_ge(rm_ready, 1)
            MMf = MM.rearrange("p t e -> p (t e)")
            pe.wait_ge(iotas, 2)
            pe.matmul(bank(6, P), tri, MMf, start=True, stop=True)
            pe.matmul(bank(7, P), ones[:, :], MMf, start=True, stop=True).then_inc(rp_ready, 1)

            def turn_rows(i, o):
                p = o % 2
                pe.wait_ge(m_hg[p], i * 16 + (16 * (o // 2) + 16))
                wait_past(pe, m_ht, i * 2 + o)
                for c in range(KD):
                    tp = pe.transpose(bank(c // 4, P, (c % 4) * P), hg[:, p, c * P:(c + 1) * P], ident[:, :])
                tp.then_inc(m_xt, 1)

            def gate_up(i, o, ks):
                p = o % 2
                if 0 in ks:
                    pe.wait_ge(m_ht, i * 2 + (o + 1))
                    pe.wait_ge(m_wgu[p], i * 32 + (32 * (o // 2) + 32))
                    wait_past(pe, m_act, i * 2 + (o - 1))
                for k in ks:
                    mm = pe.matmul(bank(2 + p), hgT[:, p, k, :], WT[:, p, k, :], start=(k == 0), stop=(k == KD - 1))
                if KD - 1 in ks:
                    mm.then_inc(m_gu, 1)

            def turn_act(i, o):
                pe.wait_ge(m_act, i * 2 + (o + 1))
                wait_past(pe, m_aT, i * 2 + o)
                for k in range(2):
                    tp = pe.transpose(bank(4, P, k * P), actb[:, o % 2, k * P:(k + 1) * P], ident[:, :])
                tp.then_inc(m_at, 1)

            def down(i, o):
                p = o % 2
                pe.wait_ge(m_aT, i * 2 + (o + 1))
                pe.wait_ge(m_wd[p], i * 16 + (16 * (o // 2) + 16))
                wait_past(pe, m_y, i * 2 + o)
                for n in range(2):
                    mm = accumulate(pe, bank(6 + n), [(actT[:, p, k, :], wd[:, p, k, n * HALF:(n + 1) * HALF]) for k in range(2)])
                mm.then_inc(m_dn, 1)

            def expert_pe(i, o):
                if has(i, o):
                    gate_up(i, o, range(0, 5))
                if has(i, o - 1):
                    turn_act(i, o - 1)
                if has(i, o):
                    gate_up(i, o, range(5, KD))
                if has(i, o + 1):
                    turn_rows(i, o + 1)
                if has(i, o - 1):
                    down(i, o - 1)
            turn_rows(0, 0)
            experts(pe, expert_pe)

            def layer(L):
                nt_pe(pe, L * 2 + 2)
                pe.wait_ge(n_ht, L * 2 * NT + 3 * NT + 2)

                def unit(kind, i):
                    u = UI[(kind, i)]
                    s = u % 2
                    pe.wait_ge(u_w[s], L * 16 * W_LAYER[s] + 16 * W_SOFAR[u])
                    for half in range(2):
                        pe.wait_ge(u_evac[half], L * NU + u + 1)
                        if kind == "gv":
                            for t in range(4):
                                mm = accumulate(pe, bank(half, P, t * P), [(HT[:, k, (4 * half + t) * P:(4 * half + t + 1) * P], WF[:, s, k, :]) for k in range(KD)])
                        else:
                            m = UNITS[u][3]
                            mm = accumulate(pe, ps[0:m, half, :], [(WF[:, s, k, 0:m], HT[:, k, half * HALF:(half + 1) * HALF]) for k in range(KD)])
                        mm.then_inc(u_ready, 1)

                def gates(h):
                    if h == 0:
                        pe.wait_ge(wg_in, L * 32 + 32)
                        for half in range(2):
                            pe.wait_ge(u_evac[half], unit_evac(L, 0, half))
                    else:
                        pe.wait_ge(*gla(L, "kvc", h - 1))
                    for half in range(2):
                        mm = pe.matmul(bank(2 + half), wgs[:, h, :], lrz[:, half * HALF:(half + 1) * HALF], start=True, stop=True)
                    mm.then_inc(g_pe, 1)

                def inner(h):
                    pe.wait_ge(*gla(L, "k", h))
                    if h >= 1:
                        pe.wait_ge(*gla(L, "r", h - 1))
                    for d, kk in enumerate((kf, kb)):
                        for t in range(NT):
                            mm = pe.matmul(bank(2 + 2 * d + t // 4, P, (t % 4) * P), kk[:, t * P:(t + 1) * P], q_in[:, t * P:(t + 1) * P], start=True, stop=True)
                    mm.then_inc(g_pe, 1)
                    if h >= 1:
                        pe.wait_ge(*gla(L, "done", h - 1))
                    for t in range(NT):
                        tp = pe.transpose(bank(6 + t // 4, P, (t % 4) * P), la[:, t * P:(t + 1) * P], ident[:, :])
                    tp.then_inc(g_pe, 1)

                def states(h):
                    pe.wait_ge(*gla(L, "ks", h))
                    pe.wait_ge(*gla(L, "am", h))
                    for half in range(2):
                        pe.wait_ge(u_evac[half], unit_evac(L, UI[("gv", h)], half))
                    for c in range(NCH):
                        t = c // 2
                        mm = pe.matmul(bank(2 + c // 4, P, (c % 4) * P), (ks_even, ks_odd)[c % 2][:, t * P:(t + 1) * P], gv[h % 2][:, t * P:(t + 1) * P], start=True, stop=True)
                    mm.then_inc(g_pe, 1)

                def outputs(h):
                    pe.wait_ge(*gla(L, "st", h))
                    for t in range(NT):
                        ts = slice(t * P, (t + 1) * P)
                        mm = accumulate(pe, bank(6 + t // 4, P, (t % 4) * P), [(gv[h % 2][:, ts], Af[:, ts]), (gv[h % 2][:, ts], Ab[:, ts]),
                                                                             (st[:, 2 * t, :], q_even[:, ts]), (st[:, 2 * t + 1, :], q_odd[:, ts])])
                    mm.then_inc(g_pe, 1)

                def squares(h):
                    pe.wait_ge(*gla(L, "sq", h))
                    for half in range(2):
                        mm = pe.matmul(bank(4 + half), ones[:, :], sqg[:, half * HALF:(half + 1) * HALF], start=True, stop=True)
                    mm.then_inc(g_pe, 1)

                unit("lr", 0)
                unit("gq", 0)
                unit("gk", 0)
                gates(0)
                unit("gv", 0)
                unit("gg", 0)
                under = ((("gv", 1), ("gg", 1), ("gq", 1)), (("gk", 1), ("gv", 2), ("gg", 2)), (("gv", 3), ("gg", 3), ("cq", 0)), (("cq", 1), ("cq", 2), ("ckv", 0)))
                for h in range(4):
                    inner(h)
                    unit(*under[h][0])
                    states(h)
                    if h < 3:
                        gates(h + 1)
                    unit(*under[h][1])
                    outputs(h)
                    unit(*under[h][2])
                    squares(h)
                unit("ckv", 1)
                for half in range(2):
                    accumulate(pe, bank(2 + half), [(ones[:, :], q[:, half * HALF:(half + 1) * HALF]) for q in sq_q])
                pe.drain().then_inc(l_ms, 1)
                unit("kr", 0)
                unit("ga", 0)
                pe.wait_ge(*gla(L, "done", 3))
                for half in range(2):
                    accumulate(pe, bank(6 + half), [(ones[:, :], q[:, half * HALF:(half + 1) * HALF]) for q in sq_kv])
                pe.drain().then_inc(l_ms, 1)
                for i in range(1, 4):
                    unit("ga", i)
                for half in range(2):
                    pe.wait_ge(u_evac[half], unit_evac(L, NU - 1, half))

                def fill(f):
                    kind, h, j = FILLS[f]
                    pe.wait_ge(f_evac[f % 2], L * (NF // 2) + f // 2 + 1)
                    o = bank(f % 2)
                    if kind == "p":
                        s, hs = h % 2, slice((j % 2) * HALF, (j % 2 + 1) * HALF)
                        if j == 0:
                            pe.wait_ge(uw[s], L * 128 + 64 * (h // 2) + 64)
                        if j < 4:
                            c = (j // 2) * P
                            mm = accumulate(pe, o, [(uq[s][:, k, c:c + P], c_q[k][:, hs]) for k in range(3)])
                        elif j < 6:
                            mm = accumulate(pe, o, [(ukv[s][:, k, 0:P], c_kv[k][:, hs]) for k in range(2)])
                        else:
                            for t in range(4):
                                ts = slice((4 * (j % 2) + t) * P, (4 * (j % 2) + t + 1) * P)
                                mm = accumulate(pe, bank(f % 2, P, t * P), [(c_kv[k][:, ts], ukv[s][:, k, P:2 * P]) for k in range(2)])
                    else:
                        G = h
                        hd = G // 2
                        for i in range(2):
                            pe.wait_ge(a_tev[i], L * 4 * NT + 4 * G + 4)
                            fv = FI[("p", hd, 6 + i)]
                            if fv % 2 != f % 2:
                                pe.wait_ge(f_evac[fv % 2], fill_evac(L, fv))
                        mm = accumulate(pe, o, [(HT[:, 4 * (hd % 2) + 3, k * P:(k + 1) * P], PT[G % 2][:, k, :]) for k in range(KD)])
                    mm.then_inc(f_ready, 1)
                pe.wait_ge(l_c, L * 2 + 2)
                pe.wait_ge(hz_ready, L + 1)
                for f in range(8):
                    fill(f)
                f = 8
                for g in range(STEPS):
                    if g < 4 * NT:
                        h, b, s = g // NT, g % NT, 4 * (g // NT % 2)
                        if b == 0:
                            for j in (4, 5):
                                fv = FI[("p", h, j)]
                                pe.wait_ge(f_evac[fv % 2], fill_evac(L, fv))
                        if g >= 2:
                            pe.wait_ge(a_e, L * 4 * NT + g - 1)
                        for half in range(2):
                            hs = slice(half * HALF, (half + 1) * HALF)
                            mm = accumulate(pe, bank(2 + 2 * (g % 2) + half), [(HT[:, s, b * P:(b + 1) * P], HT[:, s + 2, hs]),
                                                                               (HT[:, s + 1, b * P:(b + 1) * P], kr[:, hs])])
                        mm.then_inc(a_s, 1)
                    if g < 3 * NT:
                        fill(f)
                        f += 1
                    if g >= 5 and (g - 2) % 4 == 3:
                        fill(f)
                        f += 1
                    if 1 <= g <= 4 * NT:
                        q = g - 1
                        pe.wait_ge(a_p, L * 4 * NT + q + 1)
                        for half in range(2):
                            if q >= 1:
                                pe.wait_ge(a_tev[half], L * 4 * NT + q)
                            for k in range(4):
                                tp = pe.transpose(bank(6 + half, P, k * P), xn[:, q % 2, (4 * half + k) * P:(4 * half + k + 1) * P], ident[:, :])
                            tp.then_inc(a_t[half], 1)
                assert f == NF
                for i in range(2):
                    pe.wait_ge(f_evac[i], L * (NF // 2) + NF // 2 + 1)
                for n in range(2):
                    pe.wait_ge(wo_w[n], L * 32 + 32)
                    for t in range(NT):
                        u = n * NT + t
                        pe.wait_ge(wo_evac, L * 2 * NT + (2 * NT + u - 1))
                        accumulate(pe, bank(u % 2), [(MIX[:, k, t * P:(t + 1) * P], WT[:, n, k, :]) for k in range(KD)]).then_inc(wo_ready, 1)
                    if n == 0:
                        pe.wait_ge(p_in, L * 32 + 32)
                        for b in range(4):
                            for t in range(4):
                                tp = pe.transpose(bank(2 + b, P, t * P), p_tok[:, 4 * (b % 2) + t, (b // 2) * P:(b // 2 + 1) * P], ident[:, :])
                            tp.then_inc(p_tp, 1)
                pe.wait_ge(p_ev, L * 4 + 4)
                pe.wait_ge(wo_evac, L * 2 * NT + 4 * NT)
                settle(pe, settled)
                nt_pe(pe, L * 2 + 3)
                pe.wait_ge(n_ht, L * 2 * NT + 4 * NT + 2)
                for n in range(2):
                    pe.wait_ge(wo_w[n], L * 32 + 48)
                    for t in range(NT):
                        u = n * NT + t
                        pe.wait_ge(pg_evac, L * 2 * NT + u + 1)
                        accumulate(pe, bank(u % 2), [(HT[:, k, t * P:(t + 1) * P], WT[:, n, k, :]) for k in range(KD)])
                        accumulate(pe, bank(2 + u % 2), [(pT[:, c, t * P:(t + 1) * P], wpp[:, c, n * HALF:(n + 1) * HALF]) for c in range(2)]).then_inc(pg_ready, 1)
            layers(pe, layer)

        @block.vector
        def _(dve):
            chain = Chain(dve, dve_chain)
            dve.sem_inc(n_ht, 2)
            dve.wait_ge(const_in, 16 * 19)
            chain.link(dve.tensor_scalar(vec1[:, V_QG:V_QG + 1], vec1[:, V_QG:V_QG + 1], DH ** -0.5, None, ALU.mult))
            chain.link(dve.tensor_scalar(vec1[:, V_SG:V_SG + 1], vec1[:, V_SG:V_SG + 1], 1.0 - LAM_INIT, None, ALU.mult))
            for i in range(2):
                chain.link(dve.tensor_tensor(lamt[:, 2 * i, :], lamt[:, 2 * i, :], lamt[:, 2 * i + 1, :], ALU.mult))
                chain.link(dve.tensor_reduce(lam4[:, i:i + 1], lamt[:, 2 * i, :], AX.X, ALU.add))
            dve.sem_inc(lam_e, 1)
            nt_dve(dve, 0, vec1[:, V_AG:V_AG + 8])
            dve.wait_ge(b_ready, 1)
            dve.memset(p_pad[:, :, 0:PADP], 0.0).then_inc(padded, 1)
            dve.memset(u_pad[:, :, 0:PADC], 0.0).then_inc(padded, 1)
            for c in range(2):
                for half in range(2):
                    n = 6 * c + 2 + half
                    dve.wait_ge(b_ready, n + 1)
                    dve.wait_ge(b_evac[n % 2], 3 * c + 1)
                    dve.tensor_tensor(u_pad[:, c, PADC + half * HALF:PADC + (half + 1) * HALF], bank(n % 2),
                                      sig_g[:, c, half * HALF:(half + 1) * HALF], ALU.mult).then_inc(b_evac[n % 2], 1)
            dve.wait_ge(lam_e, 2)
            chain.link(dve.tensor_tensor(lam4[:, 4:5], lam4[:, 2:3], lam4[:, 3:4], ALU.subtract))
            chain.link(dve.tensor_scalar(lam4[:, 4:5], lam4[:, 4:5], LAM_INIT, -1.0, ALU.add, ALU.mult))
            dve.wait_ge(padded, 3)
            tap = 0
            for n in range(2 * NT + 2):
                if n < 2 * NT:
                    dve.wait_ge(c_evac, n + 1)
                    if n >= 2:
                        dve.wait_ge(c_rs, n - 1)
                    dve.tensor_reduce(qsum[:, n % 2, :], xn[:, n % 2, 0:HALF].rearrange("p (g d) -> p g d", d=DH), AX.X, ALU.add).then_inc(c_red, 1)
                    for _ in range(2):
                        if tap < TAPS:
                            for c in range(2):
                                w = vec1[:, V_CW + TAPS * c + tap:V_CW + TAPS * c + tap + 1]
                                uu = u_pad[:, c, tap:tap + S]
                                if tap == 0:
                                    o = dve.tensor_scalar(y_cv[:, c, :], uu, w, vec1[:, V_CB + c:V_CB + c + 1], ALU.mult, ALU.add)
                                else:
                                    o = dve.scalar_tensor_tensor(out=y_cv[:, c, :], in0=uu, scalar=w, in1=y_cv[:, c, :], op0=ALU.mult, op1=ALU.add)
                            chain.link(o)
                            tap += 1
                if 1 <= n <= 2 * NT:
                    q = n - 1
                    dve.wait_ge(c_rs, q + 1)
                    if q >= 2:
                        dve.wait_ge(c_tp, q - 1)
                    dve.tensor_tensor(qn[:, q % 2, :].rearrange("p (g d) -> p g d", d=DH), qtok[:, q % 2, :].rearrange("p (g d) -> p g d", d=DH),
                                      qrs[:, q % 2, :].unsqueeze(2).to_broadcast([P, 8, DH]), ALU.mult).then_inc(c_qn, 1)
                if n >= 2:
                    q = n - 2
                    dve.wait_ge(c_tp, q + 1)
                    to, gc = (qT, V_QG) if q < NT else (kT, V_KG)
                    dve.tensor_scalar(to[:, :, (q % NT) * P:(q % NT + 1) * P], quads(2 + q % 2), vec1[:, gc:gc + 1], None, ALU.mult).then_inc(c_tev, 1)
            dve.drain().then_inc(cv_dve, 1)
            for half in range(2):
                hs = slice(half * HALF, (half + 1) * HALF)
                dve.wait_ge(ln_mu, half + 1)
                for c in range(2):
                    xc = dve.scalar_tensor_tensor(out=y_cv[:, c, hs], in0=bank(4 + half), scalar=-1.0 / 256, in1=y_cv[:, c, hs], op0=ALU.mult, op1=ALU.add)
                xc.then_inc(ln_xc, 1)
            for half in range(2):
                hs = slice(half * HALF, (half + 1) * HALF)
                dve.wait_ge(ln_sd, half + 1)
                chain.link(dve.reciprocal(r_cv[:, hs], r_cv[:, hs]))
                for c in range(2):
                    yn = dve.tensor_tensor(y_cv[:, c, hs], y_cv[:, c, hs], r_cv[:, hs], ALU.mult)
                yn.then_inc(ln_n, 1)

            dve.wait_ge(c_ready, 3 * NT)
            for g in range(NB + 5):
                if g < NB and g % NT == 0:
                    h = BLOCKS[g][0]
                    if g >= 1:
                        dve.wait_ge(s_max, 2 * g)
                    chain.link(dve.tensor_scalar(BH, shared[:, 0:S], kc[:, K_SLOPE + h:K_SLOPE + h + 1], None, ALU.mult))
                if 1 <= g <= NB:
                    q = g - 1
                    W = (BLOCKS[q][1] + 1) * P
                    t = sm[:, q % 4, :]
                    dve.wait_ge(e_ready, 2 * q + 2)
                    chain.link(dve.reciprocal(t[:, 6:8], t[:, 4:6]))
                    chain.link(dve.scalar_tensor_tensor(out=t[:, 7:8], in0=t[:, 7:8], scalar=t[:, 4:5], in1=lam4[:, 4:5], op0=ALU.mult, op1=ALU.mult))
                    dve.scalar_tensor_tensor(out=sS[0][q % 3][:, 0:W], in0=sS[1][q % 2][:, 0:W], scalar=t[:, 7:8], in1=sS[0][q % 3][:, 0:W],
                                             op0=ALU.mult, op1=ALU.add).then_inc(a_ready, 1)
                if g < NB:
                    b = BLOCKS[g][1]
                    W = (b + 1) * P
                    for m in range(2):
                        dve.wait_ge(s_ready, 2 * g + m + 1)
                        if m == 0 and g >= 3:
                            dve.wait_ge(t_ready, TURNS[g - 2])
                        if m == 1 and g >= 2:
                            dve.wait_ge(a_ready, g - 1)
                        dve.tensor_tensor_reduce(sS[m][g % (3 - m)][:, 0:W], psf[:, 2 * m * HALF:2 * m * HALF + W], BH[:, S - P - b * P:S],
                                                 1.0, NEG, ALU.add, ALU.max, sm[:, g % 4, m:m + 1]).then_inc(s_max, 1)
                        dve.wait_ge(s_max, 2 * g + m + 1)
                        dve.tensor_scalar(sm[:, g % 4, 2 + m:3 + m], sm[:, g % 4, m:m + 1], -1.0, None, ALU.mult).then_inc(s_neg, 1)
                if g >= 5:
                    q = g - 5
                    h, b = BLOCKS[q]
                    dve.wait_ge(ot_ready, q + 1)
                    dve.tensor_scalar(MIX[:, 4 + h, b * P:(b + 1) * P], bank(7, P, (q % 4) * P), vec1[:, V_SG:V_SG + 1], None, ALU.mult).then_inc(ot_evac, 1)

            for u in range(2 * NT):
                n, t = u // NT, u % NT
                dve.wait_ge(wo_ready, u + 1)
                dve.wait_ge(x_in[t], 32)
                hh = H[:, t, n * HALF:(n + 1) * HALF]
                dve.tensor_tensor(hh, bank(u % 2), hh, ALU.add).then_inc(wo_evac, 1)
            nt_dve(dve, 1, vec1[:, V_FG:V_FG + 8])
            dve.wait_ge(rt_tp, 1)
            dve.wait_ge(rw_in, 64)
            for j in range(2):
                chain.link(dve.tensor_tensor(lg[:, 4 * j:4 * j + 4, :], quads(2 + j)[:, :, 0:20], rb.unsqueeze(1).to_broadcast([P, 4, 20]), ALU.add))

            dve.wait_ge(iotas, 2)

            def col(a, n=4):
                return a.unsqueeze(2).to_broadcast([P, NT, n])

            def tt(o, a, b, op):
                chain.link(dve.tensor_tensor(o, a, b, op))

            def first_max(o, values, eq):
                chain.link(dve.tensor_reduce(m1, values, AX.X, ALU.max))
                tt(eq, values, col(m1), ALU.is_equal)
                tt(eq, eq, first4.unsqueeze(1).to_broadcast([P, NT, 4]), ALU.mult)
                chain.link(dve.tensor_reduce(m1, eq, AX.X, ALU.max))
                tt(o, eq, col(m1), ALU.is_equal)
            chain.link(dve.tensor_reduce(g_max, lg[:, :, 0:4], AX.X, ALU.max))
            tt(ge, lg[:, :, 0:4], col(g_max), ALU.subtract)
            dve.sem_inc(rx, 1)
            dve.wait_ge(rx, 2)
            chain.link(dve.tensor_reduce(g_sum, ge, AX.X, ALU.add))
            chain.link(dve.reciprocal(g_p, g_sum))
            first_max(oh, ge, geq)
            ev = lg[:, :, 4:20].rearrange("p t (g e) -> p t g e", g=GROUPS)
            tt(lsel, ev, oh.unsqueeze(3).to_broadcast([P, NT, 4, 4]), ALU.mult)
            chain.link(dve.tensor_reduce(le, lsel.rearrange("p t g e -> p t e g"), AX.X, ALU.add))
            chain.link(dve.tensor_reduce(g_max, le, AX.X, ALU.max))
            tt(le, le, col(g_max), ALU.subtract)
            dve.sem_inc(rx, 1)
            dve.wait_ge(rx, 4)
            first_max(oh1, le, leq)
            chain.link(dve.tensor_reduce(v1, le, AX.X, ALU.max))
            chain.link(dve.scalar_tensor_tensor(out=pe2, in0=oh1, scalar=-2.0, in1=le, op0=ALU.mult, op1=ALU.add))
            first_max(oh2, pe2, leq)
            chain.link(dve.tensor_reduce(v2, pe2, AX.X, ALU.max))
            tt(den, v1, v2, ALU.add)
            chain.link(dve.reciprocal(den, den))
            tt(den, den, g_p, ALU.mult)
            tt(w1, v1, den, ALU.mult)
            tt(w2, v2, den, ALU.mult)
            for o, e in ((S1, oh1), (S2, oh2)):
                tt(o.rearrange("p t (g e) -> p t g e", g=GROUPS), oh.unsqueeze(3).to_broadcast([P, NT, 4, 4]),
                   e.unsqueeze(2).to_broadcast([P, NT, 4, 4]), ALU.mult)
            tt(MM, S1, S2, ALU.add)
            dve.sem_inc(rm_ready, 1)
            dve.wait_ge(rp_ready, 1)
            within = bank(6, P).rearrange("p (t e) -> p t e", t=NT)
            intile = bank(7, P).rearrange("p (t e) -> p t e", t=NT)
            chain.link(dve.memset(toff[:, 0, :], 0.0))
            for t in range(1, NT):
                tt(toff[:, t, :], toff[:, t - 1, :], intile[:, t - 1, :], ALU.add)
            tt(cnt, toff[:, NT - 1, :], intile[:, NT - 1, :], ALU.add)
            tt(posn, toff, within, ALU.add)
            chain.link(dve.tensor_scalar(tiles_i, cnt, float(P - 1), None, ALU.add))
            chain.link(dve.tensor_single_scalar(tiles_i, tiles_i, 7, ALU.arith_shift_right))
            chain.link(dve.tensor_copy(tiles_f, tiles_i))
            chain.link(dve.tensor_tensor_scan(tend, one16, tiles_f, 0.0, ALU.mult, ALU.add))
            tt(tbase, tend, tiles_f, ALU.subtract)
            chain.link(dve.scalar_tensor_tensor(out=posn, in0=tbase.unsqueeze(1).to_broadcast([P, NT, 16]), scalar=float(P), in1=posn, op0=ALU.mult, op1=ALU.add))
            for k, (o, s, w) in enumerate(((pos1, S1, w1), (pos2, S2, w2))):
                tt(tmpe, s, posn, ALU.mult)
                chain.link(dve.tensor_reduce(o, tmpe, AX.X, ALU.add))
                chain.link(dve.tensor_copy(sidx[:, :, k:k + 1], o.unsqueeze(2)))
                chain.link(dve.tensor_copy(rows_f[:, :, k, 2:3], w.unsqueeze(2)))
            dve.sem_inc(rx_done, 1)
            tt(cmpt, iot.unsqueeze(2).to_broadcast([P, MTILES + 1, 16]), tend.unsqueeze(1).to_broadcast([P, MTILES + 1, 16]), ALU.is_ge)
            chain.link(dve.tensor_reduce(et_f, cmpt, AX.X, ALU.add))
            chain.link(dve.tensor_scalar(et_f, et_f, float(EXPERTS - 1), None, ALU.min))
            chain.link(dve.tensor_copy(et_i, et_f))
            dve.sem_inc(experts_set, 1)
            C1 = 6.28125
            C2 = float(np.float32(np.round((2 * np.pi - C1) * 2.0 ** 20) * 2.0 ** -20))
            C3 = float(2 * np.pi - C1 - C2)
            MAGIC = 1.5 * 2.0 ** 23
            dve.wait_ge(pos_in, 16)
            chain.link(dve.tensor_copy(ang, pos_i))
            chain.link(dve.tensor_scalar(ang, ang, kc[:, K_INV:K_INV + 1], None, ALU.mult))
            chain.link(dve.tensor_scalar(turns, ang, 1.0 / (2 * np.pi), kc[:, K_OFF:K_OFF + 1], ALU.mult, ALU.add))
            chain.link(dve.tensor_scalar(turns, turns, MAGIC, None, ALU.add))
            chain.link(dve.tensor_scalar(turns, turns, -MAGIC, None, ALU.add))
            for c in (C1, C2, C3):
                chain.link(dve.scalar_tensor_tensor(out=ang, in0=turns, scalar=-c, in1=ang, op0=ALU.mult, op1=ALU.add))
            chain.link(dve.tensor_scalar(ang, ang, kc[:, K_RAD:K_RAD + 1], 3.1415925, ALU.add, ALU.min))
            dve.tensor_scalar(ang, ang, -3.1415925, None, ALU.max).then_inc(rope_set, 1)
            dve.wait_ge(rope_set, 2)
            dve.tensor_scalar(rope[:, :], ang, kc[:, K_SIGN:K_SIGN + 1], None, ALU.mult).then_inc(rope_set, 1)
            dve.wait_ge(rope_set, 3)

            def rows_to_ht(i, o):
                p = o % 2
                dve.wait_ge(m_xt, i * 2 + (o + 1))
                wait_past(dve, m_gu, i * 2 + (o - 1))
                for c in range(2):
                    g = vec1[:, V_FG + 4 * c:V_FG + 4 * c + 4].unsqueeze(2).to_broadcast([P, 4, P])
                    ins = dve.tensor_tensor(hgT[:, p, 4 * c:4 * c + 4, :], quads(c), g, ALU.mult)
                ins.then_inc(m_ht, 1)

            def expert_dve(i, o):
                if has(i, o):
                    dve.wait_ge(m_sg, i * 2 + (o + 1))
                    wait_past(dve, m_at, i * 2 + (o - 1))
                    dve.scalar_tensor_tensor(out=actb[:, o % 2, :], in0=sgb[:, o % 2, :], scalar=tabs_f[:, ds(i * 2 + o, 1), 2:3].rearrange("p a c -> p (a c)"),
                                             in1=bank(2 + o % 2, DE, DE), op0=ALU.mult, op1=ALU.mult).then_inc(m_act, 1)
                if has(i, o + 1):
                    rows_to_ht(i, o + 1)
            dve.wait_ge(m_tab, 16)
            rows_to_ht(0, 0)
            experts(dve, expert_dve)
            dve.wait_ge(y_in[0], 16)
            dve.wait_ge(y_in[1], 16)
            for t in range(NT):
                dve.tensor_tensor(HT[:, t, :], HT[:, t, :], MIX[:, t, :], ALU.add).then_inc(comb, 1)
            for t in range(NT):
                dve.wait_ge(comb, t + 1)
                dve.tensor_tensor(H[:, t, :], H[:, t, :], HT[:, t, :], ALU.add).then_inc(h_in, 1)

            dve.sem_inc(pg_evac, 2)
            dve.wait_ge(masks_set, 1)
            base = chain.n
            PER = 159

            def layer(L):
                hc = Chain(dve, dve_chain, L * (PER or 0) + base)
                dve.wait_ge(vl_ready, L + 1)
                settle(dve, settled)
                nt_dve(dve, L * 2 + 2, vl[:, L_MIX:L_MIX + 8])
                dirs = ((slice(0, 64), 1), (slice(64, P), -1))

                def chunks(a):
                    return a.rearrange("p (c i) -> p c i", c=NCH)

                def gate(h):
                    dve.wait_ge(*gla(L, "t", h))
                    hc.link(dve.scalar_tensor_tensor(out=la, in0=la, scalar=0.0, in1=gt, op0=ALU.min, op1=ALU.subtract))
                    hc.link(dve.tensor_tensor_scan(cum[0:64, :], reset[0:64, :], la[0:64, :], 0.0, ALU.mult, ALU.add))
                    hc.link(dve.tensor_tensor_scan(cum[64:P, ::-1], reset[64:P, :], la[64:P, ::-1], 0.0, ALU.mult, ALU.add))
                    cc = chunks(cum)
                    for r, ref, last in ((slice(0, 64), CH // 2 - 1, CH - 1), (slice(64, P), CH // 2, 0)):
                        dve.tensor_copy(refs[r, :].unsqueeze(2), cc[r, :, ref:ref + 1])
                        o = dve.tensor_copy(lasts[r, :].unsqueeze(2), cc[r, :, last:last + 1])
                    hc.link(o)
                    dve.tensor_tensor(chunks(gt), cc, refs.unsqueeze(2).to_broadcast([P, NCH, CH]), ALU.subtract)
                    dve.tensor_tensor(chunks(la), lasts.unsqueeze(2).to_broadcast([P, NCH, CH]), cc, ALU.subtract).then_inc(g_dve, 1)

                def products(h):
                    dve.wait_ge(*gla(L, "e", h))
                    dve.wait_ge(z_ready, L + 1)
                    for half in range(2):
                        dve.wait_ge(u_evac[half], unit_evac(L, UI[("gk", h // 2)], half))
                    q, k = q_dup[h % 2], k_dup[h % 2]
                    dve.tensor_tensor(q_in, q_in, q, ALU.mult)
                    dve.tensor_tensor(kf[0:64, :], gt[0:64, :], k[0:64, :], ALU.mult)
                    dve.tensor_tensor(kb[64:P, :], gt[64:P, :], k[64:P, :], ALU.mult)
                    dve.tensor_tensor(la, la, k, ALU.mult).then_inc(g_dve, 1)
                    if h >= 1:
                        dve.wait_ge(*gla(L, "o", h - 1))
                    for par, to in ((0, q_even), (1, q_odd)):
                        v = lambda a: a.rearrange("p (t c i) -> p t c i", t=NT, c=2)[:, :, par, :]
                        o = dve.tensor_tensor(v(to), v(cum), v(q), ALU.mult)
                    o.then_inc(g_dve, 1)

                def causal(h):
                    dve.wait_ge(*gla(L, "a", h))
                    settle(dve, settled)
                    for d, (to, mask) in enumerate(((Af, mask_f), (Ab, mask_b))):
                        for b in range(2):
                            o = dve.copy_predicated(to[:, b * HALF:(b + 1) * HALF].rearrange("p (t i) -> p t i", t=4),
                                                    mask.bitcast(U32).unsqueeze(1).to_broadcast([P, 4, P]), quads(2 + 2 * d + b))
                    o.then_inc(g_dve, 1)

                def scan_states(h):
                    dve.wait_ge(*gla(L, "kvc", h))
                    if h == 0:
                        dve.memset(st[0:64, 0, :], 0.0)
                        hc.link(dve.memset(st[64:P, NCH - 1, :], 0.0))
                    for c in range(1, NCH):
                        b = NCH - 1 - c
                        dve.scalar_tensor_tensor(out=st[0:64, c, :], in0=st[0:64, c - 1, :], scalar=decay[0:64, c - 1:c], in1=kv[0:64, c - 1, :], op0=ALU.mult, op1=ALU.add)
                        o = dve.scalar_tensor_tensor(out=st[64:P, b, :], in0=st[64:P, b + 1, :], scalar=decay[64:P, b + 1:b + 2], in1=kv[64:P, b + 1, :], op0=ALU.mult, op1=ALU.add)
                        if c < NCH - 1:
                            hc.link(o)
                    o.then_inc(g_dve, 1)

                def finish(h):
                    dve.wait_ge(*gla(L, "r", h))
                    for half in range(2):
                        dve.wait_ge(u_evac[half], unit_evac(L, UI[("gg", h)], half))
                    for half in range(2):
                        hs = slice(half * HALF, (half + 1) * HALF)
                        o = dve.tensor_tensor(sqg[:, hs], bank(6 + half), sqg[:, hs], ALU.mult)
                    hc.link(o)
                    dve.scalar_tensor_tensor(out=MIX[:, 4 + h, :], in0=sqg, scalar=vl[:, L_GO:L_GO + 1], in1=MIX[:, 4 + h, :], op0=ALU.mult, op1=ALU.mult).then_inc(g_dve, 1)

                def rotate(to, src, hs, tmp):
                    dve.tensor_tensor(tmp, src[64:P, :], rope[64:P, hs], ALU.mult)
                    hc.link(dve.tensor_tensor(to[0:64, hs], src[0:64, :], rope[0:64, hs], ALU.mult))
                    return dve.tensor_tensor(to[0:64, hs], to[0:64, hs], tmp, ALU.add)

                gate(0)
                products(0)
                for h in range(4):
                    causal(h)
                    scan_states(h)
                    if h < 3:
                        gate(h + 1)
                        products(h + 1)
                    finish(h)
                for half in range(2):
                    dve.wait_ge(u_ready, L * 2 * NU + 2 * UI[("kr", 0)] + half + 1)
                    rotate(kr, ps[:, half, :], slice(half * HALF, (half + 1) * HALF), X[0:64, 7 * S + half * HALF:7 * S + (half + 1) * HALF]).then_inc(u_evac[half], 1)
                for j, (lat, g0, r) in enumerate(((c_q, L_QN, r_q), (c_kv, L_KVN, r_kv))):
                    dve.wait_ge(l_r, L * 2 + j + 1)
                    for i, c in enumerate(lat):
                        o = dve.scalar_tensor_tensor(out=c, in0=c, scalar=vl[:, g0 + i:g0 + i + 1], in1=r, op0=ALU.mult, op1=ALU.mult)
                    o.then_inc(l_c, 1)

                def fill(f):
                    kind, h, j = FILLS[f]
                    if kind == "p" and j not in (2, 3):
                        return
                    dve.wait_ge(f_ready, L * NF + f + 1)
                    if kind == "p":
                        dve.wait_ge(hz_ready, L + 1)
                        if (h, j) != (0, 2):
                            fv = FI[("p", h, 2) if j == 3 else ("p", h - 1, 3)]
                            dve.wait_ge(f_evac[fv % 2], fill_evac(L, fv))
                        o = rotate(HT[:, 4 * (h % 2) + 1, :], ps[:, f % 2, :], slice((j % 2) * HALF, (j % 2 + 1) * HALF), rtmp)
                    else:
                        mm = MIX[:, h // 2, (h % 2) * HALF:(h % 2 + 1) * HALF]
                        o = dve.tensor_tensor(mm, bank(f % 2), mm, ALU.mult)
                    o.then_inc(f_evac[f % 2], 1)
                for f in range(8):
                    fill(f)
                f = 8
                for g in range(STEPS):
                    if 1 <= g <= 4 * NT:
                        q = g - 1
                        dve.wait_ge(a_e, L * 4 * NT + q + 1)
                        hc.link(dve.reciprocal(sm[:, q % 2, 3:4], sm[:, q % 2, 2:3]))
                        dve.tensor_scalar(xn[:, q % 2, :], xn[:, q % 2, :], sm[:, q % 2, 3:4], None, ALU.mult).then_inc(a_p, 1)
                    if g < 4 * NT:
                        dve.wait_ge(a_s, L * 4 * NT + g + 1)
                        hc.link(dve.tensor_reduce(sm[:, g % 2, 0:1], psf[:, (2 + 2 * (g % 2)) * HALF:(4 + 2 * (g % 2)) * HALF], AX.X, ALU.max))
                        dve.tensor_scalar(sm[:, g % 2, 1:2], sm[:, g % 2, 0:1], -MLA_SCALE, None, ALU.mult).then_inc(a_neg, 1)
                    if g < 3 * NT:
                        fill(f)
                        f += 1
                    if g >= 5 and (g - 2) % 4 == 3:
                        fill(f)
                        f += 1
                    if 1 <= g <= 4 * NT:
                        q = g - 1
                        G = q // 4
                        dve.wait_ge(a_t[0], L * 4 * NT + q + 1)
                        if G >= 2 and q % 4 == 0:
                            dve.wait_ge(f_ready, L * NF + FI[("v", G - 2, 0)] + 1)
                        dve.tensor_copy(PT[G % 2][:, 0:4, (q % 4) * P:(q % 4 + 1) * P], quads(6)).then_inc(a_tev[0], 1)
                for u in range(2 * NT):
                    n, t = u // NT, u % NT
                    dve.wait_ge(wo_ready, L * 2 * NT + (2 * NT + u + 1))
                    hh = H[:, t, n * HALF:(n + 1) * HALF]
                    dve.tensor_tensor(hh, bank(u % 2), hh, ALU.add).then_inc(wo_evac, 1)
                nt_dve(dve, L * 2 + 3, vl[:, L_PLE:L_PLE + 8])
                for u in range(2 * NT):
                    n, t = u // NT, u % NT
                    dve.wait_ge(pg_sg, L * 2 * NT + u + 1)
                    if n == 1 and t >= 1:
                        dve.wait_ge(h_in, L * NT + NT + t)
                    dve.tensor_tensor(gp, sgp[:, u % 2, :], bank(2 + u % 2), ALU.mult).then_inc(pg_evac, 1)
                    dve.wait_ge(pg_evac, L * 2 * NT + u + 3)
                    hh = H[:, t, n * HALF:(n + 1) * HALF]
                    o = dve.tensor_tensor(hh, gp, hh, ALU.add)
                    if n == 0:
                        hc.link(o)
                    else:
                        o.then_inc(h_in, 1)
                assert PER is None or hc.n == PER, (hc.n, PER)
            layers(dve, layer)
            dve.wait_ge(f_rs, 1)
            dve.wait_ge(fg_in, 16)
            for t in range(NT):
                dve.scalar_tensor_tensor(out=HT[:, t, :], in0=H[:, t, :], scalar=rs[:, t:t + 1], in1=fgain, op0=ALU.mult, op1=ALU.mult).then_inc(f_out, 1)


def kernel(**inputs):
    import concourse.bacc as bacc
    from concourse.bass_utils import run_bass_kernel_spmd

    nc = bacc.Bacc("TRN2", target_bir_lowering=False, num_devices=1)
    arrays, A = {}, {}
    for name, a in list(inputs.items()) + [("kc", shape_constants())]:
        a = np.ascontiguousarray(a)
        arrays["in_" + name] = a
        A[name] = nc.dram_tensor("in_" + name, a.shape, mybir.dt.from_np(a.dtype), kind="ExternalInput").ap()
    out = nc.dram_tensor("out", (1, S, D), F32, kind="ExternalOutput").ap()
    program(nc, A, out)
    return run_bass_kernel_spmd(nc, [arrays], core_ids=[0]).results[0]["out"]
```

```python
from contextlib import ExitStack

import numpy as np
import concourse.bass as bass
from concourse import mybir

F32 = mybir.dt.float32
F32R = mybir.dt.float32r
I32 = mybir.dt.int32
U32 = mybir.dt.uint32
ALU = mybir.AluOpType
ACT = mybir.ActivationFunctionType
AX = mybir.AxisListType
ds = bass.ds

P = 128
S = 1024
D = 1024
NT = S // P
KD = D // P
HALF = 512
EPS = 1e-6

TAPS = 31
PADC = TAPS - 1
HEADS = 4
DH = 64
C_POOL0, C_Q, C_K, C_V = 512, 768, 1280, 1792
WINDOWS = (2, 4, 8, 16)
PADP = 16
LAM_INIT = 0.8 - 0.6 * np.exp(-0.3 * 0)
GROUPS, PER_GROUP, EXPERTS = 4, 4, 16
DE = 256
MTILES = EXPERTS + 2 * S // P - 1
NEG = -3.0e38

LAYERS = 2
C_CQ, C_CKV, C_KR, C_GA, C_GQ, C_GK, C_GV, C_LR, C_GG = 0, 384, 640, 704, 1216, 1472, 1728, 2240, 2272
CH = 64
NCH = S // CH
MLA_SCALE = float(np.float32(192) ** np.float32(-0.5))
PLE = 256

V_AG, V_FG, V_CB, V_LG, V_LB, V_PB, V_PS, V_QG, V_KG, V_SG, V_CW = 0, 8, 16, 18, 20, 22, 24, 26, 27, 28, 29
NV1 = V_CW + 2 * TAPS
L_MIX, L_PLE, L_QN, L_KVN, L_GB, L_GO = 0, 8, 16, 19, 21, 25
NV2 = 26
K_INV, K_OFF, K_RAD, K_SIGN, K_SLOPE, K_POOLW, K_POOL16 = 0, 1, 2, 3, 4, 8, 10
NK = K_POOL16 + 2 * 16


def shape_constants():
    c = np.zeros((P, NK), np.float32)
    p = np.arange(P)
    c[:, K_INV] = 10000.0 ** (-(p % 32) / 32.0)
    c[:, K_OFF] = np.where(p < 64, 0.25, 0.0)
    c[:, K_RAD] = np.where(p < 64, np.pi / 2, 0.0)
    c[:, K_SIGN] = np.where((p >= 64) & (p < 96), -1.0, 1.0)
    for h in range(HEADS):
        c[:, K_SLOPE + h] = (2.0 ** (-8.0 / HEADS)) ** (h + 1)
    for i in range(2):
        w = np.where(p < 64, WINDOWS[2 * i], WINDOWS[2 * i + 1])
        c[:, K_POOLW + i] = 1.0 / w
        c[:, K_POOL16 + 16 * i:K_POOL16 + 16 * i + 16] = 1.0 / np.minimum(np.arange(16)[None, :] + 1, w[:, None])
    return c



class Chain:

    def __init__(self, eng, semaphore, base=0):
        self.eng, self.semaphore, self.base, self.n = eng, semaphore, base, 0

    def link(self, ins):
        self.n += 1
        ins.then_inc(self.semaphore, 1)
        self.eng.wait_ge(self.semaphore, self.base + self.n)


def settle(eng, semaphore):
    eng.sem_inc(semaphore, 1)


def accumulate(pe, o, pairs):
    last = len(pairs) - 1
    for i, (l, r) in enumerate(pairs):
        mm = pe.matmul(o, l, r, start=(i == 0), stop=(i == last))
    return mm


def accumulate_split(pe, o, parts, before=None):
    last = len(parts) - 1
    for i, (lh, ll, rh, rl) in enumerate(parts):
        if before is not None:
            before(i)
        pe.matmul(o, lh, rh, start=(i == 0), stop=False)
        pe.matmul(o, lh, rl, start=False, stop=False)
        mm = pe.matmul(o, ll, rh, start=False, stop=(i == last))
    return mm


def program(nc, A, out):
    ctx = ExitStack()
    with ctx:
        def sb(name, shape, dt=F32):
            return ctx.enter_context(nc.sbuf_tensor(name, shape, dt))

        def sem(name):
            return ctx.enter_context(nc.semaphore(name))

        def sems(name, n):
            return [sem(f"{name}{i}") for i in range(n)]

        big = -(-nc.sbuf_base // 32) * 32
        H = sb("H", [P, NT, D])
        HT = sb("HT", [P, KD, S])
        MIX = sb("MIX", [P, KD, S])
        WF = sb("WF", [P, 4, KD, P])
        WT = sb("WT", [P, 2, KD, HALF])
        X = sb("X", [P, 10240])
        xn = sb("xn", [P, 2, D])
        assert nc.sbuf_base == big + 4 * (3 * KD * S + 4 * KD * P + 2 * KD * HALF + 10240 + 2 * D)
        row = 4 * KD * S
        HTr = nc.alloc_sbuf_tensor_at("HT_hi", [P, KD, S], F32R, offset=big + row)
        MIXr = nc.alloc_sbuf_tensor_at("MIX_lo", [P, KD, S], F32R, offset=big + 2 * row)
        WTr = nc.alloc_sbuf_tensor_at("WT_lo", [P, 2, KD, HALF], F32R, offset=big + 3 * row + 4 * 4 * KD * P)
        X_at = big + 3 * row + 4 * 4 * KD * P + 4 * 2 * KD * HALF
        WF_at, WT_at = big + 3 * row, big + 3 * row + 4 * 4 * KD * P
        WFr = nc.alloc_sbuf_tensor_at("WF_lo", [P, 4, KD, P], F32R, offset=WF_at)
        wb_hi = nc.alloc_sbuf_tensor_at("WB_hi", [P, 3, KD, P], F32R, offset=X_at)
        wc_hi = [nc.alloc_sbuf_tensor_at("WQ_hi", [P, KD, HALF], F32R, offset=X_at + 4 * 4 * S),
                 nc.alloc_sbuf_tensor_at("WK_hi", [P, KD, HALF], F32R, offset=WF_at), WTr[:, 1, :, :]]
        w_hi = [nc.alloc_sbuf_tensor_at(f"W_hi{i}", [P, KD, HALF], F32R, offset=X_at + 4 * KD * P * i) for i in (0, 6)]
        wu_hi = nc.alloc_sbuf_tensor_at("WU_hi", [P, 2, KD, P], F32R, offset=X_at + 4 * 9 * S)
        Hr = nc.alloc_sbuf_tensor_at("H_lo", [P, NT, KD, P], F32R, offset=big)
        w1_hi = [nc.alloc_sbuf_tensor_at("W1a_hi", [P, KD, HALF], F32R, offset=X_at), None]
        w1_hi[1] = (nc.alloc_sbuf_tensor_at("W1b_hi", [P, 6, HALF], F32R, offset=WF_at + 4 * KD * P),
                    nc.alloc_sbuf_tensor_at("W1c_hi", [P, 2, HALF], F32R, offset=X_at + 4 * 5 * S))
        ident = sb("ident", [P, P])
        ones = sb("ones", [P, P])
        vec1 = sb("vec1", [P, NV1])
        vec2 = sb("vec2", [P, LAYERS + 1, NV2])
        vl = sb("vl", [P, NV2])
        kc = sb("kc", [P, NK])
        eps = sb("eps", [P, 1])
        mhalf = sb("mhalf", [P, 8])
        ss = sb("ss", [P, 8])
        rs = sb("rs", [P, 8])
        stat = sb("stat", [P, 64])
        rope_w = sb("rope", [P, S + PADP])
        rope = rope_w[:, 0:S]
        shared = sb("shared", [P, 1280])
        small = sb("small", [P, 512])
        lamt = small[:, 0:4 * DH].rearrange("p (i d) -> p i d", i=4)
        pwb = small[:, 256:512].rearrange("p (c n) -> p c n", c=2)
        marks = sb("marks", [P, 48])
        ps = ctx.enter_context(nc.psum_tensor("ps", [P, 8, HALF], F32))
        psf = ps[:, :, :].rearrange("p b n -> p (b n)")

        def bank(b, n=HALF, at=0):
            return ps[:, b, at:at + n]

        def quads(b):
            return ps[:, b, :].rearrange("p (c n) -> p c n", n=P)

        xn_dram = nc.dram_tensor("xn_dram", (S, D), F32).ap()
        h_dram = nc.dram_tensor("h_dram", (S, D), F32).ap()
        y_dram = nc.dram_tensor("y_dram", (2 * S, D), F32).ap()
        slot_dram = nc.dram_tensor("slot_dram", (MTILES * P, 4), I32).ap()

        Hf = H[:, :, :].rearrange("p t d -> p (t d)")
        HTf = HT[:, :, :].rearrange("p k t -> p (k t)")
        MXf = MIX[:, :, :].rearrange("p k t -> p (k t)")
        WTf = WT[:, :, :, :].rearrange("p s k n -> p (s k n)")
        WFf = WF[:, :, :, :].rearrange("p s k n -> p (s k n)")

        def slot(flat, i, n=1):
            return flat[:, i * S:(i + n) * S]

        u_pad = Hf[:, 0:2108].rearrange("p (c t) -> p c t", c=2)
        y_cv = Hf[:, 2108:4156].rearrange("p (c t) -> p c t", c=2)
        sq_cv = Hf[:, 0:2048].rearrange("p (c t) -> p c t", c=2)
        sig_g = Hf[:, 2108:4156].rearrange("p (c t) -> p c t", c=2)
        p_pad = Hf[:, 4156:6236].rearrange("p (c t) -> p c t", c=2)
        wA = Hf[:, 6236:7276]
        fix16 = Hf[:, 7276:7292]
        wB = rope_w[:, 0:S + PADP]
        r_cv = MXf[:, 0:1024]
        qT = X[:, 0:4096].rearrange("p (h t) -> p h t", h=4)
        kT = X[:, 4096:8192].rearrange("p (h t) -> p h t", h=4)
        qtok = X[:, 8192:9216].rearrange("p (b n) -> p b n", b=2)
        qn = X[:, 9216:10240].rearrange("p (b n) -> p b n", b=2)
        V1 = WFf.rearrange("p (t n) -> p t n", t=NT)
        qz = [[X[:, 8192:9216], X[:, 9216:10240]], [rope[:, :], xn[:, 1, :]]]
        sS = [[slot(HTf, i) for i in range(3)], [slot(HTf, i) for i in (3, 4)]]
        ATb = slot(HTf, 5, 2).rearrange("p (b k q) -> p b k q", b=2, k=8)
        BH = slot(HTf, 7)
        on = xn[:, 0, 0:384].rearrange("p (b q) -> p b q", b=3)
        osq = xn[:, 0, 384:512]
        ORDER = [b for i in range(NT // 2) for b in (NT - 1 - i, i)]
        BLOCKS = [(h, b) for h in range(HEADS) for b in ORDER]
        NB = len(BLOCKS)
        TURNS = [sum(b // 4 + 1 for _, b in BLOCKS[:g]) for g in range(NB + 1)]
        qsum = stat[:, 0:16].rearrange("p (b g) -> p b g", b=2)
        qrs = stat[:, 16:32].rearrange("p (b g) -> p b g", b=2)
        lam4 = stat[:, 32:40]
        sm = sb("sm", [P, 4, 16])
        cpw = xn[:, 0, 512:1024].rearrange("p (k n) -> p k n", k=2)
        lgT = X[:, 0:1024]
        rb = X[:, 1024:1044]
        R0 = 1056

        def rbuf(at, *shape):
            n = int(np.prod(shape))
            v = X[:, R0 + at:R0 + at + n]
            if len(shape) == 2:
                v = v.rearrange("p (a b) -> p a b", a=shape[0])
            if len(shape) == 3:
                v = v.rearrange("p (a b c) -> p a b c", a=shape[0], b=shape[1])
            return v
        lg = rbuf(0, NT, 20)
        first4 = rbuf(160, 4)
        g_max, g_sum, g_p, m1, v1, v2, w1, w2, den, pos1, pos2 = (rbuf(176 + 8 * i, NT) for i in range(11))
        ge, geq, oh, le, leq, oh1, oh2, pe2 = (rbuf(272 + 32 * i, NT, 4) for i in range(8))
        lsel = rbuf(544, NT, 4, 4)
        S1, S2, MM = rbuf(672, NT, 16), rbuf(800, NT, 16), rbuf(928, NT, 16)
        posn, toff, tmpe = rbuf(1056, NT, 16), rbuf(1184, NT, 16), rbuf(1312, NT, 16)
        cnt, tiles_f, tend, tbase, one16 = (rbuf(1440 + 16 * i, 16) for i in range(5))
        tiles_i = rbuf(1520, 16).bitcast(I32)
        cmpt = rbuf(1552, MTILES + 1, 16)
        iot = rbuf(2064, MTILES + 1)
        et_f = rbuf(2096, MTILES + 1)
        et_i = rbuf(2128, MTILES + 1).bitcast(I32)
        rows = rbuf(2160, NT, 2, 4).bitcast(I32)
        rows_f = rbuf(2160, NT, 2, 4)
        sidx = rbuf(2224, NT, 2).bitcast(I32)
        initrow = rbuf(2240, MTILES, 4).bitcast(I32)
        initrow_f = rbuf(2240, MTILES, 4)
        tri = rbuf(2368, P)
        tokid = rbuf(2496, NT)
        tabs = rbuf(2512, MTILES, 4).bitcast(I32)
        tabs_f = rbuf(2512, MTILES, 4)
        tok_of = rbuf(2512 + 4 * MTILES, 2, 2).bitcast(I32)
        dst_of = rbuf(2512 + 4 * MTILES + 4, 2, 2).bitcast(I32)
        M0 = R0 + 2512 + 4 * MTILES + 12
        sgb = X[:, M0:M0 + 512].rearrange("p (b n) -> p b n", b=2)
        actb = X[:, M0 + 512:M0 + 1024].rearrange("p (b n) -> p b n", b=2)
        actT = X[:, M0 + 1024:M0 + 1536].rearrange("p (b k n) -> p b k n", b=2, k=2)
        yb = X[:, M0 + 1536:M0 + 3584].rearrange("p (b n) -> p b n", b=2)
        wd = MXf[:, 0:4096].rearrange("p (b k n) -> p b k n", b=2, k=2)
        hg = MXf[:, 4096:6144].rearrange("p (b n) -> p b n", b=2)
        hgT = MXf[:, 6144:8192].rearrange("p (b k n) -> p b k n", b=2, k=KD)

        q_dup = [slot(X, 0), slot(X, 1)]
        k_dup = [slot(X, 2), slot(X, 3)]
        cum, la, gt, q_in, sqg = (slot(X, i) for i in range(4, 9))
        wgs = small[:, :].rearrange("p (h n) -> p h n", h=4)
        refs, lasts, decay = (marks[:, 16 * i:16 * i + 16] for i in range(3))
        kf, kb = slot(WTf, 0), slot(WTf, 1)
        q_even, q_odd = slot(WTf, 2), slot(WTf, 3)
        kv = slot(WTf, 4, 2).rearrange("p (c v) -> p c v", c=NCH)
        st = slot(WTf, 6, 2).rearrange("p (c v) -> p c v", c=NCH)
        ks_even, ks_odd, Af, Ab = (MIX[:, i, :] for i in range(4))
        Hlo = Hr[:, :, :, :].rearrange("p t k n -> p t (k n)")
        kr_hi, kr_lo = Hlo[:, 3, :], Hlo[:, 7, :]
        gv = [slot(WFf, 2), slot(WFf, 3)]
        lrz = xn[:, 1, :]
        reset = shared[:, 0:S]
        mask_f, mask_b = shared[:, S:S + P], shared[:, S + P:S + 2 * P]
        y_tok = [[slot(X, t) for t in range(NT)], [slot(WTf, t) for t in range(NT)]]
        c_q = [slot(X, i) for i in range(3)]
        c_kv = [slot(X, 3), slot(X, 4)]
        kr = slot(X, 5)
        sq_q = [slot(X, 6), slot(X, 7), slot(WTf, 0)]
        sq_kv = [xn[:, 1, :], slot(X, 8)]
        r_q, r_kv = slot(WTf, 4), slot(X, 6)
        PT = [WTf[:, 4 * S:8 * S].rearrange("p (k q) -> p k q", k=KD), X[:, 6 * S:10 * S].rearrange("p (k q) -> p k q", k=KD)]
        uq = [WFf[:, o:o + 768].rearrange("p (k n) -> p k n", k=3) for o in (2048, 0)]
        ukv = [WFf[:, o + 768:o + 1280].rearrange("p (k n) -> p k n", k=2) for o in (2048, 0)]
        rtmp = WFf[0:64, 1280:1792]
        p_tok = slot(WFf, 0, 2).rearrange("p (t c) -> p t c", t=NT)
        wpp = slot(WFf, 2, 2).rearrange("p (c n) -> p c n", c=2)
        pT = slot(X, 4, 2).rearrange("p (c t) -> p c t", c=2)
        sgp = slot(WFf, 0).rearrange("p (b n) -> p b n", b=2)
        fgain = rope[:, :]
        krr = slot(X, 8)
        kr0 = xn[64:P, 1, :]
        pos_i = X[:, 7 * S:8 * S].bitcast(I32)
        ang, turns = slot(X, 8), slot(X, 9)

        UNITS = [("kl", 0, C_KR, 96)]
        for pair in range(2):
            UNITS += [("gq", pair, C_GQ + pair * P, P), ("gk", pair, C_GK + pair * P, P)]
            for h in (2 * pair, 2 * pair + 1):
                UNITS += [("gv", h, C_GV + h * P, P), ("gg", h, C_GG + h * P, P)]
        UNITS += [("cq", i, C_CQ + i * P, P) for i in range(3)] + [("ckv", i, C_CKV + i * P, P) for i in range(2)]
        UNITS += [("ga", i, C_GA + i * P, P) for i in range(4)]
        NU = len(UNITS)
        UI = {(k, i): u for u, (k, i, _, _) in enumerate(UNITS)}
        W_DMAS = [2 if k == "kl" else 1 for k, _, _, _ in UNITS]
        W_SOFAR = [sum(W_DMAS[v] for v in range(u % 2, u + 1, 2)) for u in range(NU)]
        W_LAYER = [sum(W_DMAS[s::2]) for s in range(2)]
        FILLS = [("p", 0, j) for j in range(8)]
        STEPS = 4 * NT + 2
        for g in range(STEPS):
            if g // NT + 1 < 4 and g < 4 * NT:
                FILLS.append(("p", g // NT + 1, g % NT))
            if g >= 5 and (g - 2) % 4 == 3:
                FILLS.append(("v", (g - 2) // 4, 0))
        NF = len(FILLS)
        FI = {f: i for i, f in enumerate(FILLS)}

        x_in = sems("x_in", NT)
        const_in, ag_in, idready = sem("const_in"), sem("ag_in"), sem("idready")
        n_ss, n_rs, n_xn = sem("n_ss"), sem("n_rs"), sem("n_xn")
        n_tp, n_ht = sem("n_tp"), sem("n_ht")
        pool_chain, dve_chain, act_chain = sem("pool_chain"), sem("dve_chain"), sem("act_chain")
        b_w, b_ready, b_evac = sems("b_w", 3), sem("b_ready"), sems("b_evac", 2)
        p_ready = sem("p_ready")
        c_w, c_ready, c_evac = sems("c_w", 2), sem("c_ready"), sem("c_evac")
        c_red, c_rs, c_qn, c_tp, c_tev = (sem(n) for n in ("c_red", "c_rs", "c_qn", "c_tp", "c_tev"))
        cv_dve, pool_d = sem("cv_dve"), sem("pool_d")
        pl_ready, pl_evac = sem("pl_ready"), sem("pl_evac")
        ln_pe, ln_dve, ln_act = sem("ln_pe"), sem("ln_dve"), sem("ln_act")
        pw_ready, pw_evac = sem("pw_ready"), sem("pw_evac")
        lam_e, padded = sem("lam_e"), sem("padded")
        pw_in = sem("pw_in")
        qz_ready, s_ready, s_max, s_neg, e_ready, a_ready, t_ready, at_evac, o_ready, o_cp, o_n, ot_ready, ot_evac, qz_zero = (
            sem(n) for n in ("qz_ready", "s_ready", "s_max", "s_neg", "e_ready", "a_ready", "t_ready", "at_evac",
                             "o_ready", "o_cp", "o_n", "ot_ready", "ot_evac", "qz_zero"))
        wo_w, wo_ready, wo_evac = sems("wo_w", 2), sem("wo_ready"), sem("wo_evac")
        xn_st = sems("xn_st", 2)
        rw_zero, rw_in, rt_ready, rt_cp, rt_tp = (
            sem(n) for n in ("rw_zero", "rw_in", "rt_ready", "rt_cp", "rt_tp"))
        rx, rx_done, rm_ready, rp_ready, slots_set, slots_init, slots_in, experts_set = (
            sem(n) for n in ("rx", "rx_done", "rm_ready", "rp_ready", "slots_set", "slots_init", "slots_in", "experts_set"))
        iotas = sem("iotas")
        m_wgu, m_wd, m_hg, m_sc = (sems(n, 2) for n in ("m_wgu", "m_wd", "m_hg", "m_sc"))
        m_tab, m_tok, m_dst = sem("m_tab"), sem("m_tok"), sem("m_dst")
        m_xt, m_ht, m_gu, m_sg, m_act, m_at, m_aT, m_dn, m_y = (
            sem(n) for n in ("m_xt", "m_ht", "m_gu", "m_sg", "m_act", "m_at", "m_aT", "m_dn", "m_y"))
        h_in = sem("h_in")
        comb = sem("comb")
        v2_in, vl_ready, row_in, rope_set = (
            sem(n) for n in ("v2_in", "vl_ready", "row_in", "rope_set"))
        z_ready, lz_ready, hz_ready, wg_in, kr_done = (sem(n) for n in ("z_ready", "lz_ready", "hz_ready", "wg_in", "kr_done"))
        uh_ready, ul_ready = sem("uh_ready"), sem("ul_ready")
        v_tp, v_ev = sem("v_tp"), sem("v_ev")
        h_st, fh_ready = sems("h_st", 2), sem("fh_ready")
        u_w, u_ready, u_evac = sems("u_w", 2), sem("u_ready"), sems("u_evac", 2)
        g_pe, g_act, g_dve = sem("g_pe"), sem("g_act"), sem("g_dve")
        GLA_STEPS = {g_pe: [("z", 0)], g_act: [("t", 0), ("e", 0)], g_dve: [("d", 0), ("k", 0), ("q", 0)]}
        for h in range(4):
            more = h < 3
            GLA_STEPS[g_pe] += [("a", h), ("kt", h), ("kv", h)] + [("z", h + 1)] * more + [("o", h), ("ms", h)]
            GLA_STEPS[g_act] += [("ks", h), ("kvc", h)] + [("t", h + 1), ("e", h + 1)] * more + [("sq", h), ("r", h)]
            GLA_STEPS[g_dve] += [("am", h), ("st", h)] + [("d", h + 1), ("k", h + 1), ("q", h + 1)] * more + [("done", h)]
        GLA_AT = {step: (s, i) for s, steps in GLA_STEPS.items() for i, step in enumerate(steps)}

        def gla(L, step, h):
            s, i = GLA_AT[(step, h)]
            return s, L * len(GLA_STEPS[s]) + i + 1

        l_ms, l_r, l_c = sem("l_ms"), sem("l_r"), sem("l_c")
        wh_ready, wl_ready, mx_hi, mx_lo = sem("wh_ready"), sem("wl_ready"), sem("mx_hi"), sem("mx_lo")
        uw, f_ready, f_evac = sems("uw", 2), sem("f_ready"), sems("f_evac", 2)
        a_s, a_neg, a_e, a_p, a_t, a_tev = sem("a_s"), sem("a_neg"), sem("a_e"), sem("a_p"), sems("a_t", 2), sems("a_tev", 2)
        p_in, p_tp, p_ev, pg_ready, pg_sg, pg_evac = sem("p_in"), sem("p_tp"), sem("p_ev"), sem("pg_ready"), sem("pg_sg"), sem("pg_evac")
        f_out, out_st = sem("f_out"), sem("out_st")


        settled = sem("settled")

        block = ctx.enter_context(nc.Block())

        def nt_act(act, N, t, ready, stored=None, squares=None, scale=True):
            if t < NT:
                act.wait_ge(*ready(t))
                if squares is None:
                    act.wait_ge(n_tp, N * NT + (t + 1))
                elif t >= 1:
                    act.wait_ge(n_ss, N * NT + t)
                act.activation(xn[:, t % 2, :] if squares is None else squares, H[:, t, :], ACT.Square, accum_out=ss[:, t:t + 1]).then_inc(n_ss, 1)
            if t >= 1 and scale:
                act.wait_ge(n_rs, N * NT + t)
                act.wait_ge(n_tp, N * NT + t)
                if stored is not None:
                    act.wait_ge(stored[(t - 1) % 2], 16 * ((t - 1) // 2) + 16)
                act.activation(xn[:, (t - 1) % 2, :], H[:, t - 1, :], ACT.Copy, scale=rs[:, t - 1:t]).then_inc(n_xn, 1)

        def nt_pool(pool, chain, N, scale=False):
            for t in range(NT):
                pool.wait_ge(n_ss, N * NT + (t + 1))
                settle(pool, settled)
                chain.link(pool.tensor_scalar(ss[:, t:t + 1], ss[:, t:t + 1], 1.0 / D, EPS, ALU.mult, ALU.add))
                pool.tensor_tensor(rs[:, t:t + 1], ss[:, t:t + 1], mhalf[:, 0:1], ALU.pow).then_inc(n_rs, 1)
                if scale:
                    pool.wait_ge(n_rs, N * NT + t + 1)
                    pool.wait_ge(n_tp, N * NT + t + 1)
                    pool.tensor_scalar(xn[:, t % 2, :], H[:, t, :], rs[:, t:t + 1], None, ALU.mult).then_inc(n_xn, 1)

        def nt_pe(pe, N, t):
            pe.wait_ge(n_xn, N * NT + (t + 1))
            pe.wait_ge(n_ht, N * NT + (t + 1))
            for c in range(KD):
                tp = pe.transpose(bank(2 + 2 * (t % 2) + c // 4, P, (c % 4) * P), xn[:, t % 2, c * P:(c + 1) * P], ident[:, :])
            tp.then_inc(n_tp, 1)

        def nt_dve(dve, N, t, gain, to=HT):
            dve.wait_ge(n_tp, N * NT + (t + 3))
            for c in range(2):
                g = gain[:, 4 * c:4 * c + 4].unsqueeze(2).to_broadcast([P, 4, P])
                o = dve.tensor_tensor(to[:, 4 * c:4 * c + 4, t * P:(t + 1) * P], quads(2 + 2 * (t % 2) + c), g, ALU.mult)
            o.then_inc(n_ht, 1)

        def ht_ready(N, tiles=NT):
            return N * NT + (2 + tiles)

        W_O = 6 + 3 * KD
        W_1 = W_O + 2 * KD

        def part_hi(act, to, of):
            act.activation(to, of, ACT.Copy).then_inc(wh_ready, 1)

        def part_lo(dve, i, to, of, hi):
            dve.wait_ge(wh_ready, i + 1)
            dve.tensor_tensor(to, of, hi.bitcast(F32), ALU.subtract).then_inc(wl_ready, 1)

        def b_hi(act, u):
            act.wait_ge(b_w[u % 3], 16 * (u // 3 + 1))
            part_hi(act, wb_hi[:, u % 3, :, :], WF[:, u % 3, :, :])

        def b_lo(dve, u):
            part_lo(dve, u, WFr[:, u % 3, :, :], WF[:, u % 3, :, :], wb_hi[:, u % 3, :, :])

        def c_hi(act, b, k):
            if k == 0:
                act.wait_ge(c_w[b % 2], 16 * (b // 2 + 1))
                if b == 1:
                    act.wait_ge(b_ready, 12)
                if b == 2:
                    act.wait_ge(c_ready, 2 * NT)
            part_hi(act, wc_hi[b][:, k, :], WT[:, b % 2, k, :])

        def c_lo(dve, b, k):
            part_lo(dve, 6 + b * KD + k, WTr[:, b % 2, k, :], WT[:, b % 2, k, :], wc_hi[b][:, k, :])

        def ht_hi(act, t):
            act.wait_ge(n_ht, ht_ready(0, t + 1))
            ts = slice(t * P, (t + 1) * P)
            act.activation(HTr[:, :, ts], MIX[:, :, ts], ACT.Copy).then_inc(mx_hi, 1)

        def ht_lo(dve, t):
            dve.wait_ge(mx_hi, t + 1)
            ts = slice(t * P, (t + 1) * P)
            dve.tensor_tensor(MIXr[:, :, ts], MIX[:, :, ts], HTr[:, :, ts].bitcast(F32), ALU.subtract).then_inc(mx_lo, 1)

        def out_hi(n, k):
            if n == 0:
                return w1_hi[0][:, k, :]
            return w1_hi[1][0][:, k, :] if k < 6 else w1_hi[1][1][:, k - 6, :]

        def o_hi(act, n, k):
            if k == 0:
                act.wait_ge(wo_w[n], 16)
                if n == 0:
                    act.wait_ge(qz_ready, HEADS)
            part_hi(act, out_hi(n, k), WT[:, n, k, :])

        def o_lo(dve, n, k):
            part_lo(dve, W_O + n * KD + k, WTr[:, n, k, :], WT[:, n, k, :], out_hi(n, k))

        def mix1_hi(act, t):
            ts = slice(t * P, (t + 1) * P)
            act.activation(HTr[:, :, ts], MIX[:, :, ts], ACT.Copy).then_inc(mx_hi, 1)

        def mix1_lo(dve, t):
            dve.wait_ge(mx_hi, NT + t + 1)
            ts = slice(t * P, (t + 1) * P)
            dve.tensor_tensor(MIXr[:, :, ts], MIX[:, :, ts], HTr[:, :, ts].bitcast(F32), ALU.subtract).then_inc(mx_lo, 1)

        def experts(eng, step):
            for o in range(3):
                step(0, o)
            with eng.Fori(1, (MTILES - 5) // 2) as i:
                for o in (1, 2):
                    step(i, o)
            for o in range(MTILES - 4, MTILES + 1):
                step(0, o)

        def has(i, o):
            return not isinstance(i, int) or 0 <= 2 * i + o < MTILES

        def wait_past(eng, semaphore, value):
            if not isinstance(value, int) or value > 0:
                eng.wait_ge(semaphore, value)

        def layers(eng, layer):
            with eng.Fori(0, LAYERS) as L:
                layer(L)

        def unit_evac(L, u, half):
            return L * NU + (u + 2)

        def mx_at(L, j, t):
            return L * 3 * NT + (2 * NT + j * NT + t + 1)

        def fill_evac(L, f):
            return L * (NF // 2) + (f // 2 + 2)

        @block.sync
        def _(sp):
            for p in range(2):
                sp.sem_inc(xn_st[p], 16)
            for t in range(NT):
                sp.dma_start(H[:, t, :], A["x"][0, t * P:(t + 1) * P, :]).then_inc(x_in[t], 16)
            def vec(dst, src):
                sp.dma_start(dst, src).then_inc(const_in, 16)
            for u in range(6):
                c, kind = u // 3, u % 3
                if u == 3:
                    with nc.allow_non_contiguous_dma(reason="gains and biases, one value a partition"):
                        for at, n, name in ((V_FG, 8, "ffn_norm_g"), (V_CB, 2, "conv_b"), (V_LG, 2, "conv_ln_g"),
                                            (V_LB, 2, "conv_ln_b"), (V_PB, 2, "conv_pw_b"), (V_PS, 2, "pool_scale"), (V_SG, 1, "attn_sub_norm_g")):
                            vec(vec1[:, at:at + n], A[name][0].rearrange("(c p) -> p c", p=P))
                        vec(kc[:, :], A["kc"])
                        for m in range(2):
                            vec(vec1[64 * m:64 * m + 64, V_QG:V_QG + 1], A["q_norm_g"][0].rearrange("(p c) -> p c", c=1))
                            vec(vec1[64 * m:64 * m + 64, V_KG:V_KG + 1], A["k_norm_g"][0].rearrange("(p c) -> p c", c=1))
                        for c in range(2):
                            vec(vec1[:, V_CW + TAPS * c:V_CW + TAPS * (c + 1)], A["conv_w"][0, :, c * P:(c + 1) * P].rearrange("j p -> p j"))
                        for i, name in enumerate(("lambda_q1", "lambda_k1", "lambda_q2", "lambda_k2")):
                            vec(lamt[:, i, :], A[name][0:1, :].to_broadcast([P, DH]))
                        sp.wait_ge(padded, 1)
                        for g in range(4):
                            r = slice(64 * (g % 2), 64 * (g % 2) + 64)
                            sp.dma_start(pwb[r, g // 2, r], A["pool_w"][0, g]).then_inc(pw_in, 16)
                c0 = (256, 0, C_POOL0)[kind] + c * P
                if u >= 3:
                    sp.wait_ge(b_ready, 2 * (u - 3) + 2)
                sp.dma_start(WF[:, kind, :, :], A["w_in"][0, :, c0:c0 + P].rearrange("(k p) c -> p k c", p=P)).then_inc(b_w[kind], 16)
            for b in range(3):
                if b == 2:
                    sp.wait_ge(c_ready, NT)
                sp.dma_start(WT[:, b % 2, :, :], A["w_in"][0, :, C_Q + b * HALF:C_Q + (b + 1) * HALF]
                             .rearrange("(k p) c -> p k c", p=P)).then_inc(c_w[b % 2], 16)
                if b == 1:
                    sp.wait_ge(b_ready, 2)
                    sp.dma_start(cpw, A["conv_pw_w"][0].rearrange("(k p) n -> p k n", p=P)).then_inc(pw_in, 16)
            for n in (1, 0):
                sp.wait_ge(c_ready, 3 * NT)
                sp.dma_start(WT[:, n, :, :], A["w_out"][0, :, n * HALF:(n + 1) * HALF].rearrange("(k p) c -> p k c", p=P)).then_inc(wo_w[n], 16)
            sp.wait_ge(pw_ready, 4)
            sp.wait_ge(pl_ready, 4)
            for t in range(NT):
                sp.dma_start(H[:, t, :], A["x"][0, t * P:(t + 1) * P, :]).then_inc(x_in[t], 16)
            sp.wait_ge(o_ready, HEADS * NT)
            sp.wait_ge(ot_evac, HEADS * NT)
            sp.dma_start(pos_i, A["positions_2"][0:1, :].to_broadcast([P, S])).then_inc(row_in, 16)
            with nc.allow_non_contiguous_dma(reason="gains and biases, one value a partition"):
                for l in range(LAYERS):
                    for at, n, name in ((L_MIX, 8, "ln_mix_2"), (L_PLE, 8, "ple_norm_2"), (L_QN, 3, "mla_q_norm_2"),
                                        (L_KVN, 2, "mla_kv_norm_2"), (L_GO, 1, "gla_out_norm_2")):
                        sp.dma_start(vec2[:, l, at:at + n], A[name][l].rearrange("(c p) -> p c", p=P)).then_inc(v2_in, 16)
                    for r, name in ((slice(0, 64), "gla_b_gate_fwd_2"), (slice(64, P), "gla_b_gate_bwd_2")):
                        sp.dma_start(vec2[r, l, L_GB:L_GB + 4], A[name][l].rearrange("(h p) -> p h", h=4)).then_inc(v2_in, 16)
            sp.wait_ge(wo_ready, NT)
            sp.dma_start(rb[:, 0:4], A["router_g_b"][0:1, :].to_broadcast([P, 4])).then_inc(rw_in, 16)
            sp.dma_start(rb[:, 4:20], A["router_e_b"][0:1, :].to_broadcast([P, 16])).then_inc(rw_in, 16)
            sp.wait_ge(rw_zero, 1)
            sp.dma_start(WF[:, 0, :, 0:4], A["router_g_w"][0].rearrange("(k p) c -> p k c", p=P)).then_inc(rw_in, 16)
            sp.dma_start(WF[:, 0, :, 4:20], A["router_e_w"][0].rearrange("(k p) c -> p k c", p=P)).then_inc(rw_in, 16)
            with sp.Fori(0, NT // 2) as i:
                for p in range(2):
                    sp.wait_ge(n_xn, i * 2 + (NT + p + 1))
                    sp.dma_start(xn_dram[ds((i * 2 + p) * P, P), :], xn[:, p, :]).then_inc(xn_st[p], 16)
            sp.wait_ge(slots_init, 1)
            sp.dma_start(slot_dram.rearrange("(a p) c -> p a c", p=P), initrow).then_inc(slots_in, 16)
            sp.wait_ge(experts_set, 1)
            sp.wait_ge(wo_ready, 2 * NT)

            def expert(i, o):
                return sp.value_load(et_i[0:1, ds(i * 2 + o, 1)], min_val=0, max_val=EXPERTS - 1)

            def load_gu(i, o):
                e, p = expert(i, o), o % 2
                wait_past(sp, m_gu, i * 2 + (o - 1))
                sp.dma_start(WT[:, p, :, 0:DE], A["w_gate"][0, ds(e, 1)].rearrange("a (k p) c -> p (a k) c", p=P)).then_inc(m_wgu[p], 16)
                sp.dma_start(WT[:, p, :, DE:2 * DE], A["w_up"][0, ds(e, 1)].rearrange("a (k p) c -> p (a k) c", p=P)).then_inc(m_wgu[p], 16)

            def load_d(i, o):
                e, p = expert(i, o), o % 2
                wait_past(sp, m_dn, i * 2 + (o - 1))
                sp.dma_start(wd[:, p, :, :], A["w_down"][0, ds(e, 1)].rearrange("a (k p) c -> p (a k) c", p=P)).then_inc(m_wd[p], 16)

            def expert_sp(i, o):
                if has(i, o + 2):
                    load_gu(i, o + 2)
                if has(i, o + 1) and o != 0:
                    load_d(i, o + 1)
            for o in range(2):
                load_gu(0, o)
                load_d(0, o)
            sp.wait_ge(slots_set, 16 * 2 * NT)
            sp.dma_start(tabs, slot_dram.rearrange("(a p) c -> p a c", p=P)).then_inc(m_tab, 16)
            experts(sp, expert_sp)
            sp.wait_ge(m_sc[0], 16 * (MTILES // 2 + 1))
            sp.wait_ge(m_sc[1], 16 * (MTILES // 2))
            sp.wait_ge(m_dn, MTILES)
            for t in range(NT):
                for k in range(2):
                    sp.dma_start(y_tok[k][t], y_dram[k * S + t * P:k * S + (t + 1) * P, :]).then_inc(x_in[t], 16)

            def layer(L):
                win = A["w_in_2"][ds(L, 1)].rearrange("a (k p) c -> p (a k) c", p=P)

                def up_weights(h):
                    s = h % 2
                    wq = A["w_uq_2"][ds(L, 1)].rearrange("a (k p) c -> p (a k) c", p=P)
                    sp.dma_start(uq[s][:, :, 0:192], wq[:, :, h * 192:h * 192 + 192]).then_inc(uw[s], 16)
                    sp.dma_start(uq[s][:, :, 192:224], wq[:, :, h * 192 + 160:h * 192 + 192]).then_inc(uw[s], 16)
                    sp.dma_start(uq[s][:, :, 224:256], wq[:, :, h * 192 + 128:h * 192 + 160]).then_inc(uw[s], 16)
                    sp.dma_start(ukv[s], A["w_ukv_2"][ds(L, 1), :, h * 256:h * 256 + 256].rearrange("a (k p) c -> p (a k) c", p=P)).then_inc(uw[s], 16)
                for u, (kind, i, c0, n) in enumerate(UNITS):
                    if u >= 2:
                        sp.wait_ge(u_ready, L * 2 * NU + 2 * (u - 1))
                        settle(sp, settled)
                    if u == 1:
                        for t in range(NT):
                            sp.wait_ge(h_in, L * NT + (t + 1))
                            settle(sp, settled)
                            sp.dma_start(h_dram[t * P:(t + 1) * P, :], H[:, t, :]).then_inc(h_st[2 * t // NT], 16)
                        sp.wait_ge(h_in, L * NT + NT)
                        settle(sp, settled)
                    if (kind, i) == ("ga", 0):
                        up_weights(0)
                    if kind == "kl":
                        for to, c, m in ((0, C_KR, 64), (64, C_LR, 32)):
                            sp.dma_start(WF[:, 1 - u % 2, :, to:to + m], win[:, :, c:c + m]).then_inc(u_w[u % 2], 16)
                    else:
                        sp.dma_start(WF[:, 1 - u % 2, :, 0:n], win[:, :, c0:c0 + n]).then_inc(u_w[u % 2], 16)
                    if u == 1:
                        sp.wait_ge(z_ready, L * 5 + 1)
                        for r, name in ((0, "gla_w_gate_fwd_2"), (1, "gla_w_gate_bwd_2")):
                            sp.dma_start(wgs[16 * r:16 * r + 16, :, 64 * r:64 * r + 64],
                                         A[name][ds(L, 1)].rearrange("a r (h d) -> r (a h) d", h=4)).then_inc(wg_in, 16)
                sp.dma_start(WT[:, 0, :, :], A["w_out_2"][ds(L, 1), :, 0:HALF].rearrange("a (k p) c -> p (a k) c", p=P)).then_inc(wo_w[0], 16)
                sp.wait_ge(u_ready, L * 2 * NU + 2 * NU)
                up_weights(1)
                for h in (2, 3):
                    sp.wait_ge(f_ready, L * NF + FI[("p", h - 2, 7)] + 1)
                    up_weights(h)
                sp.wait_ge(f_ready, L * NF + FI[("v", 6, 0)] + 1)
                sp.dma_start(WT[:, 1, :, :], A["w_out_2"][ds(L, 1), :, HALF:D].rearrange("a (k p) c -> p (a k) c", p=P)).then_inc(wo_w[1], 16)
                sp.wait_ge(a_s, L * 4 * NT + 4 * NT)
                for half in range(2):
                    sp.wait_ge(h_st[half], L * 64 + 64)
                settle(sp, settled)
                for t in range(NT):
                    sp.dma_start(H[:, t, :], h_dram[t * P:(t + 1) * P, :]).then_inc(x_in[t], 16)
                sp.wait_ge(f_ready, L * NF + NF)
                sp.dma_start(p_tok, A["p_2"][ds(L, 1), 0].rearrange("a (t p) c -> p (a t) c", p=P)).then_inc(p_in, 16)
                sp.dma_start(wpp, A["w_ple_proj_2"][ds(L, 1)].rearrange("a (k p) c -> p (a k) c", p=P)).then_inc(p_in, 16)
                for n in range(2):
                    sp.wait_ge(wo_ready, L * 2 * NT + (n + 3) * NT)
                    sp.dma_start(WT[:, n, :, :], A["w_ple_gate_2"][ds(L, 1), :, n * HALF:(n + 1) * HALF]
                                 .rearrange("a (k p) c -> p (a k) c", p=P)).then_inc(wo_w[n], 16)
            layers(sp, layer)
            sp.dma_start(fgain, A["final_norm_2"].rearrange("(a d) -> a d", a=1).to_broadcast([P, D])).then_inc(row_in, 16)
            for t in range(NT):
                sp.wait_ge(f_out, t + 1)
                sp.dma_start(out[0, t * P:(t + 1) * P, :], HT[:, t, :]).then_inc(out_st, 16)
            sp.wait_ge(out_st, 16 * NT)

        @block.gpsimd
        def _(pool):
            chain = Chain(pool, pool_chain)
            chain.link(pool.memset(ident[:, :], 0.0))
            pool.affine_select(out=ident[:, :], in_=ident[:, :], pattern=[[-1, P]], compare_op=ALU.not_equal, fill=1.0,
                               base=0, channel_multiplier=1).then_inc(idready, 1)
            pool.memset(ones[:, :], 1.0).then_inc(idready, 1)
            pool.memset(mhalf[:, :], -0.5)
            pool.memset(eps[:, :], EPS).then_inc(idready, 1)
            pool.memset(vec2[:, LAYERS, :], 0.0)
            pool.memset(pwb[:, :, :], 0.0).then_inc(padded, 1)
            chain.link(pool.iota(shared[:, 0:S], pattern=[[1, S]], base=-(S - P), channel_multiplier=-1, allow_small_or_imprecise_dtypes=True))
            pool.affine_select(out=shared[:, 0:S], in_=shared[:, 0:S], pattern=[[-1, S]], compare_op=ALU.is_ge, fill=NEG,
                               base=S - P, channel_multiplier=1).then_inc(idready, 1)
            nt_pool(pool, chain, 0, scale=True)

            for n in range(2 * NT):
                pool.wait_ge(c_red, n + 1)
                if n >= 2:
                    pool.wait_ge(c_qn, n - 1)
                chain.link(pool.tensor_scalar(qsum[:, n % 2, :], qsum[:, n % 2, :], 1.0 / DH, EPS, ALU.mult, ALU.add))
                pool.tensor_tensor(qrs[:, n % 2, :], qsum[:, n % 2, :], mhalf[:, :], ALU.pow).then_inc(c_rs, 1)
            pool.wait_ge(p_ready, 4)
            W0 = S + PADP
            for c in range(2):
                pp = p_pad[:, c, :]
                chain.link(pool.tensor_tensor(wA[:, 1:W0], pp[:, 1:W0], pp[:, 0:W0 - 1], ALU.add))
                if c == 0:
                    chain.link(pool.tensor_tensor(wB[64:P, 3:W0], wA[64:P, 3:W0], wA[64:P, 1:W0 - 2], ALU.add))
                else:
                    chain.link(pool.tensor_tensor(wB[:, 3:W0], wA[:, 3:W0], wA[:, 1:W0 - 2], ALU.add))
                    chain.link(pool.tensor_tensor(wA[:, 7:W0], wB[:, 7:W0], wB[:, 3:W0 - 4], ALU.add))
                    chain.link(pool.tensor_tensor(wB[64:P, 15:W0], wA[64:P, 15:W0], wA[64:P, 7:W0 - 8], ALU.add))
                for lo, ww in ((0, wA), (64, wB)):
                    r = slice(lo, lo + 64)
                    k16 = kc[r, K_POOL16 + 16 * c:K_POOL16 + 16 * c + 16]
                    chain.link(pool.tensor_tensor(fix16[r, :], ww[r, PADP:2 * PADP], k16, ALU.mult))
                    pool.tensor_tensor(pp[r, PADP:2 * PADP], fix16[r, :], pp[r, PADP:2 * PADP], ALU.subtract)
                    chain.link(pool.tensor_scalar(ww[r, 2 * PADP:W0], ww[r, 2 * PADP:W0], kc[r, K_POOLW + c:K_POOLW + c + 1], None, ALU.mult))
                    last = pool.tensor_tensor(pp[r, 2 * PADP:W0], ww[r, 2 * PADP:W0], pp[r, 2 * PADP:W0], ALU.subtract)
                    chain.link(last)
            pool.sem_inc(pool_d, 1)

            pool.wait_ge(c_tp, 2 * NT)
            pool.wait_ge(c_tev, 2 * NT)
            for s in range(2):
                for m in range(2):
                    z = pool.memset(qz[s][m], 0.0)
            z.then_inc(qz_zero, 1)
            for q in range(NB):
                o, ssq, rsq = on[:, q % 3, :], sm[:, q % 4, 8:9], sm[:, q % 4, 9:10]
                pool.wait_ge(o_cp, q + 1)
                chain.link(pool.tensor_scalar(ssq, ssq, 1.0 / P, EPS, ALU.mult, ALU.add))
                chain.link(pool.tensor_tensor(rsq, ssq, mhalf[:, 0:1], ALU.pow))
                pool.tensor_scalar(o, o, rsq, None, ALU.mult).then_inc(o_n, 1)

            pool.wait_ge(ot_evac, HEADS * NT)
            chain.link(pool.memset(shared[:, :], 1.0))
            pool.memset(reset.rearrange("p (c i) -> p c i", c=NCH)[:, :, 0:1], 0.0)
            pool.affine_select(out=mask_f, in_=mask_f, pattern=[[1, P]], compare_op=ALU.is_ge, fill=0.0, base=0, channel_multiplier=-1)
            chain.link(pool.affine_select(out=mask_b, in_=mask_b, pattern=[[-1, P]], compare_op=ALU.is_ge, fill=0.0, base=0, channel_multiplier=1))
            chain.link(pool.memset(mask_f[0:64, CH:P], 0.0))
            chain.link(pool.memset(mask_b[64:P, 0:CH], 0.0))
            pool.sem_inc(iotas, 1)
            pool.wait_ge(o_ready, HEADS * NT)
            pool.wait_ge(ot_evac, HEADS * NT)
            pool.memset(WF[:, 0, :, :], 0.0).then_inc(rw_zero, 1)
            pool.wait_ge(wo_ready, NT)
            chain.link(pool.memset(tri, 1.0))
            pool.affine_select(out=tri, in_=tri, pattern=[[1, P]], compare_op=ALU.is_gt, fill=0.0, base=0, channel_multiplier=-1).then_inc(iotas, 1)
            pool.iota(first4, pattern=[[-1, 4]], base=4, channel_multiplier=0, allow_small_or_imprecise_dtypes=True)
            pool.iota(iot, pattern=[[1, MTILES + 1]], base=0, channel_multiplier=0, allow_small_or_imprecise_dtypes=True)
            pool.iota(tokid, pattern=[[P, NT]], base=0, channel_multiplier=1, allow_small_or_imprecise_dtypes=True)
            pool.memset(one16, 1.0)
            pool.iota(initrow[:, :, 0:2], pattern=[[0, MTILES], [0, 2]], base=1 << 20, channel_multiplier=0)
            pool.memset(initrow_f[:, :, 2:4], 0.0).then_inc(slots_init, 1)
            pool.iota(rows[:, :, 0, 0:1], pattern=[[P, NT]], base=0, channel_multiplier=1)
            pool.iota(rows[:, :, 1, 0:1], pattern=[[P, NT]], base=0, channel_multiplier=1)
            pool.iota(rows[:, :, 0, 1:2], pattern=[[P, NT]], base=0, channel_multiplier=1)
            pool.iota(rows[:, :, 1, 1:2], pattern=[[P, NT]], base=S, channel_multiplier=1)
            pool.memset(rows_f[:, :, :, 3:4], 0.0).then_inc(iotas, 1)
            nt_pool(pool, chain, 1)
            pool.wait_ge(wo_ready, 2 * NT)
            chain.link(pool.memset(hg, 0.0))
            pool.wait_ge(slots_in, 16)
            pool.wait_ge(rx_done, 1)
            for t in range(NT):
                for k in range(2):
                    pool.indirect_dma_start(out=slot_dram[:, :], out_offset=bass.IndirectOffsetOnAxis(ap=sidx[:, t, k:k + 1].bitcast(U32), axis=0),
                                            in_=rows[:, t, k, :], in_offset=None).then_inc(slots_set, 16)
            pool.wait_ge(xn_st[0], 16 * 5)
            pool.wait_ge(xn_st[1], 16 * 5)

            pool.wait_ge(m_tab, 16)
            base = chain.n

            def gather(i, o):
                p = o % 2
                wait_past(pool, m_hg[p], i * 16 + 16 * (o // 2))
                settle(pool, settled)
                pool.tensor_copy(tok_of[:, p, 0:1], tabs[:, ds(i * 2 + o, 1), 0:1].rearrange("p a c -> p (a c)")).then_inc(m_tok, 1)
                pool.wait_ge(m_tok, i * 2 + (o + 1))
                wait_past(pool, m_xt, i * 2 + (o - 1))
                settle(pool, settled)
                pool.indirect_dma_start(out=hg[:, p, :], out_offset=None, in_=xn_dram[:, :],
                                        in_offset=bass.IndirectOffsetOnAxis(ap=tok_of[:, p, 0:1].bitcast(U32), axis=0),
                                        bounds_check=S - 1, oob_is_err=False).then_inc(m_hg[p], 16)

            def scatter(i, o):
                p = o % 2
                wait_past(pool, m_sc[p], i * 16 + 16 * (o // 2))
                settle(pool, settled)
                pool.tensor_copy(dst_of[:, p, 0:1], tabs[:, ds(i * 2 + o, 1), 1:2].rearrange("p a c -> p (a c)")).then_inc(m_dst, 1)
                pool.wait_ge(m_dst, i * 2 + (o + 1))
                pool.wait_ge(m_y, i * 2 + (o + 1))
                settle(pool, settled)
                pool.indirect_dma_start(out=y_dram[:, :], out_offset=bass.IndirectOffsetOnAxis(ap=dst_of[:, p, 0:1].bitcast(U32), axis=0),
                                        in_=yb[:, p, :], in_offset=None, bounds_check=2 * S - 1, oob_is_err=False).then_inc(m_sc[p], 16)

            def expert_pool(i, o):
                if has(i, o + 3):
                    gather(i, o + 3)
                if has(i, o - 1):
                    scatter(i, o - 1)
            for o in range(3):
                gather(0, o)
            experts(pool, expert_pool)
            pool.wait_ge(v2_in, 16 * 14)
            nt_pool(pool, chain, 2)
            base = chain.n

            def layer(L):
                hc = Chain(pool, pool_chain, L * 2 * NT + base)
                pool.wait_ge(h_in, L * NT + NT)
                pool.tensor_copy(vl[:, :], vec2[:, ds(L, 1), :].rearrange("p a n -> p (a n)")).then_inc(vl_ready, 1)

                def unit_lo(u):
                    w, n = 1 - u % 2, UNITS[u][3]
                    pool.wait_ge(uh_ready, L * NU + (u + 1))
                    settle(pool, settled)
                    pool.tensor_tensor(WFr[:, w, :, 0:n], WF[:, w, :, 0:n], wu_hi[:, w, :, 0:n].bitcast(F32), ALU.subtract).then_inc(ul_ready, 1)
                unit_lo(0)
                pool.memset(wgs, 0.0)
                pool.memset(WT[:, 0, :, :], 0.0).then_inc(z_ready, 1)
                pool.wait_ge(n_tp, L * 2 * NT + (3 * NT + 2))
                settle(pool, settled)
                pool.memset(lrz[0:64, :], 0.0).then_inc(lz_ready, 1)
                unit_lo(1)
                pool.wait_ge(mx_lo, mx_at(L, 0, NT - 1))
                settle(pool, settled)
                pool.memset(MIX[:, 0:4, :], 0.0).then_inc(z_ready, 1)
                for u in range(2, 16):
                    unit_lo(u)
                pool.wait_ge(kr_done, L + 1)
                pool.wait_ge(*gla(L, "kt", 3))
                pool.wait_ge(ul_ready, L * NU + 16)
                settle(pool, settled)
                pool.memset(kr[64:P, :], 0.0).then_inc(z_ready, 1)
                pool.wait_ge(z_ready, L * 5 + 3)
                settle(pool, settled)
                pool.tensor_copy(kr[0:64, :], kr0).then_inc(hz_ready, 1)
                pool.wait_ge(hz_ready, L * 2 + 1)
                for u in range(16, NU):
                    unit_lo(u)
                nt_pool(pool, hc, L * 2 + 3)
                nt_pool(pool, hc, L * 2 + 4)
                assert hc.n == 2 * NT
            layers(pool, layer)
        @block.scalar
        def _(act):
            with nc.allow_non_contiguous_dma(reason="a gain, one value a partition"):
                act.dma_start(vec1[:, V_AG:V_AG + 8], A["attn_norm_g"][0].rearrange("(c p) -> p c", p=P)).then_inc(ag_in, 16)
            for t in range(NT):
                nt_act(act, 0, t, lambda t: (x_in[t], 16), squares=psf[:, 6 * HALF:8 * HALF], scale=False)
                if t == 3:
                    b_hi(act, 0)
                if t >= 3:
                    ht_hi(act, t - 3)
            for t in range(NT - 3, NT):
                ht_hi(act, t)
            b_hi(act, 1)
            b_hi(act, 2)
            act.wait_ge(n_xn, NT)
            act.wait_ge(padded, 3)
            for c in range(2):
                for half in range(2):
                    n = 6 * c + half
                    act.wait_ge(b_ready, n + 1)
                    act.activation(sig_g[:, c, half * HALF:(half + 1) * HALF], bank(n % 2), ACT.Sigmoid).then_inc(b_evac[n % 2], 1)
                if c == 1:
                    b_hi(act, 5)
                    for k in range(KD):
                        c_hi(act, 0, k)
                for half in range(2):
                    n = 6 * c + 4 + half
                    act.wait_ge(b_ready, n + 1)
                    act.activation(p_pad[:, c, PADP + half * HALF:PADP + (half + 1) * HALF], bank(n % 2), ACT.Copy).then_inc(b_evac[n % 2], 1)
                    if c == 0:
                        b_hi(act, 3 + half)
            act.drain().then_inc(p_ready, 4)
            act.wait_ge(lam_e, 1)
            act.activation(lam4[:, 2:4], lam4[:, 0:2], ACT.Exp).then_inc(lam_e, 1)
            for n in range(3 * NT):
                act.wait_ge(c_ready, n + 1)
                if n < 2 * NT:
                    if n >= 2:
                        act.wait_ge(c_qn, n - 1)
                        act.wait_ge(c_red, n - 1)
                    act.activation(qtok[:, n % 2, :], bank(n % 2), ACT.Copy)
                    act.activation(xn[:, n % 2, 0:HALF], bank(n % 2), ACT.Square).then_inc(c_evac, 1)
                else:
                    act.activation(V1[:, n - 2 * NT, :], bank(n % 2), ACT.Copy).then_inc(c_evac, 1)
                if n < NT:
                    c_hi(act, 1, n)
                if n == 2 * NT - 1:
                    for k in range(KD):
                        c_hi(act, 2, k)
            for c in range(2):
                for half in range(2):
                    n = 2 * c + half
                    act.wait_ge(pl_ready, n + 1)
                    act.activation(MIX[:, 2 + c, half * HALF:(half + 1) * HALF], bank(n), ACT.Copy, scale=vec1[:, V_PS + c:V_PS + c + 1]).then_inc(pl_evac, 1)
            for half in range(2):
                act.wait_ge(ln_dve, half + 1)
                for c in range(2):
                    sq = act.activation(sq_cv[:, c, half * HALF:(half + 1) * HALF], y_cv[:, c, half * HALF:(half + 1) * HALF], ACT.Square)
                sq.then_inc(ln_act, 1)
            for half in range(2):
                act.wait_ge(ln_pe, half + 3)
                act.activation(r_cv[:, half * HALF:(half + 1) * HALF], bank(6 + half), ACT.Sqrt, scale=1.0 / 256, bias=eps[:, 0:1]).then_inc(ln_act, 1)
            for half in range(2):
                act.wait_ge(ln_dve, half + 3)
                for c in range(2):
                    yy = y_cv[:, c, half * HALF:(half + 1) * HALF]
                    si = act.activation(yy, yy, ACT.Silu, scale=vec1[:, V_LG + c:V_LG + c + 1], bias=vec1[:, V_LB + c:V_LB + c + 1])
                si.then_inc(ln_act, 1)
            for n in range(4):
                half, m = n // 2, n % 2
                act.wait_ge(pw_ready, n + 1)
                act.activation(MIX[:, m, half * HALF:(half + 1) * HALF], bank(n), ACT.Identity, bias=vec1[:, V_PB + m:V_PB + m + 1]).then_inc(pw_evac, 1)

            def stage(h):
                if h >= 2:
                    act.wait_ge(s_ready, 2 * NT * (h - 1))
                act.activation(qz[h % 2][0][0:64, :], qT[0:64, h, :], ACT.Copy)
                act.activation(qz[h % 2][1][64:P, :], qT[64:P, h, :], ACT.Copy).then_inc(qz_ready, 1)
            act.wait_ge(c_tev, 2 * NT)
            act.wait_ge(qz_zero, 1)
            stage(0)
            for g in range(NB + 3):
                if 2 <= g < NB + 2:
                    q = g - 2
                    b = BLOCKS[q][1]
                    for j in range(b // 4 + 1):
                        act.wait_ge(t_ready, TURNS[q] + j + 1)
                        if q >= 2:
                            act.wait_ge(o_ready, q - 1)
                        k = min(4, b + 1 - 4 * j)
                        act.activation(ATb[:, q % 2, 4 * j:4 * j + k, :], quads(4 + j)[:, 0:k, :], ACT.Copy).then_inc(at_evac, 1)
                if g < NB:
                    W = (BLOCKS[g][1] + 1) * P
                    for m in range(2):
                        act.wait_ge(s_neg, 2 * g + m + 1)
                        w = sS[m][g % (3 - m)][:, 0:W]
                        act.activation(w, w, ACT.Exp, bias=sm[:, g % 4, 2 + m:3 + m], accum_out=sm[:, g % 4, 4 + m:5 + m]).then_inc(e_ready, 1)
                if g >= 3:
                    q = g - 3
                    act.wait_ge(o_ready, q + 1)
                    if q >= 3:
                        act.wait_ge(ot_ready, q - 2)
                    act.activation(on[:, q % 3, :], bank(6, P, (q % 4) * P), ACT.Copy, scale=sm[:, q % 4, 6:7])
                    if q >= 1:
                        act.wait_ge(o_cp, q)
                    act.activation(osq, bank(6, P, (q % 4) * P), ACT.Square, scale=sm[:, q % 4, 6:7], accum_out=sm[:, q % 4, 8:9]).then_inc(o_cp, 1)
                if g < NB and g % NT == 2 and BLOCKS[g][0] + 1 < HEADS:
                    stage(BLOCKS[g][0] + 1)
                if NB - NT <= g < NB:
                    o_hi(act, 0, g - (NB - NT))
            act.wait_ge(ot_evac, NB)
            for t in range(3):
                mix1_hi(act, t)
            for t in range(NT):
                if t + 3 < NT:
                    mix1_hi(act, t + 3)
                o_hi(act, 1, t)
            for t in range(NT + 1):
                nt_act(act, 1, t, lambda t: (wo_evac, NT + t + 1), stored=xn_st, squares=psf[:, 6 * HALF:8 * HALF])
            for half in range(2):
                act.wait_ge(rt_ready, half + 1)
                act.activation(lgT[:, half * HALF:(half + 1) * HALF], bank(half), ACT.Copy).then_inc(rt_cp, 1)
            act.wait_ge(rx, 1)
            act.activation(ge, ge, ACT.Exp).then_inc(rx, 1)
            act.wait_ge(rx, 3)
            act.activation(le, le, ACT.Exp).then_inc(rx, 1)
            act.wait_ge(rope_set, 1)
            act.activation(ang, ang, ACT.Sin).then_inc(rope_set, 1)

            def expert_act(i, o):
                t = i * 2 + o
                if has(i, o - 1):
                    p = (o - 1) % 2
                    act.wait_ge(m_at, t)
                    wait_past(act, m_dn, i * 2 + (o - 2))
                    act.activation(actT[:, p, :, :], quads(4)[:, 0:2, :], ACT.Copy).then_inc(m_aT, 1)
                if has(i, o):
                    act.wait_ge(m_gu, i * 2 + (o + 1))
                    wait_past(act, m_act, i * 2 + (o - 1))
                    act.activation(sgb[:, o % 2, :], bank(2 + o % 2, DE), ACT.Silu).then_inc(m_sg, 1)
                if has(i, o - 1):
                    act.wait_ge(m_dn, t)
                    wait_past(act, m_sc[p], i * 16 + 16 * ((o - 1) // 2))
                    act.activation(yb[:, p, :], psf[:, 6 * HALF:8 * HALF], ACT.Copy).then_inc(m_y, 1)
            experts(act, expert_act)

            for half in range(2):
                act.sem_inc(u_evac[half], 1)
                act.sem_inc(f_evac[half], 1)
            PER = 4 * 2 + 4 + 2

            def rows_hi(act, L, t):
                act.wait_ge(n_ht, ht_ready(L * 2 + 2, t + 1))
                ts = slice(t * P, (t + 1) * P)
                act.activation(HTr[:, :, ts], MIX[:, :, ts], ACT.Copy).then_inc(mx_hi, 1)
            for t in range(NT + 1):
                nt_act(act, 2, t, lambda t: (h_in, t + 1), squares=psf[:, 6 * HALF:8 * HALF])
                if 4 <= t < NT:
                    rows_hi(act, 0, t - 4)

            def layer(L):
                hc = Chain(act, act_chain, L * PER)

                def unit_hi(u):
                    w, n = 1 - u % 2, UNITS[u][3]
                    act.wait_ge(u_w[u % 2], L * 16 * W_LAYER[u % 2] + 16 * W_SOFAR[u])
                    act.activation(wu_hi[:, w, :, 0:n], WF[:, w, :, 0:n], ACT.Copy).then_inc(uh_ready, 1)
                act.wait_ge(vl_ready, L + 1)
                act.wait_ge(n_tp, L * 2 * NT + (3 * NT + 1))
                unit_hi(0)
                for t in range(4, NT - 1):
                    rows_hi(act, L, t)
                unit_hi(1)
                rows_hi(act, L, NT - 1)

                def evac(kind, i, between=None):
                    u = UI[(kind, i)]
                    for half in range(2):
                        hs = slice(half * HALF, (half + 1) * HALF)
                        act.wait_ge(u_ready, L * 2 * NU + 2 * u + half + 1)
                        if kind == "kl":
                            for to, at, m in ((0, 0, 64), (64, 32, 32), (96, 0, 32)):
                                act.activation(krr[to:to + m, hs], ps[at:at + m, half, :], ACT.Copy)
                            act.wait_ge(lz_ready, L + 1)
                            o = act.activation(lrz[0:32, hs], ps[64:96, half, :], ACT.Copy)
                        if kind in ("gq", "gk"):
                            if i == 1:
                                act.wait_ge(*gla(L, "q", 1))
                            dup, scale = (q_dup, 64 ** -0.5) if kind == "gq" else (k_dup, 1.0)
                            for h in range(2):
                                for r in range(2):
                                    o = act.activation(dup[h][64 * r:64 * r + 64, hs], ps[64 * h:64 * h + 64, half, :], ACT.Copy, scale=scale)
                        if kind == "gv":
                            o = act.activation(gv[i % 2][:, hs], bank(half), ACT.Copy)
                        if kind == "gg":
                            o = act.activation(MIX[:, 4 + i, hs], bank(half), ACT.Silu)
                        if kind == "ga":
                            o = act.activation(MIX[:, i, hs], bank(half), ACT.Silu)
                        if kind in ("cq", "ckv"):
                            if (kind, i) == ("cq", 0):
                                act.wait_ge(*gla(L, "q", 3))
                            if (kind, i) == ("ckv", 0):
                                act.wait_ge(hz_ready, L * 2 + 1)
                            if (kind, i) == ("ckv", 1):
                                act.wait_ge(*gla(L, "done", 3))
                            to, sq = (c_q, sq_q) if kind == "cq" else (c_kv, sq_kv)
                            act.activation(to[i][:, hs], bank(half), ACT.Copy)
                            o = act.activation(sq[i][:, hs], bank(half), ACT.Square)
                        o.then_inc(u_evac[half], 1)
                        if 1 <= u < NU - 1 and half == 0:
                            unit_hi(u + 1)
                        if half == 0 and between is not None:
                            between()
                    if kind == "gv":
                        for half in range(2):
                            act.wait_ge(v_tp, L * 8 + (2 * i + half + 1))
                            act.activation(gv[i % 2][:, half * HALF:(half + 1) * HALF], bank(half), ACT.Copy).then_inc(v_ev, 1)

                def gate(h):
                    act.wait_ge(*gla(L, "z", h))
                    if h >= 1:
                        act.wait_ge(*gla(L, "k", h - 1))
                    for half in range(2):
                        hs, bias = slice(half * HALF, (half + 1) * HALF), vl[:, L_GB + h:L_GB + h + 1]
                        act.activation(la[:, hs], bank(2 + half), ACT.Identity, bias=bias)
                        o = act.activation(gt[:, hs], bank(2 + half), ACT.Abs, bias=bias)
                    hc.link(o)
                    hc.link(act.activation(gt, gt, ACT.Exp, scale=-1.0))
                    act.activation(gt, gt, ACT.Ln, bias=ones[:, 0:1]).then_inc(g_act, 1)

                def exps(h):
                    act.wait_ge(*gla(L, "d", h))
                    if h >= 1:
                        act.wait_ge(*gla(L, "a", h - 1))
                    act.activation(q_in, gt, ACT.Exp, scale=1 / 16.0)
                    act.activation(gt, gt, ACT.Exp, scale=-1 / 16.0)
                    act.activation(la, la, ACT.Exp, scale=1 / 16.0)
                    act.activation(cum, cum, ACT.Exp, scale=1 / 16.0)
                    act.activation(decay, lasts, ACT.Exp, scale=1 / 16.0).then_inc(g_act, 1)

                def ks_copy(h):
                    act.wait_ge(*gla(L, "kt", h))
                    act.wait_ge(z_ready, L * 5 + 2)
                    for half in range(2):
                        act.activation(ks_even[0:64, half * HALF:(half + 1) * HALF], ps[0:64, 6 + half, :], ACT.Copy)
                        o = act.activation(ks_odd[64:P, half * HALF:(half + 1) * HALF], ps[64:P, 6 + half, :], ACT.Copy)
                    o.then_inc(g_act, 1)

                def kv_copy(h):
                    act.wait_ge(*gla(L, "kv", h))
                    for b in range(4):
                        o = act.activation(kv[:, 4 * b:4 * b + 4, :], quads(2 + b), ACT.Copy)
                    o.then_inc(g_act, 1)

                def square(h):
                    act.wait_ge(*gla(L, "o", h))
                    if h >= 1:
                        act.wait_ge(*gla(L, "done", h - 1))
                    for half in range(2):
                        o = act.activation(sqg[:, half * HALF:(half + 1) * HALF], bank(6 + half), ACT.Square)
                    o.then_inc(g_act, 1)

                def inv_rms(to, b, width, done):
                    for half in range(2):
                        o = act.activation(to[:, half * HALF:(half + 1) * HALF], bank(b + half), ACT.Ln, scale=1.0 / width, bias=eps[:, 0:1])
                    hc.link(o)
                    act.activation(to, to, ACT.Exp, scale=-0.5).then_inc(done, 1)

                def rms(h):
                    act.wait_ge(*gla(L, "ms", h))
                    inv_rms(sqg, 4, P, g_act)

                for e in (("kl", 0), ("gq", 0), ("gk", 0)):
                    evac(*e)
                gate(0)
                evac("gv", 0)
                exps(0)
                evac("gg", 0)
                under = ((("gv", 1), ("gg", 1), ("gq", 1)), (("gk", 1), ("gv", 2), ("gg", 2)), (("gv", 3), ("gg", 3), ("cq", 0)), (("cq", 1), ("cq", 2), ("ckv", 0)))
                for h in range(4):
                    ks_copy(h)
                    evac(*under[h][0])
                    kv_copy(h)
                    if h < 3:
                        gate(h + 1)
                    evac(*under[h][1])
                    if h < 3:
                        exps(h + 1)
                    square(h)
                    evac(*under[h][2], between=lambda: rms(h))
                evac("ckv", 1)
                act.wait_ge(l_ms, L * 2 + 1)
                inv_rms(r_q, 2, 384, l_r)
                evac("ga", 0)
                act.wait_ge(l_ms, L * 2 + 2)
                inv_rms(r_kv, 6, 256, l_r)
                for i in range(1, 4):
                    evac("ga", i)
                act.activation(kr_hi, kr, ACT.Copy).then_inc(z_ready, 1)
                for s in (1, 5):
                    o = act.activation(HTr[64:P, s, :], kr[64:P, :], ACT.Copy)
                o.then_inc(hz_ready, 1)
                assert hc.n == PER, hc.n

                def fill(f):
                    kind, h, j = FILLS[f]
                    if kind != "p" or j in (2, 3):
                        return
                    act.wait_ge(f_ready, L * NF + f + 1)
                    at = (0, 0, None, None, 2, 2, 3, 3)[j]
                    to = (HT if at == 3 else HTr)[:, 4 * (h % 2) + at, (j % 2) * HALF:(j % 2 + 1) * HALF]
                    act.activation(to, bank(f % 2), ACT.Copy).then_inc(f_evac[f % 2] if at == 3 else fh_ready, 1)

                def weights_hi(i, k):
                    n = i % 2
                    if k == 0:
                        act.wait_ge(wo_w[n], L * 32 + (32 + 16 * (i // 2)))
                    act.activation(w_hi[n][:, k, :], WT[:, n, k, :], ACT.Copy).then_inc(wh_ready, 1)

                def mix_hi(t):
                    ts = slice(t * P, (t + 1) * P)
                    act.activation(HTr[:, :, ts], MIX[:, :, ts], ACT.Copy).then_inc(mx_hi, 1)
                for f in range(8):
                    fill(f)
                f = 8
                for g in range(STEPS):
                    if g < 4 * NT:
                        act.wait_ge(a_neg, L * 4 * NT + g + 1)
                        if g >= 2:
                            act.wait_ge(a_t[1], L * 4 * NT + g - 1)
                        act.activation(xn[:, g % 2, :], psf[:, (2 + 2 * (g % 2)) * HALF:(4 + 2 * (g % 2)) * HALF], ACT.Exp, scale=MLA_SCALE,
                                       bias=sm[:, g % 2, 1:2], accum_out=sm[:, g % 2, 2:3]).then_inc(a_e, 1)
                    if g < 3 * NT:
                        fill(f)
                        f += 1
                    if g >= 5 and (g - 2) % 4 == 3:
                        f += 1
                    if 1 <= g <= 4 * NT:
                        q = g - 1
                        G = q // 4
                        act.wait_ge(a_t[1], L * 4 * NT + q + 1)
                        if G >= 2 and q % 4 == 0:
                            act.wait_ge(f_ready, L * NF + FI[("v", G - 2, 0)] + 1)
                        act.activation(PT[G % 2][:, 4:8, (q % 4) * P:(q % 4 + 1) * P], quads(7), ACT.Copy).then_inc(a_tev[1], 1)
                    if g >= STEPS - KD:
                        weights_hi(0, g - (STEPS - KD))
                fv = FI[("v", 7, 0)]
                act.wait_ge(f_evac[fv % 2], fill_evac(L, fv))
                act.wait_ge(f_ready, L * NF + NF)
                for t in range(3):
                    mix_hi(t)
                for u in range(NT):
                    if u + 3 < NT:
                        mix_hi(u + 3)
                    weights_hi(1, u)
                for b in range(4):
                    act.wait_ge(p_tp, L * 4 + b + 1)
                    act.activation(pT[:, b // 2, (b % 2) * HALF:(b % 2 + 1) * HALF], bank(2 + b), ACT.Copy).then_inc(p_ev, 1)

                def norm(t):
                    nt_act(act, L * 2 + 3, t, lambda t: (wo_evac, L * 2 * NT + (3 * NT + t + 1)), squares=psf[:, 6 * HALF:8 * HALF])

                def normed_hi(t):
                    act.wait_ge(n_ht, ht_ready(L * 2 + 3, t + 1))
                    mix_hi(t)
                for t in range(NT):
                    norm(t)
                    if 3 <= t < 7:
                        weights_hi(2, 2 * (t - 3))
                        weights_hi(2, 2 * (t - 3) + 1)
                    if t >= 3:
                        normed_hi(t - 3)
                norm(NT)
                for t in range(NT - 3, NT):
                    normed_hi(t)
                for u in range(2 * NT):
                    act.wait_ge(pg_ready, L * 2 * NT + u + 1)
                    act.wait_ge(pg_evac, L * 2 * NT + u + 2)
                    act.activation(sgp[:, u % 2, :], bank(u % 2), ACT.Sigmoid).then_inc(pg_sg, 1)
                    if 2 <= u < 6:
                        weights_hi(3, 2 * (u - 2))
                        weights_hi(3, 2 * (u - 2) + 1)
                    if u >= NT + 1:
                        nt_act(act, L * 2 + 4, u - NT - 1, lambda t: (h_in, L * NT + (NT + t + 1)))
                    if u >= NT + 4:
                        rows_hi(act, L + 1, u - NT - 4)
                for t in (NT - 1, NT):
                    nt_act(act, L * 2 + 4, t, lambda t: (h_in, L * NT + (NT + t + 1)))
            layers(act, layer)
        @block.tensor
        def _(pe):
            pe.sem_inc(n_tp, 2)
            pe.wait_ge(idready, 3)
            for t in range(NT - 2):
                nt_pe(pe, 0, t)
            for u in range(6):
                pe.wait_ge(wl_ready, u + 1)
                for half in range(2):
                    n, hs = 2 * u + half, slice(half * HALF, (half + 1) * HALF)
                    if n >= 2:
                        pe.wait_ge(b_evac[n % 2], n // 2)
                    if n == 1:
                        for t in range(NT - 2, NT):
                            nt_pe(pe, 0, t)
                    if n <= 1:
                        pe.wait_ge(mx_lo, (n + 1) * NT // 2)
                    accumulate_split(pe, bank(n % 2), [(wb_hi[:, u % 3, k, :], WFr[:, u % 3, k, :], HTr[:, k, hs], MIXr[:, k, hs]) for k in range(KD)]).then_inc(b_ready, 1)
            pe.wait_ge(b_evac[0], 6)
            pe.wait_ge(b_evac[1], 6)

            def turn(n):
                pe.wait_ge(c_qn, n + 1)
                if n >= 2:
                    pe.wait_ge(c_tev, n - 1)
                for h in range(4):
                    tp = pe.transpose(bank(2 + n % 2, P, h * P), qn[:, n % 2, h * P:(h + 1) * P], ident[:, :])
                tp.then_inc(c_tp, 1)
            for n in range(3 * NT):
                blk, t = n // NT, n % NT
                ts = slice(t * P, (t + 1) * P)
                if t == 0 and blk < 2:
                    pe.wait_ge(wl_ready, 6 + (blk + 1) * KD)
                if n >= 2:
                    pe.wait_ge(c_evac, n - 1)
                accumulate_split(pe, bank(n % 2), [(HTr[:, k, ts], MIXr[:, k, ts], wc_hi[blk][:, k, :], WTr[:, blk % 2, k, :]) for k in range(KD)],
                                 (lambda k: pe.wait_ge(wl_ready, 6 + 2 * KD + k + 1)) if n == 2 * NT else None).then_inc(c_ready, 1)
                if 2 <= n < 2 * NT + 2:
                    turn(n - 2)
            pe.wait_ge(c_evac, 3 * NT)
            pe.wait_ge(c_tev, 2 * NT)
            pe.wait_ge(pool_d, 1)
            pe.wait_ge(pw_in, 80)
            for c in range(2):
                for half in range(2):
                    pe.matmul(bank(2 * c + half), pwb[:, c, :], p_pad[:, c, PADP + half * HALF:PADP + (half + 1) * HALF], start=True, stop=True).then_inc(pl_ready, 1)
            pe.wait_ge(cv_dve, 1)
            for half in range(2):
                accumulate(pe, bank(4 + half), [(ones[:, :], y_cv[:, c, half * HALF:(half + 1) * HALF]) for c in range(2)]).then_inc(ln_pe, 1)
            for half in range(2):
                pe.wait_ge(ln_act, half + 1)
                accumulate(pe, bank(6 + half), [(ones[:, :], sq_cv[:, c, half * HALF:(half + 1) * HALF]) for c in range(2)]).then_inc(ln_pe, 1)
            pe.wait_ge(pl_evac, 4)
            pe.wait_ge(pw_in, 80)
            for n in range(4):
                half, m = n // 2, n % 2
                pe.wait_ge(ln_act, half + 5)
                accumulate(pe, bank(n), [(cpw[:, c, m * P:(m + 1) * P], y_cv[:, c, half * HALF:(half + 1) * HALF]) for c in range(2)]).then_inc(pw_ready, 1)

            pe.wait_ge(pw_evac, 4)
            for g in range(NB + 5):
                if g < NB:
                    h, b = BLOCKS[g]
                    W = (b + 1) * P
                    if g % NT == 0:
                        pe.wait_ge(qz_ready, h + 1)
                    for m in range(2):
                        if g >= 1:
                            pe.wait_ge(s_max, 2 * g + m - 1)
                        for j in range((W + HALF - 1) // HALF):
                            w = min(HALF, W - j * HALF)
                            mm = pe.matmul(bank(2 * m + j, w), qz[h % 2][m][:, b * P:(b + 1) * P], kT[:, h, j * HALF:j * HALF + w], start=True, stop=True)
                        mm.then_inc(s_ready, 1)
                if 2 <= g < NB + 2:
                    q = g - 2
                    b = BLOCKS[q][1]
                    pe.wait_ge(a_ready, q + 1)
                    if q >= 1:
                        pe.wait_ge(at_evac, TURNS[q])
                    for j in range(b // 4 + 1):
                        for k in range(4 * j, min(4 * j + 4, b + 1)):
                            tp = pe.transpose(bank(4 + j, P, (k % 4) * P), sS[0][q % 3][:, k * P:(k + 1) * P], ident[:, :])
                        tp.then_inc(t_ready, 1)
                if 3 <= g < NB + 3:
                    q = g - 3
                    h, b = BLOCKS[q]
                    pe.wait_ge(at_evac, TURNS[q + 1])
                    if q >= 1:
                        pe.wait_ge(o_cp, q)
                    accumulate(pe, bank(6, P, (q % 4) * P), [(ATb[:, q % 2, k, :], V1[:, k, h * P:(h + 1) * P]) for k in range(b + 1)]).then_inc(o_ready, 1)
                if g >= 5:
                    q = g - 5
                    pe.wait_ge(o_n, q + 1)
                    if q >= 1:
                        pe.wait_ge(ot_evac, q)
                    pe.transpose(bank(7, P, (q % 4) * P), on[:, q % 3, :], ident[:, :]).then_inc(ot_ready, 1)
            pe.wait_ge(ot_evac, NB)
            for n in range(2):
                pe.wait_ge(wl_ready, W_O + (n + 1) * KD)
                for t in range(NT):
                    u, ts = n * NT + t, slice(t * P, (t + 1) * P)
                    if u >= 2:
                        pe.wait_ge(wo_evac, u - 1)
                    if n == 0:
                        pe.wait_ge(mx_lo, NT + t + 1)
                    accumulate_split(pe, bank(u % 2), [(HTr[:, k, ts], MIXr[:, k, ts], out_hi(n, k), WTr[:, n, k, :]) for k in range(KD)]).then_inc(wo_ready, 1)
                    if u >= NT + 2:
                        nt_pe(pe, 1, t - 2)
            nt_pe(pe, 1, NT - 2)
            pe.wait_ge(rw_in, 64)
            pe.wait_ge(wo_evac, 2 * NT)
            for half in range(2):
                if half == 1:
                    nt_pe(pe, 1, NT - 1)
                pe.wait_ge(n_ht, ht_ready(1, (half + 1) * NT // 2))
                accumulate(pe, bank(half), [(WF[:, 0, k, :], HT[:, k, half * HALF:(half + 1) * HALF]) for k in range(KD)]).then_inc(rt_ready, 1)
            pe.wait_ge(rt_cp, 2)
            for t in range(NT):
                tp = pe.transpose(bank(2 + t // 4, P, (t % 4) * P), lgT[:, t * P:(t + 1) * P], ident[:, :])
            tp.then_inc(rt_tp, 1)
            pe.wait_ge(rm_ready, 1)
            MMf = MM.rearrange("p t e -> p (t e)")
            pe.wait_ge(iotas, 3)
            pe.matmul(bank(6, P), tri, MMf, start=True, stop=True)
            pe.matmul(bank(7, P), ones[:, :], MMf, start=True, stop=True).then_inc(rp_ready, 1)

            def turn_rows(i, o):
                p = o % 2
                pe.wait_ge(m_hg[p], i * 16 + (16 * (o // 2) + 16))
                wait_past(pe, m_ht, i * 2 + o)
                for c in range(KD):
                    tp = pe.transpose(bank(c // 4, P, (c % 4) * P), hg[:, p, c * P:(c + 1) * P], ident[:, :])
                tp.then_inc(m_xt, 1)

            def gate_up(i, o, ks):
                p = o % 2
                if 0 in ks:
                    pe.wait_ge(m_ht, i * 2 + (o + 1))
                    pe.wait_ge(m_wgu[p], i * 32 + (32 * (o // 2) + 32))
                    wait_past(pe, m_act, i * 2 + (o - 1))
                for k in ks:
                    mm = pe.matmul(bank(2 + p), hgT[:, p, k, :], WT[:, p, k, :], start=(k == 0), stop=(k == KD - 1))
                if KD - 1 in ks:
                    mm.then_inc(m_gu, 1)

            def turn_act(i, o):
                pe.wait_ge(m_act, i * 2 + (o + 1))
                wait_past(pe, m_aT, i * 2 + o)
                for k in range(2):
                    tp = pe.transpose(bank(4, P, k * P), actb[:, o % 2, k * P:(k + 1) * P], ident[:, :])
                tp.then_inc(m_at, 1)

            def down(i, o):
                p = o % 2
                pe.wait_ge(m_aT, i * 2 + (o + 1))
                pe.wait_ge(m_wd[p], i * 16 + (16 * (o // 2) + 16))
                wait_past(pe, m_y, i * 2 + o)
                for n in range(2):
                    mm = accumulate(pe, bank(6 + n), [(actT[:, p, k, :], wd[:, p, k, n * HALF:(n + 1) * HALF]) for k in range(2)])
                mm.then_inc(m_dn, 1)

            def expert_pe(i, o):
                if has(i, o):
                    gate_up(i, o, range(0, 5))
                if has(i, o - 1):
                    turn_act(i, o - 1)
                if has(i, o):
                    gate_up(i, o, range(5, KD))
                if has(i, o + 1):
                    turn_rows(i, o + 1)
                if has(i, o - 1):
                    down(i, o - 1)
            turn_rows(0, 0)
            experts(pe, expert_pe)
            for t in range(NT - 1):
                nt_pe(pe, 2, t)

            def layer(L):

                def unit(kind, i, between=None):
                    u = UI[(kind, i)]
                    s = u % 2
                    w = 1 - s
                    if u == 0:
                        nt_pe(pe, L * 2 + 2, NT - 1)
                    pe.wait_ge(ul_ready, L * NU + (u + 1))
                    for half in range(2):
                        if u == 0:
                            pe.wait_ge(mx_lo, mx_at(L, 0, (half + 1) * NT // 2 - 1))
                        pe.wait_ge(u_evac[half], L * NU + u + 1)
                        if u >= 1 and UNITS[u - 1][0] == "gv":
                            pe.wait_ge(v_ev, L * 8 + (2 * UNITS[u - 1][1] + half + 1))
                        m, hs = UNITS[u][3], slice(half * HALF, (half + 1) * HALF)
                        mm = accumulate_split(pe, ps[0:m, half, :].rearrange("p (t n) -> p t n", t=4),
                                                  [(wu_hi[:, w, k, 0:m], WFr[:, w, k, 0:m], HTr[:, k, hs].rearrange("p (t n) -> p t n", t=4), Hr[:, 4 * half:4 * half + 4, k, :])
                                                   for k in range(KD)])
                        mm.then_inc(u_ready, 1)
                        if half == 0 and between is not None:
                            between()
                    if kind == "gv":
                        for half in range(2):
                            pe.wait_ge(u_evac[half], unit_evac(L, u, half))
                            for t in range(4):
                                at = (4 * half + t) * P
                                tp = pe.transpose(bank(half, P, t * P), gv[i % 2][:, at:at + P], ident[:, :])
                            tp.then_inc(v_tp, 1)

                def gates(h):
                    if h == 0:
                        pe.wait_ge(wg_in, L * 32 + 32)
                        pe.wait_ge(kr_done, L + 1)
                        for half in range(2):
                            pe.wait_ge(u_evac[half], unit_evac(L, 0, half))
                    else:
                        pe.wait_ge(*gla(L, "kvc", h - 1))
                    for half in range(2):
                        mm = pe.matmul(bank(2 + half), wgs[:, h, :], lrz[:, half * HALF:(half + 1) * HALF], start=True, stop=True)
                    mm.then_inc(g_pe, 1)

                def inner(h):
                    pe.wait_ge(*gla(L, "k", h))
                    if h >= 1:
                        pe.wait_ge(*gla(L, "r", h - 1))
                    for d, kk in enumerate((kf, kb)):
                        for t in range(NT):
                            mm = pe.matmul(bank(2 + 2 * d + t // 4, P, (t % 4) * P), kk[:, t * P:(t + 1) * P], q_in[:, t * P:(t + 1) * P], start=True, stop=True)
                    mm.then_inc(g_pe, 1)
                    if h >= 1:
                        pe.wait_ge(*gla(L, "done", h - 1))
                    for t in range(NT):
                        tp = pe.transpose(bank(6 + t // 4, P, (t % 4) * P), la[:, t * P:(t + 1) * P], ident[:, :])
                    tp.then_inc(g_pe, 1)

                def states(h):
                    pe.wait_ge(*gla(L, "ks", h))
                    pe.wait_ge(*gla(L, "am", h))
                    pe.wait_ge(v_ev, L * 8 + 2 * h + 2)
                    for c in range(NCH):
                        t = c // 2
                        mm = pe.matmul(bank(2 + c // 4, P, (c % 4) * P), (ks_even, ks_odd)[c % 2][:, t * P:(t + 1) * P], gv[h % 2][:, t * P:(t + 1) * P], start=True, stop=True)
                    mm.then_inc(g_pe, 1)

                def outputs(h):
                    pe.wait_ge(*gla(L, "st", h))
                    for t in range(NT):
                        ts = slice(t * P, (t + 1) * P)
                        mm = accumulate(pe, bank(6 + t // 4, P, (t % 4) * P), [(gv[h % 2][:, ts], Af[:, ts]), (gv[h % 2][:, ts], Ab[:, ts]),
                                                                             (st[:, 2 * t, :], q_even[:, ts]), (st[:, 2 * t + 1, :], q_odd[:, ts])])
                    mm.then_inc(g_pe, 1)

                def squares(h):
                    pe.wait_ge(*gla(L, "sq", h))
                    for half in range(2):
                        mm = pe.matmul(bank(4 + half), ones[:, :], sqg[:, half * HALF:(half + 1) * HALF], start=True, stop=True)
                    mm.then_inc(g_pe, 1)

                unit("kl", 0)
                unit("gq", 0)
                unit("gk", 0)
                gates(0)
                unit("gv", 0)
                unit("gg", 0)
                under = ((("gv", 1), ("gg", 1), ("gq", 1)), (("gk", 1), ("gv", 2), ("gg", 2)), (("gv", 3), ("gg", 3), ("cq", 0)), (("cq", 1), ("cq", 2), ("ckv", 0)))
                for h in range(4):
                    inner(h)
                    unit(*under[h][0])
                    states(h)
                    if h < 3:
                        gates(h + 1)
                    unit(*under[h][1])
                    outputs(h)
                    unit(*under[h][2], between=lambda: squares(h))
                unit("ckv", 1)
                for half in range(2):
                    accumulate(pe, bank(2 + half), [(ones[:, :], q[:, half * HALF:(half + 1) * HALF]) for q in sq_q])
                pe.drain().then_inc(l_ms, 1)
                unit("ga", 0)
                pe.wait_ge(*gla(L, "done", 3))
                for half in range(2):
                    accumulate(pe, bank(6 + half), [(ones[:, :], q[:, half * HALF:(half + 1) * HALF]) for q in sq_kv])
                pe.drain().then_inc(l_ms, 1)
                for i in range(1, 4):
                    unit("ga", i)
                for half in range(2):
                    pe.wait_ge(u_evac[half], unit_evac(L, NU - 1, half))

                def fill(f):
                    kind, h, j = FILLS[f]
                    pe.wait_ge(f_evac[f % 2], L * (NF // 2) + f // 2 + 1)
                    o = bank(f % 2)
                    if kind == "p":
                        s, hs = h % 2, slice((j % 2) * HALF, (j % 2 + 1) * HALF)
                        if j == 0:
                            pe.wait_ge(uw[s], L * 128 + 64 * (h // 2) + 64)
                        if j < 4:
                            c = (j // 2) * P
                            mm = accumulate(pe, o, [(uq[s][:, k, c:c + P], c_q[k][:, hs]) for k in range(3)])
                        elif j < 6:
                            mm = accumulate(pe, o, [(ukv[s][:, k, 0:P], c_kv[k][:, hs]) for k in range(2)])
                        else:
                            for t in range(4):
                                ts = slice((4 * (j % 2) + t) * P, (4 * (j % 2) + t + 1) * P)
                                mm = accumulate(pe, bank(f % 2, P, t * P), [(c_kv[k][:, ts], ukv[s][:, k, P:2 * P]) for k in range(2)])
                    else:
                        G = h
                        hd = G // 2
                        for i in range(2):
                            pe.wait_ge(a_tev[i], L * 4 * NT + 4 * G + 4)
                            fv = FI[("p", hd, 6 + i)]
                            if fv % 2 != f % 2:
                                pe.wait_ge(f_evac[fv % 2], fill_evac(L, fv))
                        mm = accumulate(pe, o, [(HT[:, 4 * (hd % 2) + 3, k * P:(k + 1) * P], PT[G % 2][:, k, :]) for k in range(KD)])
                    mm.then_inc(f_ready, 1)
                pe.wait_ge(l_c, L * 2 + 2)
                for f in range(8):
                    fill(f)
                pe.wait_ge(hz_ready, L * 2 + 2)
                pe.wait_ge(z_ready, L * 5 + 5)
                f = 8
                for g in range(STEPS):
                    if g < 4 * NT:
                        h, b, s = g // NT, g % NT, 4 * (g // NT % 2)
                        if b == 0:
                            for j in (4, 5):
                                fv = FI[("p", h, j)]
                                pe.wait_ge(f_evac[fv % 2], fill_evac(L, fv))
                        if g >= 2:
                            pe.wait_ge(a_e, L * 4 * NT + g - 1)
                        for half in range(2):
                            hs = slice(half * HALF, (half + 1) * HALF)
                            qs = slice(b * P, (b + 1) * P)
                            mm = accumulate_split(pe, bank(2 + 2 * (g % 2) + half), [(HTr[:, s, qs], Hlo[:, s, qs], HTr[:, s + 2, hs], Hlo[:, s + 2, hs]),
                                                                                     (HTr[:, s + 1, qs], Hlo[:, s + 1, qs], kr_hi[:, hs], kr_lo[:, hs])])
                        mm.then_inc(a_s, 1)
                    if g < 3 * NT:
                        fill(f)
                        f += 1
                    if g >= 5 and (g - 2) % 4 == 3:
                        fill(f)
                        f += 1
                    if 1 <= g <= 4 * NT:
                        q = g - 1
                        pe.wait_ge(a_p, L * 4 * NT + q + 1)
                        for half in range(2):
                            if q >= 1:
                                pe.wait_ge(a_tev[half], L * 4 * NT + q)
                            for k in range(4):
                                tp = pe.transpose(bank(6 + half, P, k * P), xn[:, q % 2, (4 * half + k) * P:(4 * half + k + 1) * P], ident[:, :])
                            tp.then_inc(a_t[half], 1)
                assert f == NF
                for i in range(2):
                    pe.wait_ge(f_evac[i], L * (NF // 2) + NF // 2 + 1)
                for n in range(2):
                    pe.wait_ge(wl_ready, L * 4 * KD + W_1 + (n + 1) * KD)
                    for t in range(NT):
                        u, ts = n * NT + t, slice(t * P, (t + 1) * P)
                        pe.wait_ge(wo_evac, L * 2 * NT + (2 * NT + u - 1))
                        if n == 0:
                            pe.wait_ge(mx_lo, mx_at(L, 1, t))
                        accumulate_split(pe, bank(u % 2), [(HTr[:, k, ts], MIXr[:, k, ts], w_hi[n][:, k, :], WTr[:, n, k, :]) for k in range(KD)]).then_inc(wo_ready, 1)
                        if u == NT + 2:
                            pe.wait_ge(p_ev, L * 4 + 4)
                        if u >= NT + 2:
                            nt_pe(pe, L * 2 + 3, t - 2)
                    if n == 0:
                        pe.wait_ge(p_in, L * 32 + 32)
                        for b in range(4):
                            for t in range(4):
                                tp = pe.transpose(bank(2 + b, P, t * P), p_tok[:, 4 * (b % 2) + t, (b // 2) * P:(b // 2 + 1) * P], ident[:, :])
                            tp.then_inc(p_tp, 1)
                nt_pe(pe, L * 2 + 3, NT - 2)
                pe.wait_ge(wo_evac, L * 2 * NT + 4 * NT)
                for n in range(2):
                    pe.wait_ge(wl_ready, L * 4 * KD + W_1 + (n + 3) * KD)
                    for t in range(NT):
                        u, ts = n * NT + t, slice(t * P, (t + 1) * P)
                        pe.wait_ge(pg_evac, L * 2 * NT + u + 1)
                        if n == 0:
                            pe.wait_ge(mx_lo, mx_at(L, 2, t))
                        accumulate_split(pe, bank(u % 2), [(HTr[:, k, ts], MIXr[:, k, ts], w_hi[n][:, k, :], WTr[:, n, k, :]) for k in range(KD)])
                        if u == 0:
                            nt_pe(pe, L * 2 + 3, NT - 1)
                        accumulate(pe, bank(6 + u % 2), [(pT[:, c, t * P:(t + 1) * P], wpp[:, c, n * HALF:(n + 1) * HALF]) for c in range(2)]).then_inc(pg_ready, 1)
                        if u >= NT + 3:
                            nt_pe(pe, L * 2 + 4, u - NT - 3)
                for t in (NT - 3, NT - 2):
                    nt_pe(pe, L * 2 + 4, t)
            layers(pe, layer)

        @block.vector
        def _(dve):
            chain = Chain(dve, dve_chain)
            dve.sem_inc(n_ht, 2)
            dve.wait_ge(ag_in, 16)
            for t in range(NT):
                nt_dve(dve, 0, t, vec1[:, V_AG:V_AG + 8], MIX)
                if t == 2:
                    b_lo(dve, 0)
                if t >= 1:
                    ht_lo(dve, t - 1)
            ht_lo(dve, NT - 1)
            b_lo(dve, 1)
            b_lo(dve, 2)
            dve.wait_ge(b_ready, 2)
            dve.memset(p_pad[:, :, 0:PADP], 0.0).then_inc(padded, 1)
            dve.memset(u_pad[:, :, 0:PADC], 0.0).then_inc(padded, 1)
            dve.wait_ge(const_in, 16 * 18)
            chain.link(dve.tensor_scalar(vec1[:, V_QG:V_QG + 1], vec1[:, V_QG:V_QG + 1], DH ** -0.5, None, ALU.mult))
            chain.link(dve.tensor_scalar(vec1[:, V_SG:V_SG + 1], vec1[:, V_SG:V_SG + 1], 1.0 - LAM_INIT, None, ALU.mult))
            for i in range(2):
                chain.link(dve.tensor_tensor(lamt[:, 2 * i, :], lamt[:, 2 * i, :], lamt[:, 2 * i + 1, :], ALU.mult))
                chain.link(dve.tensor_reduce(lam4[:, i:i + 1], lamt[:, 2 * i, :], AX.X, ALU.add))
            dve.sem_inc(lam_e, 1)
            for c in range(2):
                for half in range(2):
                    n = 6 * c + 2 + half
                    dve.wait_ge(b_ready, n + 1)
                    dve.wait_ge(b_evac[n % 2], 3 * c + 1)
                    dve.tensor_tensor(u_pad[:, c, PADC + half * HALF:PADC + (half + 1) * HALF], bank(n % 2),
                                      sig_g[:, c, half * HALF:(half + 1) * HALF], ALU.mult).then_inc(b_evac[n % 2], 1)
                if c == 0:
                    for u in range(3, 6):
                        b_lo(dve, u)
            for k in range(KD):
                c_lo(dve, 0, k)
            dve.wait_ge(lam_e, 2)
            chain.link(dve.tensor_tensor(lam4[:, 4:5], lam4[:, 2:3], lam4[:, 3:4], ALU.subtract))
            chain.link(dve.tensor_scalar(lam4[:, 4:5], lam4[:, 4:5], LAM_INIT, -1.0, ALU.add, ALU.mult))
            dve.wait_ge(padded, 3)
            tap = 0

            def convolve(last):
                nonlocal tap
                while tap < min(last, TAPS):
                    for c in range(2):
                        w = vec1[:, V_CW + TAPS * c + tap:V_CW + TAPS * c + tap + 1]
                        uu = u_pad[:, c, tap:tap + S]
                        if tap == 0:
                            o = dve.tensor_scalar(y_cv[:, c, :], uu, w, vec1[:, V_CB + c:V_CB + c + 1], ALU.mult, ALU.add)
                        else:
                            o = dve.scalar_tensor_tensor(out=y_cv[:, c, :], in0=uu, scalar=w, in1=y_cv[:, c, :], op0=ALU.mult, op1=ALU.add)
                    chain.link(o)
                    tap += 1
            for n in range(2 * NT + 2):
                if n < 2 * NT:
                    dve.wait_ge(c_evac, n + 1)
                    if n >= 2:
                        dve.wait_ge(c_rs, n - 1)
                    dve.tensor_reduce(qsum[:, n % 2, :], xn[:, n % 2, 0:HALF].rearrange("p (g d) -> p g d", d=DH), AX.X, ALU.add).then_inc(c_red, 1)
                    if n < NT:
                        c_lo(dve, 1, n)
                    if n == 2 * NT - 1:
                        for k in range(KD):
                            c_lo(dve, 2, k)
                    else:
                        convolve(5 * (n + 1) // 4)
                if 1 <= n <= 2 * NT:
                    q = n - 1
                    dve.wait_ge(c_rs, q + 1)
                    if q >= 2:
                        dve.wait_ge(c_tp, q - 1)
                    dve.tensor_tensor(qn[:, q % 2, :].rearrange("p (g d) -> p g d", d=DH), qtok[:, q % 2, :].rearrange("p (g d) -> p g d", d=DH),
                                      qrs[:, q % 2, :].unsqueeze(2).to_broadcast([P, 8, DH]), ALU.mult).then_inc(c_qn, 1)
                if n >= 2:
                    q = n - 2
                    dve.wait_ge(c_tp, q + 1)
                    to, gc = (qT, V_QG) if q < NT else (kT, V_KG)
                    dve.tensor_scalar(to[:, :, (q % NT) * P:(q % NT + 1) * P], quads(2 + q % 2), vec1[:, gc:gc + 1], None, ALU.mult).then_inc(c_tev, 1)
            convolve(TAPS)
            dve.drain().then_inc(cv_dve, 1)
            for half in range(2):
                hs = slice(half * HALF, (half + 1) * HALF)
                dve.wait_ge(ln_pe, half + 1)
                for c in range(2):
                    xc = dve.scalar_tensor_tensor(out=y_cv[:, c, hs], in0=bank(4 + half), scalar=-1.0 / 256, in1=y_cv[:, c, hs], op0=ALU.mult, op1=ALU.add)
                xc.then_inc(ln_dve, 1)
            for half in range(2):
                hs = slice(half * HALF, (half + 1) * HALF)
                dve.wait_ge(ln_act, half + 3)
                chain.link(dve.reciprocal(r_cv[:, hs], r_cv[:, hs]))
                for c in range(2):
                    yn = dve.tensor_tensor(y_cv[:, c, hs], y_cv[:, c, hs], r_cv[:, hs], ALU.mult)
                yn.then_inc(ln_dve, 1)

            dve.wait_ge(c_ready, 3 * NT)
            dve.wait_ge(idready, 4)
            for g in range(NB + 5):
                if g < NB and g % NT == 0:
                    h = BLOCKS[g][0]
                    if g >= 1:
                        dve.wait_ge(s_max, 2 * g)
                    chain.link(dve.tensor_scalar(BH, shared[:, 0:S], kc[:, K_SLOPE + h:K_SLOPE + h + 1], None, ALU.mult))
                if 1 <= g <= NB:
                    q = g - 1
                    W = (BLOCKS[q][1] + 1) * P
                    t = sm[:, q % 4, :]
                    dve.wait_ge(e_ready, 2 * q + 2)
                    chain.link(dve.reciprocal(t[:, 6:8], t[:, 4:6]))
                    chain.link(dve.scalar_tensor_tensor(out=t[:, 7:8], in0=t[:, 7:8], scalar=t[:, 4:5], in1=lam4[:, 4:5], op0=ALU.mult, op1=ALU.mult))
                    dve.scalar_tensor_tensor(out=sS[0][q % 3][:, 0:W], in0=sS[1][q % 2][:, 0:W], scalar=t[:, 7:8], in1=sS[0][q % 3][:, 0:W],
                                             op0=ALU.mult, op1=ALU.add).then_inc(a_ready, 1)
                if g < NB:
                    b = BLOCKS[g][1]
                    W = (b + 1) * P
                    for m in range(2):
                        dve.wait_ge(s_ready, 2 * g + m + 1)
                        if m == 0 and g >= 3:
                            dve.wait_ge(t_ready, TURNS[g - 2])
                        if m == 1 and g >= 2:
                            dve.wait_ge(a_ready, g - 1)
                        dve.tensor_tensor_reduce(sS[m][g % (3 - m)][:, 0:W], psf[:, 2 * m * HALF:2 * m * HALF + W], BH[:, S - P - b * P:S],
                                                 1.0, NEG, ALU.add, ALU.max, sm[:, g % 4, m:m + 1]).then_inc(s_max, 1)
                        dve.wait_ge(s_max, 2 * g + m + 1)
                        dve.tensor_scalar(sm[:, g % 4, 2 + m:3 + m], sm[:, g % 4, m:m + 1], -1.0, None, ALU.mult).then_inc(s_neg, 1)
                if g >= 5:
                    q = g - 5
                    h, b = BLOCKS[q]
                    dve.wait_ge(ot_ready, q + 1)
                    dve.tensor_scalar(MIX[:, 4 + h, b * P:(b + 1) * P], bank(7, P, (q % 4) * P), vec1[:, V_SG:V_SG + 1], None, ALU.mult).then_inc(ot_evac, 1)
                if NB - NT <= g < NB:
                    o_lo(dve, 0, g - (NB - NT))

            for t in range(2):
                mix1_lo(dve, t)
            for u in range(2 * NT):
                n, t = u // NT, u % NT
                if u + 2 < NT:
                    mix1_lo(dve, u + 2)
                if n == 0:
                    o_lo(dve, 1, t)
                dve.wait_ge(wo_ready, u + 1)
                dve.wait_ge(x_in[t], 32)
                hh = H[:, t, n * HALF:(n + 1) * HALF]
                dve.tensor_tensor(hh, bank(u % 2), hh, ALU.add).then_inc(wo_evac, 1)
                if u >= NT + 2:
                    nt_dve(dve, 1, t - 2, vec1[:, V_FG:V_FG + 8])
            for t in (NT - 2, NT - 1):
                nt_dve(dve, 1, t, vec1[:, V_FG:V_FG + 8])
            dve.wait_ge(rt_tp, 1)
            dve.wait_ge(rw_in, 64)
            for j in range(2):
                chain.link(dve.tensor_tensor(lg[:, 4 * j:4 * j + 4, :], quads(2 + j)[:, :, 0:20], rb.unsqueeze(1).to_broadcast([P, 4, 20]), ALU.add))

            dve.wait_ge(iotas, 3)

            def col(a, n=4):
                return a.unsqueeze(2).to_broadcast([P, NT, n])

            def tt(o, a, b, op):
                chain.link(dve.tensor_tensor(o, a, b, op))

            def first_max(o, values, eq):
                chain.link(dve.tensor_reduce(m1, values, AX.X, ALU.max))
                tt(eq, values, col(m1), ALU.is_equal)
                tt(eq, eq, first4.unsqueeze(1).to_broadcast([P, NT, 4]), ALU.mult)
                chain.link(dve.tensor_reduce(m1, eq, AX.X, ALU.max))
                tt(o, eq, col(m1), ALU.is_equal)
            chain.link(dve.tensor_reduce(g_max, lg[:, :, 0:4], AX.X, ALU.max))
            tt(ge, lg[:, :, 0:4], col(g_max), ALU.subtract)
            dve.sem_inc(rx, 1)
            dve.wait_ge(rx, 2)
            chain.link(dve.tensor_reduce(g_sum, ge, AX.X, ALU.add))
            chain.link(dve.reciprocal(g_p, g_sum))
            first_max(oh, ge, geq)
            ev = lg[:, :, 4:20].rearrange("p t (g e) -> p t g e", g=GROUPS)
            tt(lsel, ev, oh.unsqueeze(3).to_broadcast([P, NT, 4, 4]), ALU.mult)
            chain.link(dve.tensor_reduce(le, lsel.rearrange("p t g e -> p t e g"), AX.X, ALU.add))
            chain.link(dve.tensor_reduce(g_max, le, AX.X, ALU.max))
            tt(le, le, col(g_max), ALU.subtract)
            dve.sem_inc(rx, 1)
            dve.wait_ge(rx, 4)
            first_max(oh1, le, leq)
            chain.link(dve.tensor_reduce(v1, le, AX.X, ALU.max))
            chain.link(dve.scalar_tensor_tensor(out=pe2, in0=oh1, scalar=-2.0, in1=le, op0=ALU.mult, op1=ALU.add))
            first_max(oh2, pe2, leq)
            chain.link(dve.tensor_reduce(v2, pe2, AX.X, ALU.max))
            tt(den, v1, v2, ALU.add)
            chain.link(dve.reciprocal(den, den))
            tt(den, den, g_p, ALU.mult)
            tt(w1, v1, den, ALU.mult)
            tt(w2, v2, den, ALU.mult)
            for o, e in ((S1, oh1), (S2, oh2)):
                tt(o.rearrange("p t (g e) -> p t g e", g=GROUPS), oh.unsqueeze(3).to_broadcast([P, NT, 4, 4]),
                   e.unsqueeze(2).to_broadcast([P, NT, 4, 4]), ALU.mult)
            tt(MM, S1, S2, ALU.add)
            dve.sem_inc(rm_ready, 1)
            dve.wait_ge(rp_ready, 1)
            within = bank(6, P).rearrange("p (t e) -> p t e", t=NT)
            intile = bank(7, P).rearrange("p (t e) -> p t e", t=NT)
            chain.link(dve.memset(toff[:, 0, :], 0.0))
            for t in range(1, NT):
                tt(toff[:, t, :], toff[:, t - 1, :], intile[:, t - 1, :], ALU.add)
            tt(cnt, toff[:, NT - 1, :], intile[:, NT - 1, :], ALU.add)
            tt(posn, toff, within, ALU.add)
            chain.link(dve.tensor_scalar(tiles_i, cnt, float(P - 1), None, ALU.add))
            chain.link(dve.tensor_single_scalar(tiles_i, tiles_i, 7, ALU.arith_shift_right))
            chain.link(dve.tensor_copy(tiles_f, tiles_i))
            chain.link(dve.tensor_tensor_scan(tend, one16, tiles_f, 0.0, ALU.mult, ALU.add))
            tt(tbase, tend, tiles_f, ALU.subtract)
            chain.link(dve.scalar_tensor_tensor(out=posn, in0=tbase.unsqueeze(1).to_broadcast([P, NT, 16]), scalar=float(P), in1=posn, op0=ALU.mult, op1=ALU.add))
            for k, (o, s, w) in enumerate(((pos1, S1, w1), (pos2, S2, w2))):
                tt(tmpe, s, posn, ALU.mult)
                chain.link(dve.tensor_reduce(o, tmpe, AX.X, ALU.add))
                chain.link(dve.tensor_copy(sidx[:, :, k:k + 1], o.unsqueeze(2)))
                chain.link(dve.tensor_copy(rows_f[:, :, k, 2:3], w.unsqueeze(2)))
            dve.sem_inc(rx_done, 1)
            tt(cmpt, iot.unsqueeze(2).to_broadcast([P, MTILES + 1, 16]), tend.unsqueeze(1).to_broadcast([P, MTILES + 1, 16]), ALU.is_ge)
            chain.link(dve.tensor_reduce(et_f, cmpt, AX.X, ALU.add))
            chain.link(dve.tensor_scalar(et_f, et_f, float(EXPERTS - 1), None, ALU.min))
            chain.link(dve.tensor_copy(et_i, et_f))
            dve.sem_inc(experts_set, 1)
            C1 = 6.28125
            C2 = float(np.float32(np.round((2 * np.pi - C1) * 2.0 ** 20) * 2.0 ** -20))
            C3 = float(2 * np.pi - C1 - C2)
            MAGIC = 1.5 * 2.0 ** 23
            dve.wait_ge(row_in, 16)
            chain.link(dve.tensor_copy(ang, pos_i))
            chain.link(dve.tensor_scalar(ang, ang, kc[:, K_INV:K_INV + 1], None, ALU.mult))
            chain.link(dve.tensor_scalar(turns, ang, 1.0 / (2 * np.pi), kc[:, K_OFF:K_OFF + 1], ALU.mult, ALU.add))
            chain.link(dve.tensor_scalar(turns, turns, MAGIC, None, ALU.add))
            chain.link(dve.tensor_scalar(turns, turns, -MAGIC, None, ALU.add))
            for c in (C1, C2, C3):
                chain.link(dve.scalar_tensor_tensor(out=ang, in0=turns, scalar=-c, in1=ang, op0=ALU.mult, op1=ALU.add))
            chain.link(dve.tensor_scalar(ang, ang, kc[:, K_RAD:K_RAD + 1], 3.1415925, ALU.add, ALU.min))
            dve.tensor_scalar(ang, ang, -3.1415925, None, ALU.max).then_inc(rope_set, 1)
            dve.wait_ge(rope_set, 2)
            dve.tensor_scalar(rope[:, :], ang, kc[:, K_SIGN:K_SIGN + 1], None, ALU.mult).then_inc(rope_set, 1)
            dve.wait_ge(rope_set, 3)

            def rows_to_ht(i, o):
                p = o % 2
                dve.wait_ge(m_xt, i * 2 + (o + 1))
                wait_past(dve, m_gu, i * 2 + (o - 1))
                for c in range(2):
                    g = vec1[:, V_FG + 4 * c:V_FG + 4 * c + 4].unsqueeze(2).to_broadcast([P, 4, P])
                    ins = dve.tensor_tensor(hgT[:, p, 4 * c:4 * c + 4, :], quads(c), g, ALU.mult)
                ins.then_inc(m_ht, 1)

            def expert_dve(i, o):
                if has(i, o):
                    dve.wait_ge(m_sg, i * 2 + (o + 1))
                    wait_past(dve, m_at, i * 2 + (o - 1))
                    dve.scalar_tensor_tensor(out=actb[:, o % 2, :], in0=sgb[:, o % 2, :], scalar=tabs_f[:, ds(i * 2 + o, 1), 2:3].rearrange("p a c -> p (a c)"),
                                             in1=bank(2 + o % 2, DE, DE), op0=ALU.mult, op1=ALU.mult).then_inc(m_act, 1)
                if has(i, o + 1):
                    rows_to_ht(i, o + 1)
            dve.wait_ge(m_tab, 16)
            rows_to_ht(0, 0)
            experts(dve, expert_dve)
            dve.wait_ge(v2_in, 16 * 14)
            for t in range(NT):
                dve.wait_ge(x_in[t], 64)
                dve.tensor_tensor(H[:, t, :], H[:, t, :], y_tok[0][t], ALU.add).then_inc(comb, 1)
                dve.wait_ge(comb, t + 1)
                dve.tensor_tensor(H[:, t, :], H[:, t, :], y_tok[1][t], ALU.add).then_inc(h_in, 1)
                if t >= 2:
                    nt_dve(dve, 2, t - 2, vec2[:, 0, L_MIX:L_MIX + 8], MIX)
            nt_dve(dve, 2, NT - 2, vec2[:, 0, L_MIX:L_MIX + 8], MIX)

            dve.sem_inc(pg_evac, 2)
            dve.wait_ge(iotas, 3)
            base = chain.n
            PER = 166

            def layer(L):
                hc = Chain(dve, dve_chain, L * (PER or 0) + base)
                next_gain = vec2[:, ds(L + 1, 1), L_MIX:L_MIX + 8].rearrange("p a n -> p (a n)")
                dve.wait_ge(vl_ready, L + 1)
                settle(dve, settled)

                def rows_lo(t):
                    if t % 4 == 0:
                        dve.wait_ge(h_st[t // 4], L * 64 + 64)
                    dve.wait_ge(mx_hi, mx_at(L, 0, t))
                    ts = slice(t * P, (t + 1) * P)
                    dve.tensor_tensor(Hr[:, t, :, :], MIX[:, :, ts], HTr[:, :, ts].bitcast(F32), ALU.subtract).then_inc(mx_lo, 1)
                for t in range(4):
                    rows_lo(t)
                nt_dve(dve, L * 2 + 2, NT - 1, vl[:, L_MIX:L_MIX + 8], MIX)
                for t in range(4, NT):
                    rows_lo(t)
                dirs = ((slice(0, 64), 1), (slice(64, P), -1))

                def chunks(a):
                    return a.rearrange("p (c i) -> p c i", c=NCH)

                def gate(h):
                    dve.wait_ge(*gla(L, "t", h))
                    hc.link(dve.scalar_tensor_tensor(out=la, in0=la, scalar=0.0, in1=gt, op0=ALU.min, op1=ALU.subtract))
                    hc.link(dve.tensor_tensor_scan(cum[0:64, :], reset[0:64, :], la[0:64, :], 0.0, ALU.mult, ALU.add))
                    hc.link(dve.tensor_tensor_scan(cum[64:P, ::-1], reset[64:P, :], la[64:P, ::-1], 0.0, ALU.mult, ALU.add))
                    cc = chunks(cum)
                    for r, ref, last in ((slice(0, 64), CH // 2 - 1, CH - 1), (slice(64, P), CH // 2, 0)):
                        dve.tensor_copy(refs[r, :].unsqueeze(2), cc[r, :, ref:ref + 1])
                        o = dve.tensor_copy(lasts[r, :].unsqueeze(2), cc[r, :, last:last + 1])
                    hc.link(o)
                    dve.tensor_tensor(chunks(gt), cc, refs.unsqueeze(2).to_broadcast([P, NCH, CH]), ALU.subtract)
                    dve.tensor_tensor(chunks(la), lasts.unsqueeze(2).to_broadcast([P, NCH, CH]), cc, ALU.subtract).then_inc(g_dve, 1)

                def products(h):
                    dve.wait_ge(*gla(L, "e", h))
                    dve.wait_ge(z_ready, L * 5 + 1)
                    for half in range(2):
                        dve.wait_ge(u_evac[half], unit_evac(L, UI[("gk", h // 2)], half))
                    q, k = q_dup[h % 2], k_dup[h % 2]
                    dve.tensor_tensor(q_in, q_in, q, ALU.mult)
                    dve.tensor_tensor(kf[0:64, :], gt[0:64, :], k[0:64, :], ALU.mult)
                    dve.tensor_tensor(kb[64:P, :], gt[64:P, :], k[64:P, :], ALU.mult)
                    dve.tensor_tensor(la, la, k, ALU.mult).then_inc(g_dve, 1)
                    if h >= 1:
                        dve.wait_ge(*gla(L, "o", h - 1))
                    for par, to in ((0, q_even), (1, q_odd)):
                        v = lambda a: a.rearrange("p (t c i) -> p t c i", t=NT, c=2)[:, :, par, :]
                        o = dve.tensor_tensor(v(to), v(cum), v(q), ALU.mult)
                    o.then_inc(g_dve, 1)

                def causal(h):
                    dve.wait_ge(*gla(L, "a", h))
                    dve.wait_ge(z_ready, L * 5 + 2)
                    settle(dve, settled)
                    for d, (to, mask) in enumerate(((Af, mask_f), (Ab, mask_b))):
                        for b in range(2):
                            o = dve.copy_predicated(to[:, b * HALF:(b + 1) * HALF].rearrange("p (t i) -> p t i", t=4),
                                                    mask.bitcast(U32).unsqueeze(1).to_broadcast([P, 4, P]), quads(2 + 2 * d + b))
                    o.then_inc(g_dve, 1)

                def scan_states(h):
                    dve.wait_ge(*gla(L, "kvc", h))
                    if h == 0:
                        dve.memset(st[0:64, 0, :], 0.0)
                        hc.link(dve.memset(st[64:P, NCH - 1, :], 0.0))
                    for c in range(1, NCH):
                        b = NCH - 1 - c
                        dve.scalar_tensor_tensor(out=st[0:64, c, :], in0=st[0:64, c - 1, :], scalar=decay[0:64, c - 1:c], in1=kv[0:64, c - 1, :], op0=ALU.mult, op1=ALU.add)
                        o = dve.scalar_tensor_tensor(out=st[64:P, b, :], in0=st[64:P, b + 1, :], scalar=decay[64:P, b + 1:b + 2], in1=kv[64:P, b + 1, :], op0=ALU.mult, op1=ALU.add)
                        if c < NCH - 1:
                            hc.link(o)
                    o.then_inc(g_dve, 1)

                def finish(h):
                    dve.wait_ge(*gla(L, "r", h))
                    for half in range(2):
                        dve.wait_ge(u_evac[half], unit_evac(L, UI[("gg", h)], half))
                    for half in range(2):
                        hs = slice(half * HALF, (half + 1) * HALF)
                        o = dve.tensor_tensor(sqg[:, hs], bank(6 + half), sqg[:, hs], ALU.mult)
                    hc.link(o)
                    dve.scalar_tensor_tensor(out=MIX[:, 4 + h, :], in0=sqg, scalar=vl[:, L_GO:L_GO + 1], in1=MIX[:, 4 + h, :], op0=ALU.mult, op1=ALU.mult).then_inc(g_dve, 1)

                def rotate(to, src, hs, tmp):
                    dve.tensor_tensor(tmp, src[64:P, :], rope[64:P, hs], ALU.mult)
                    hc.link(dve.tensor_tensor(to[0:64, hs], src[0:64, :], rope[0:64, hs], ALU.mult))
                    return dve.tensor_tensor(to[0:64, hs], to[0:64, hs], tmp, ALU.add)

                for half in range(2):
                    dve.wait_ge(u_evac[half], unit_evac(L, 0, half))
                rotate(kr0, krr, slice(0, S), q_in[64:P, :]).then_inc(kr_done, 1)
                gate(0)
                products(0)
                for h in range(4):
                    causal(h)
                    scan_states(h)
                    if h < 3:
                        gate(h + 1)
                        products(h + 1)
                    finish(h)
                for j, (lat, g0, r) in enumerate(((c_q, L_QN, r_q), (c_kv, L_KVN, r_kv))):
                    dve.wait_ge(l_r, L * 2 + j + 1)
                    for i, c in enumerate(lat):
                        o = dve.scalar_tensor_tensor(out=c, in0=c, scalar=vl[:, g0 + i:g0 + i + 1], in1=r, op0=ALU.mult, op1=ALU.mult)
                    o.then_inc(l_c, 1)

                def fill(f):
                    kind, h, j = FILLS[f]
                    if kind == "p" and j >= 6:
                        return
                    dve.wait_ge(f_ready, L * NF + f + 1)
                    s, hs = 4 * (h % 2), slice((j % 2) * HALF, (j % 2 + 1) * HALF)
                    if kind == "p" and j not in (2, 3):
                        s += 0 if j < 2 else 2
                        dve.wait_ge(fh_ready, L * 16 + (4 * h + (j if j < 2 else j - 2) + 1))
                        dve.tensor_tensor(Hlo[:, s, hs], bank(f % 2), HTr[:, s, hs].bitcast(F32), ALU.subtract).then_inc(f_evac[f % 2], 1)
                        return
                    if kind == "p":
                        if (h, j) != (0, 2):
                            fv = FI[("p", h, 2) if j == 3 else ("p", h - 1, 3)]
                            dve.wait_ge(f_evac[fv % 2], fill_evac(L, fv))
                        s += 1
                        hc.link(rotate(H[:, s, :], ps[:, f % 2, :], hs, rtmp))
                        hc.link(dve.tensor_copy(HTr[0:64, s, hs], H[0:64, s, hs]))
                        o = dve.tensor_tensor(Hlo[0:64, s, hs], H[0:64, s, hs], HTr[0:64, s, hs].bitcast(F32), ALU.subtract)
                    else:
                        mm = MIX[:, h // 2, (h % 2) * HALF:(h % 2 + 1) * HALF]
                        o = dve.tensor_tensor(mm, bank(f % 2), mm, ALU.mult)
                    o.then_inc(f_evac[f % 2], 1)

                def weights_lo(i, k):
                    n = i % 2
                    dve.wait_ge(wh_ready, L * 4 * KD + W_1 + (i * KD + k + 1))
                    dve.tensor_tensor(WTr[:, n, k, :], WT[:, n, k, :], w_hi[n][:, k, :].bitcast(F32), ALU.subtract).then_inc(wl_ready, 1)

                def mix_lo(j, t):
                    dve.wait_ge(mx_hi, mx_at(L, 1 + j, t))
                    ts = slice(t * P, (t + 1) * P)
                    dve.tensor_tensor(MIXr[:, :, ts], MIX[:, :, ts], HTr[:, :, ts].bitcast(F32), ALU.subtract).then_inc(mx_lo, 1)
                dve.wait_ge(z_ready, L * 5 + 4)
                dve.tensor_tensor(kr_lo, kr, kr_hi.bitcast(F32), ALU.subtract)
                for s in (1, 5):
                    o = dve.tensor_copy(Hlo[64:P, s, :], kr[64:P, :])
                o.then_inc(z_ready, 1)
                for f in range(8):
                    fill(f)
                f = 8
                for g in range(STEPS):
                    if 1 <= g <= 4 * NT:
                        q = g - 1
                        dve.wait_ge(a_e, L * 4 * NT + q + 1)
                        hc.link(dve.reciprocal(sm[:, q % 2, 3:4], sm[:, q % 2, 2:3]))
                        dve.tensor_scalar(xn[:, q % 2, :], xn[:, q % 2, :], sm[:, q % 2, 3:4], None, ALU.mult).then_inc(a_p, 1)
                    if g < 4 * NT:
                        dve.wait_ge(a_s, L * 4 * NT + g + 1)
                        hc.link(dve.tensor_reduce(sm[:, g % 2, 0:1], psf[:, (2 + 2 * (g % 2)) * HALF:(4 + 2 * (g % 2)) * HALF], AX.X, ALU.max))
                        dve.tensor_scalar(sm[:, g % 2, 1:2], sm[:, g % 2, 0:1], -MLA_SCALE, None, ALU.mult).then_inc(a_neg, 1)
                    if g < 3 * NT:
                        fill(f)
                        f += 1
                    if g >= 5 and (g - 2) % 4 == 3:
                        fill(f)
                        f += 1
                    if 1 <= g <= 4 * NT:
                        q = g - 1
                        G = q // 4
                        dve.wait_ge(a_t[0], L * 4 * NT + q + 1)
                        if G >= 2 and q % 4 == 0:
                            dve.wait_ge(f_ready, L * NF + FI[("v", G - 2, 0)] + 1)
                        dve.tensor_copy(PT[G % 2][:, 0:4, (q % 4) * P:(q % 4 + 1) * P], quads(6)).then_inc(a_tev[0], 1)
                    if g >= STEPS - KD:
                        weights_lo(0, g - (STEPS - KD))
                for t in range(2):
                    mix_lo(0, t)
                for u in range(2 * NT):
                    n, t = u // NT, u % NT
                    if u + 2 < NT:
                        mix_lo(0, u + 2)
                    if n == 0:
                        dve.wait_ge(x_in[t], L * 16 + 80)
                    dve.wait_ge(wo_ready, L * 2 * NT + (2 * NT + u + 1))
                    hh = H[:, t, n * HALF:(n + 1) * HALF]
                    dve.tensor_tensor(hh, bank(u % 2), hh, ALU.add).then_inc(wo_evac, 1)
                    if n == 0:
                        weights_lo(1, t)
                    else:
                        if t >= 2:
                            nt_dve(dve, L * 2 + 3, t - 2, vl[:, L_PLE:L_PLE + 8], MIX)
                        if 3 <= t < 7:
                            weights_lo(2, 2 * (t - 3))
                            weights_lo(2, 2 * (t - 3) + 1)
                        if t >= 3:
                            mix_lo(1, t - 3)
                for t in range(NT - 3, NT):
                    if t >= NT - 2:
                        nt_dve(dve, L * 2 + 3, t, vl[:, L_PLE:L_PLE + 8], MIX)
                    mix_lo(1, t)
                for u in range(2 * NT):
                    n, t = u // NT, u % NT
                    sg, hh = sgp[:, u % 2, :], H[:, t, n * HALF:(n + 1) * HALF]
                    dve.wait_ge(pg_sg, L * 2 * NT + u + 1)
                    dve.tensor_tensor(sg, sg, bank(6 + u % 2), ALU.mult).then_inc(pg_evac, 1)
                    dve.wait_ge(pg_evac, L * 2 * NT + u + 3)
                    o = dve.tensor_tensor(hh, sg, hh, ALU.add)
                    if n == 1:
                        o.then_inc(h_in, 1)
                    if 2 <= u < 6:
                        weights_lo(3, 2 * (u - 2))
                        weights_lo(3, 2 * (u - 2) + 1)
                    if u >= NT + 3:
                        nt_dve(dve, L * 2 + 4, u - NT - 3, next_gain, MIX)
                for t in (NT - 3, NT - 2):
                    nt_dve(dve, L * 2 + 4, t, next_gain, MIX)
                assert PER is None or hc.n == PER, (hc.n, PER)
            layers(dve, layer)
            dve.wait_ge(row_in, 32)
            dve.wait_ge(n_ht, ht_ready(2 * LAYERS + 2, NT - 1))
            dve.wait_ge(mx_hi, mx_at(LAYERS, 0, 3))
            for t in range(NT):
                dve.wait_ge(n_rs, (2 * LAYERS + 2) * NT + t + 1)
                dve.scalar_tensor_tensor(out=HT[:, t, :], in0=H[:, t, :], scalar=rs[:, t:t + 1], in1=fgain, op0=ALU.mult, op1=ALU.mult).then_inc(f_out, 1)


def kernel(**inputs):
    import concourse.bacc as bacc
    from concourse.bass_utils import run_bass_kernel_spmd

    nc = bacc.Bacc("TRN2", target_bir_lowering=False, num_devices=1)
    arrays, A = {}, {}
    for name, a in list(inputs.items()) + [("kc", shape_constants())]:
        a = np.ascontiguousarray(a)
        arrays["in_" + name] = a
        A[name] = nc.dram_tensor("in_" + name, a.shape, mybir.dt.from_np(a.dtype), kind="ExternalInput").ap()
    out = nc.dram_tensor("out", (1, S, D), F32, kind="ExternalOutput").ap()
    program(nc, A, out)
    return run_bass_kernel_spmd(nc, [arrays], core_ids=[0]).results[0]["out"]
```
